# Optimizing a Trainium2 kernel written in Bass

```python
import math
import jax, jax.numpy as jnp
from jax import lax
import numpy as np

D_MODEL = 1024
BATCH = 1
SEQ = 512
DEPTH = 1

GRID_W = 64
CTX_LEN = 256
N_MIXERS = 2
A_HEADS = 4
A_DK = 128
A_DV = 256
N_DIR = 2
CHUNK = 64
D_FF = 2816
EPS = 1e-6
A_PROJ = 2 * A_HEADS * A_DK + A_HEADS * A_DV + D_MODEL + 2 * N_DIR * A_HEADS
N_A = sum(1 for i in range(DEPTH) if i % N_MIXERS == 0)
N_B = DEPTH - N_A


def rmsnorm(x, g):
    xf = x.astype(jnp.float32)
    y = xf * lax.rsqrt(jnp.mean(xf * xf, axis=-1, keepdims=True) + EPS)
    return (y * g.astype(jnp.float32)).astype(x.dtype)

def modulate(x, g, shift, scale):
    return rmsnorm(x, g) * (1 + scale) + shift

def conv3(x, w, axis):
    pad = [(0, 0)] * x.ndim
    pad[axis] = (1, 1)
    xp = jnp.pad(x, pad)
    n = x.shape[axis]
    sl = lambda s: lax.slice_in_dim(xp, s, s + n, axis=axis)
    return sl(0) * w[0] + sl(1) * w[1] + sl(2) * w[2]

def mlstm_inputs(h, w_in, b_gate):
    bn, t, _ = h.shape
    p = h @ w_in
    o1 = A_HEADS * A_DK
    o2 = 2 * o1
    o3 = o2 + A_HEADS * A_DV
    o4 = o3 + D_MODEL
    heads = lambda a, d: a.reshape(bn, t, A_HEADS, d).transpose(0, 2, 1, 3).astype(jnp.float32)
    q = heads(p[..., :o1], A_DK)
    k = heads(p[..., o1:o2], A_DK) * (A_DK ** -0.5)
    v = heads(p[..., o2:o3], A_DV)
    o = p[..., o3:o4]
    gates = (p[..., o4:] + b_gate).astype(jnp.float32)
    gates = gates.reshape(bn, t, 2, N_DIR, A_HEADS).transpose(2, 3, 0, 4, 1)
    it = gates[0]
    lf = jax.nn.log_sigmoid(gates[1])
    return q, k, v, it, lf, o

def mlstm_chunk_scan(q, k, v, it, lf, state, emit):
    bn, nh, t, _ = q.shape
    nc = t // CHUNK
    chunks = lambda a: jnp.moveaxis(a.reshape(a.shape[:2] + (nc, CHUNK) + a.shape[3:]), 2, 0)
    xs = (chunks(q), chunks(k), chunks(v), chunks(it), chunks(lf))
    mask = jnp.tril(jnp.ones((CHUNK, CHUNK), dtype=bool))

    def body(carry, inp):
        cm, nv, m = carry
        qc, kc, vc, ic, fc = inp
        b = jnp.cumsum(fc, axis=-1)
        g = b[..., -1]
        a = g[..., None] - b + ic
        m_new = jnp.maximum(g + m, jnp.max(a, axis=-1))
        decay = jnp.exp(g + m - m_new)
        wa = jnp.exp(a - m_new[..., None])
        c_new = decay[..., None, None] * cm + jnp.einsum('bhsv,bhsd->bhvd', wa[..., None] * vc, kc)
        n_new = decay[..., None] * nv + jnp.einsum('bhs,bhsd->bhd', wa, kc)
        if not emit:
            return (c_new, n_new, m_new), None
        dmat = jnp.where(mask, b[..., :, None] - b[..., None, :] + ic[..., None, :], -jnp.inf)
        inter = b + m[..., None]
        m_t = jnp.maximum(inter, jnp.max(dmat, axis=-1))
        w = jnp.exp(dmat - m_t[..., None]) * jnp.einsum('bhtd,bhsd->bhts', qc, kc)
        wi = jnp.exp(inter - m_t)
        num = jnp.einsum('bhts,bhsv->bhtv', w, vc) + wi[..., None] * jnp.einsum('bhvd,bhtd->bhtv', cm, qc)
        den = jnp.sum(w, axis=-1) + wi * jnp.einsum('bhd,bhtd->bht', nv, qc)
        h = num / jnp.maximum(jnp.abs(den), jnp.exp(-m_t))[..., None]
        return (c_new, n_new, m_new), h

    state, hs = lax.scan(body, state, xs)
    if not emit:
        return None, state
    return jnp.moveaxis(hs, 0, 2).reshape(bn, nh, t, A_DV), state

def mlstm_readout(h, o, gain, w_out):
    bn, nh, t, dv = h.shape
    hn = h * lax.rsqrt(jnp.mean(h * h, axis=-1, keepdims=True) + EPS)
    hn = hn.transpose(0, 2, 1, 3).reshape(bn, t, nh * dv) * gain.astype(jnp.float32)
    y = hn * jax.nn.sigmoid(o.astype(jnp.float32))
    return y.astype(o.dtype) @ w_out

def mlstm_mixer(h_lat, h_ctx, w_in, b_gate, head_gain, w_out, emit_ctx):
    ql, kl, vl, il, fl, ol = mlstm_inputs(h_lat, w_in, b_gate)
    qc, kc, vc, ic, fc, oc = mlstm_inputs(h_ctx, w_in, b_gate)
    bn = h_lat.shape[0]
    s0 = (jnp.zeros((bn, A_HEADS, A_DV, A_DK), jnp.float32),
          jnp.zeros((bn, A_HEADS, A_DK), jnp.float32),
          jnp.zeros((bn, A_HEADS), jnp.float32))
    rq = lambda a: jnp.flip(a, axis=2)
    rg = lambda a: jnp.flip(a, axis=-1)
    hc_f, s_f = mlstm_chunk_scan(qc, kc, vc, ic[0], fc[0], s0, emit_ctx)
    hl_f, _ = mlstm_chunk_scan(ql, kl, vl, il[0], fl[0], s_f, True)
    hc_b, s_b = mlstm_chunk_scan(rq(qc), rq(kc), rq(vc), rg(ic[1]), rg(fc[1]), s0, emit_ctx)
    hl_b, _ = mlstm_chunk_scan(rq(ql), rq(kl), rq(vl), rg(il[1]), rg(fl[1]), s_b, True)
    y = mlstm_readout(hl_f + rq(hl_b), ol, head_gain, w_out)
    yc = mlstm_readout(hc_f + rq(hc_b), oc, head_gain, w_out) if emit_ctx else None
    return y, yc

def shortconv_mixer(h, w_in, w_conv, w_out, conv_fn):
    bg, cg, xv = jnp.split(h @ w_in, 3, axis=-1)
    return (bg * conv_fn(cg * xv, w_conv)) @ w_out

def conv_glu(h, w_up, w_conv, b_conv, w_down, conv_fn):
    gate, val = jnp.split(h @ w_up, 2, axis=-1)
    gate = conv_fn(gate, w_conv) + b_conv
    return (jax.nn.silu(gate) * val) @ w_down

def first_inputs(seed: int = 0) -> dict:
    key = jax.random.key(seed)
    ks = jax.random.split(key, 24)
    nrm = lambda k, s, sc: jax.random.normal(k, s, jnp.float32) * sc
    D = D_MODEL
    b_i = nrm(ks[10], (N_A, N_DIR, A_HEADS), 0.1)
    b_f = jnp.linspace(3.0, 6.0, A_HEADS, dtype=jnp.float32) + nrm(ks[11], (N_A, N_DIR, A_HEADS), 0.1)
    a_b_gate = jnp.stack([b_i, b_f], axis=1).reshape(N_A, 2 * N_DIR * A_HEADS)
    return {
        "x": nrm(ks[0], (BATCH, SEQ, D), 1.0),
        "c": nrm(ks[1], (BATCH, D), 1.0),
        "ctx": nrm(ks[2], (BATCH, CTX_LEN, D), 1.0),
        "c_ctx": nrm(ks[3], (D,), 1.0),
        "w_mod": nrm(ks[4], (DEPTH, D, 6 * D), 0.5 * D ** -0.5),
        "b_mod": nrm(ks[5], (DEPTH, 6 * D), 0.02),
        "g_mix": 1.0 + nrm(ks[6], (DEPTH, D), 0.05),
        "g_ffn": 1.0 + nrm(ks[7], (DEPTH, D), 0.05),
        "a_w_in": nrm(ks[8], (N_A, D, A_PROJ), D ** -0.5),
        "a_b_gate": a_b_gate,
        "a_head_gain": 1.0 + nrm(ks[9], (N_A, A_HEADS * A_DV), 0.05),
        "a_w_out": nrm(ks[12], (N_A, A_HEADS * A_DV, D), (A_HEADS * A_DV) ** -0.5),
        "b_w_in": nrm(ks[13], (N_B, D, 3 * D), D ** -0.5),
        "b_w_conv": nrm(ks[14], (N_B, 3, D), 3 ** -0.5),
        "b_w_out": nrm(ks[15], (N_B, D, D), D ** -0.5),
        "f_w_up": nrm(ks[16], (DEPTH, D, 2 * D_FF), D ** -0.5),
        "f_w_conv": nrm(ks[17], (DEPTH, 3, D_FF), 3 ** -0.5),
        "f_b_conv": nrm(ks[18], (DEPTH, D_FF), 0.02),
        "f_w_down": nrm(ks[19], (DEPTH, D_FF, D), D_FF ** -0.5),
        "g_final": 1.0 + nrm(ks[20], (D,), 0.05),
    }

def first_block(x, c, ctx, c_ctx, w_mod, b_mod, g_mix, g_ffn, a_w_in, a_b_gate, a_head_gain,
              a_w_out, b_w_in, b_w_conv, b_w_out, f_w_up, f_w_conv, f_b_conv, f_w_down, g_final):
    bn, t, d = x.shape
    rows = t // GRID_W
    lat_row_conv = lambda a, w: conv3(a.reshape(bn, rows, GRID_W, a.shape[-1]), w, 2).reshape(a.shape)
    lat_col_conv = lambda a, w: conv3(a.reshape(bn, rows, GRID_W, a.shape[-1]), w, 1).reshape(a.shape)
    seq_conv = lambda a, w: conv3(a, w, 1)
    rec_layers = [i for i in range(DEPTH) if i % N_MIXERS == 0]
    last_rec = max(rec_layers) if rec_layers else -1

    for i in range(DEPTH):
        j = i // N_MIXERS
        ctx_read = i <= last_rec
        ctx_live = i < last_rec
        mod = jax.nn.silu(c) @ w_mod[i] + b_mod[i]
        sh1, sc1, ga1, sh2, sc2, ga2 = [m[:, None, :] for m in jnp.split(mod, 6, axis=-1)]
        if ctx_read:
            mod_c = jax.nn.silu(c_ctx) @ w_mod[i] + b_mod[i]
            csh1, csc1, cga1, csh2, csc2, cga2 = jnp.split(mod_c, 6, axis=-1)
            hc = modulate(ctx, g_mix[i], csh1, csc1)
        hx = modulate(x, g_mix[i], sh1, sc1)
        if i % N_MIXERS == 0:
            y, yc = mlstm_mixer(hx, hc, a_w_in[j], a_b_gate[j], a_head_gain[j], a_w_out[j], ctx_live)
        else:
            y = shortconv_mixer(hx, b_w_in[j], b_w_conv[j], b_w_out[j], lat_row_conv)
            yc = shortconv_mixer(hc, b_w_in[j], b_w_conv[j], b_w_out[j], seq_conv) if ctx_live else None
        x = x + ga1 * y
        hx = modulate(x, g_ffn[i], sh2, sc2)
        x = x + ga2 * conv_glu(hx, f_w_up[i], f_w_conv[i], f_b_conv[i], f_w_down[i], lat_col_conv)
        if ctx_live:
            ctx = ctx + cga1 * yc
            hc = modulate(ctx, g_ffn[i], csh2, csc2)
            ctx = ctx + cga2 * conv_glu(hc, f_w_up[i], f_w_conv[i], f_b_conv[i], f_w_down[i], seq_conv)

    return rmsnorm(x, g_final)


HEAD_DIM = 64
DIL_GROUPS = ((128, 1), (512, 4), (2048, 16))
HEADS_PER_GROUP = 4
N_GROUPS = len(DIL_GROUPS)
N_HEADS_A = HEADS_PER_GROUP * N_GROUPS
N_HEADS_B = 4
WIDTH_A = N_HEADS_A * HEAD_DIM
WIDTH_A_OUT = HEADS_PER_GROUP * HEAD_DIM
WIDTH_B = N_HEADS_B * HEAD_DIM
N_BRANCH = 2
SPLIT_SIZES = (WIDTH_A, WIDTH_A, WIDTH_A, WIDTH_B, WIDTH_B, WIDTH_B, N_HEADS_B, D_MODEL, D_MODEL)
SPLIT_POINTS = tuple(int(v) for v in np.cumsum(SPLIT_SIZES)[:-1])
D_IN = int(sum(SPLIT_SIZES))
D_FF_2 = -(-8 * D_MODEL // (3 * 256)) * 256
BLOCK = 128
ALIBI_MAX = 8.0
N_MOD = 6


def rms_norm(x, g):
    xf = x.astype(jnp.float32)
    y = xf * lax.rsqrt(jnp.mean(xf * xf, axis=-1, keepdims=True) + EPS)
    return (y * g.astype(jnp.float32)).astype(x.dtype)

def alibi_slopes():
    h = np.arange(1, N_HEADS_A + 1, dtype=np.float32)
    return jnp.asarray(2.0 ** (-ALIBI_MAX * h / N_HEADS_A), dtype=jnp.float32)

def dilated_group_attention(q, k, v, window, dilation, slopes):
    B, S, H, Dh = q.shape
    L = S // dilation
    nb = -(-L // BLOCK)
    Lp = nb * BLOCK
    pad_end = Lp - L

    def split(t):
        return t.reshape(B, L, dilation, H, Dh).transpose(0, 2, 1, 3, 4)

    def band(t):
        t = jnp.pad(split(t), ((0, 0), (0, 0), (BLOCK, pad_end), (0, 0), (0, 0)))
        t = t.reshape(B, dilation, nb + 1, BLOCK, H, Dh)
        return jnp.concatenate([t[:, :, :-1], t[:, :, 1:]], axis=3)

    qb = jnp.pad(split(q), ((0, 0), (0, 0), (0, pad_end), (0, 0), (0, 0)))
    qb = qb.reshape(B, dilation, nb, BLOCK, H, Dh)
    kb, vb = band(k), band(v)

    scores = jnp.einsum('brnqhd,brnkhd->brnhqk', qb, kb).astype(jnp.float32) * (Dh ** -0.5)
    qi = jnp.arange(BLOCK)[:, None]
    kj = jnp.arange(2 * BLOCK)[None, :]
    dist = qi + BLOCK - kj
    kpos = jnp.arange(nb)[:, None, None] * BLOCK + kj[None] - BLOCK
    valid = (dist >= 0) & (dist <= window // dilation) & (kpos >= 0)
    bias = -slopes[:, None, None] * (dist * dilation).astype(jnp.float32)[None]
    logits = jnp.where(valid[None, None, :, None], scores + bias, -jnp.inf)
    lse = jax.nn.logsumexp(logits, axis=-1)
    p = jnp.exp(logits - lse[..., None])
    out = jnp.einsum('brnhqk,brnkhd->brnqhd', p.astype(v.dtype), vb)
    out = out.reshape(B, dilation, Lp, H, Dh)[:, :, :L].transpose(0, 2, 1, 3, 4).reshape(B, S, H, Dh)
    lse = lse.transpose(0, 1, 2, 4, 3).reshape(B, dilation, Lp, H)[:, :, :L]
    lse = lse.transpose(0, 2, 1, 3).reshape(B, S, H)
    return out, lse

def dilated_mixture(qa, ka, va):
    B, S, _ = qa.shape
    shp = (B, S, N_HEADS_A, HEAD_DIM)
    qa, ka, va = qa.reshape(shp), ka.reshape(shp), va.reshape(shp)
    slopes = alibi_slopes()
    outs, lses = [], []
    for g, (w, d) in enumerate(DIL_GROUPS):
        sl = slice(g * HEADS_PER_GROUP, (g + 1) * HEADS_PER_GROUP)
        o, l = dilated_group_attention(qa[:, :, sl], ka[:, :, sl], va[:, :, sl], w, d, slopes[sl])
        outs.append(o)
        lses.append(l)
    outs = jnp.stack(outs, axis=0)
    alpha = jax.nn.softmax(jnp.stack(lses, axis=0), axis=0)
    y = jnp.sum(alpha[..., None].astype(outs.dtype) * outs, axis=0)
    return y.reshape(B, S, WIDTH_A_OUT)

def forgetting_attention(qb, kb, vb, f_logit, b_forget):
    B, S, _ = qb.shape
    H, Dh = N_HEADS_B, HEAD_DIM
    q = qb.reshape(B, S, H, Dh)
    k = kb.reshape(B, S, H, Dh)
    v = vb.reshape(B, S, H, Dh)
    log_f = jax.nn.log_sigmoid(f_logit.astype(jnp.float32) + b_forget.astype(jnp.float32))
    F = jnp.cumsum(log_f, axis=1).transpose(0, 2, 1)
    nb = S // BLOCK
    q_blocks = q.reshape(B, nb, BLOCK, H, Dh).transpose(1, 0, 2, 3, 4)
    F_blocks = F.reshape(B, H, nb, BLOCK).transpose(2, 0, 1, 3)
    kpos = jnp.arange(S)
    scale = Dh ** -0.5

    def one_block(args):
        i, qi, Fi = args
        s = jnp.einsum('bqhd,bkhd->bhqk', qi, k).astype(jnp.float32) * scale
        s = s + (Fi[..., :, None] - F[..., None, :])
        qpos = i * BLOCK + jnp.arange(BLOCK)
        s = jnp.where(kpos[None, :] <= qpos[:, None], s, -jnp.inf)
        p = jax.nn.softmax(s, axis=-1)
        return jnp.einsum('bhqk,bkhd->bqhd', p.astype(v.dtype), v)

    out = lax.map(one_block, (jnp.arange(nb), q_blocks, F_blocks))
    return out.transpose(1, 0, 2, 3, 4).reshape(B, S, H * Dh)

def token_mixer(h, w_in, b_forget, w_up_a, w_up_b, w_out):
    z = h @ w_in
    qa, ka, va, qb, kb, vb, fz, gza, gzb = jnp.split(z, SPLIT_POINTS, axis=-1)
    ya = dilated_mixture(qa, ka, va) @ w_up_a
    yb = forgetting_attention(qb, kb, vb, fz, b_forget) @ w_up_b
    merged = jax.nn.sigmoid(gza) * ya + jax.nn.sigmoid(gzb) * yb
    return merged @ w_out

def swiglu(h, w_ffn_in, w_ffn_out):
    gate, up = jnp.split(h @ w_ffn_in, 2, axis=-1)
    return (jax.nn.silu(gate) * up) @ w_ffn_out

def second_inputs(seed: int = 0) -> dict:
    key = jax.random.key(seed)
    ks = jax.random.split(key, 16)
    f32 = jnp.float32
    nrm = lambda k, shape, s: jax.random.normal(k, shape, f32) * s
    x = jax.random.normal(ks[0], (BATCH, SEQ, D_MODEL), f32)
    c = jax.random.normal(ks[1], (BATCH, D_MODEL), f32)
    w_ada = nrm(ks[2], (DEPTH, D_MODEL, N_MOD * D_MODEL), 0.5 * D_MODEL ** -0.5)
    b_ada = nrm(ks[3], (DEPTH, N_MOD * D_MODEL), 0.02)
    norm_mix = 1.0 + nrm(ks[4], (DEPTH, D_MODEL), 0.02)
    w_in = nrm(ks[5], (DEPTH, D_MODEL, D_IN), D_MODEL ** -0.5)
    b_forget = jnp.linspace(1.0, 5.0, N_HEADS_B, dtype=f32)[None] + nrm(ks[6], (DEPTH, N_HEADS_B), 0.1)
    w_up_a = nrm(ks[7], (DEPTH, WIDTH_A_OUT, D_MODEL), WIDTH_A_OUT ** -0.5)
    w_up_b = nrm(ks[8], (DEPTH, WIDTH_B, D_MODEL), WIDTH_B ** -0.5)
    w_out = nrm(ks[9], (DEPTH, D_MODEL, D_MODEL), D_MODEL ** -0.5)
    norm_ffn = 1.0 + nrm(ks[10], (DEPTH, D_MODEL), 0.02)
    w_ffn_in = nrm(ks[11], (DEPTH, D_MODEL, 2 * D_FF_2), D_MODEL ** -0.5)
    w_ffn_out = nrm(ks[12], (DEPTH, D_FF_2, D_MODEL), D_FF_2 ** -0.5)
    norm_final = 1.0 + nrm(ks[13], (D_MODEL,), 0.02)
    return {"x": x, "c": c, "w_ada": w_ada, "b_ada": b_ada, "norm_mix": norm_mix,
            "w_in": w_in, "b_forget": b_forget, "w_up_a": w_up_a, "w_up_b": w_up_b,
            "w_out": w_out, "norm_ffn": norm_ffn, "w_ffn_in": w_ffn_in,
            "w_ffn_out": w_ffn_out, "norm_final": norm_final}

def second_block(x, c, w_ada, b_ada, norm_mix, w_in, b_forget, w_up_a, w_up_b, w_out,
              norm_ffn, w_ffn_in, w_ffn_out, norm_final):
    c_act = jax.nn.silu(c)
    for l in range(DEPTH):
        mod = c_act @ w_ada[l] + b_ada[l]
        sh1, sc1, g1, sh2, sc2, g2 = [m[:, None, :] for m in jnp.split(mod, N_MOD, axis=-1)]
        h = rms_norm(x, norm_mix[l]) * (1.0 + sc1) + sh1
        x = x + g1 * token_mixer(h, w_in[l], b_forget[l], w_up_a[l], w_up_b[l], w_out[l])
        h = rms_norm(x, norm_ffn[l]) * (1.0 + sc2) + sh2
        x = x + g2 * swiglu(h, w_ffn_in[l], w_ffn_out[l])
    return rms_norm(x, norm_final)


def setup_inputs(seed=0):
    out = dict(first_inputs(seed))
    for name, value in second_inputs(seed + 1).items():
        if name != "x":
            out[name + "_2"] = value
    return out


def reference(
    x, c, ctx, c_ctx, w_mod, b_mod, g_mix, g_ffn, a_w_in, a_b_gate, a_head_gain, a_w_out,
    b_w_in, b_w_conv, b_w_out, f_w_up, f_w_conv, f_b_conv, f_w_down, g_final, c_2, w_ada_2,
    b_ada_2, norm_mix_2, w_in_2, b_forget_2, w_up_a_2, w_up_b_2, w_out_2, norm_ffn_2,
    w_ffn_in_2, w_ffn_out_2, norm_final_2,
):
    x = first_block(
        x, c, ctx, c_ctx, w_mod, b_mod, g_mix, g_ffn, a_w_in, a_b_gate, a_head_gain, a_w_out,
        b_w_in, b_w_conv, b_w_out, f_w_up, f_w_conv, f_b_conv, f_w_down, g_final,
    )
    return second_block(
        x, c_2, w_ada_2, b_ada_2, norm_mix_2, w_in_2, b_forget_2, w_up_a_2, w_up_b_2, w_out_2,
        norm_ffn_2, w_ffn_in_2, w_ffn_out_2, norm_final_2,
    )


_drawn_inputs = setup_inputs


def setup_inputs(seed=0):
    import zlib

    import numpy as np

    out = dict(_drawn_inputs(seed))
    spreads = {}
    factors = {'g_ffn': 3.646,
     'a_head_gain': 6.432,
     'f_b_conv': 8.0,
     'b_ada_2': 2.9,
     'norm_mix_2': 8.0,
     'norm_ffn_2': 8.0,
     'norm_final_2': 2.781}
    for name, (base, spread) in spreads.items():
        noise = np.random.default_rng([zlib.crc32(name.encode()), seed]).standard_normal(out[name].shape)
        drawn = base * np.exp(spread * noise) if base else spread * noise
        out[name] = __import__('jax').numpy.asarray(drawn.astype(out[name].dtype))
    for name, factor in factors.items():
        out[name] = (out[name] * factor).astype(out[name].dtype)
    return out
```

```python
from contextlib import ExitStack

import numpy as np
import concourse.bass as bass
from concourse import mybir

F32 = mybir.dt.float32
F32R = mybir.dt.float32r
ALU = mybir.AluOpType
ACT = mybir.ActivationFunctionType
AX_X = mybir.AxisListType.X

P = 128
D = 1024
KT = D // P
T = 512
TT = T // P
TC = 256
CTT = TC // P
GRID_W = 64
NH, DK, DV = 4, 128, 256
VE = DV + 2
FF = 2816
FT = FF // P
FH = FT // 2
EPS = 1e-6
UC = 256
BWD = 32
GR = BWD + NH
NG = 2 * BWD + GR

U_Q, U_K, U_V, U_O, U_OUT = 0, 2, 4, 8, 12
U_UP = 16
U_DOWN = U_UP + FT
U_QKV2 = U_DOWN + 2 * KT
U_GZ = U_QKV2 + 12
U_OUT2 = U_GZ + KT
U_IN2 = U_OUT2 + 4
U_DOWN2 = U_IN2 + FT
U_END = U_DOWN2 + 2 * KT

CL, CA, CB = 4, 4, 32
HD = 64
GH, GROUPS = 4, 3
NHA, NHB = GH * GROUPS, 4
WA, WB = NHA * HD, NHB * HD
WINDOW0 = 128
QK_SCALE = HD ** -0.5
SLOPES = [2.0 ** (-8.0 * (h + 1) / NHA) for h in range(NHA)]
KEYS_A = T + 2 * P
ROUNDS_A = GH * CL
ROUNDS = ROUNDS_A + NHB * CL
FAR = 1e30
NF = 68

V_C, V_CC, V_C2, V_GMIX, V_GFFN, V_GAIN, V_NMIX, V_NFFN, V_GFIN, V_NFIN, V_BMOD = (
    0, 8, 16, 24, 32, 40, 48, 56, 64, 72, 80)
V_BADA, V_FB, V_CONV = 128, 176, 198
NV = V_CONV + 3 * FT


class Steps:

    def __init__(self, eng, sem):
        self.eng, self.sem, self.n, self.reg, self.at = eng, sem, 0, 0, 0

    def done(self, ins):
        ins.then_inc(self.sem, 1)
        self.n += 1
        return ins

    def wait(self, back=0):
        self.eng.wait_ge(self.sem, self.n - back + self.reg)

    def enter(self, i, per):
        self.at, self.reg = self.n, i * per

    def leave(self, iters, per):
        assert self.n - self.at == per, (self.n - self.at, per)
        self.n, self.reg = self.at + per * iters, 0


def program(nc, a, out):
    with ExitStack() as ctx:
        arena = nc.sbuf_base + 31 & ~31
        size = (nc.sbuf_usable_end - arena) & ~31
        slab = ctx.enter_context(nc.sbuf_tensor("slab", [P, size // 4], F32))

        def at(name, shape, dt, off):
            return nc.alloc_sbuf_tensor_at(name, shape, dt, offset=arena + off)

        def sem(name):
            return ctx.enter_context(nc.semaphore(name))

        o = 0

        def take(n):
            nonlocal o
            was, o = o, o + (n + 31 & ~31)
            return was

        o_raw, o_hi, o_lo, o_rawm = take(8192), take(16384), take(16384), take(8192)
        o_x, o_h = take(16384), take(32768)
        raw = at("raw", [P, 2048], F32, o_raw)
        whi = [at(f"whi{s}", [P, 2048], F32R, o_hi + 8192 * s) for s in range(2)]
        wlo = [at(f"wlo{s}", [P, 2048], F32R, o_lo + 8192 * s) for s in range(2)]
        rawm = at("rawm", [P, 2, D], F32, o_rawm)
        xT = at("xT", [P, KT, T], F32, o_x)
        hh = at("hh", [P, KT, T], F32R, o_h)
        hl = at("hl", [P, KT, T], F32R, o_h + 16384)

        ident = at("ident", [P, P], F32, take(512))
        ones = at("ones", [P, P], F32, take(512))
        vec = at("vec", [P, NV], F32, take(4 * NV))
        sil = at("sil", [P, 24], F32, take(96))
        mods = at("mods", [P, 96], F32, take(384))
        mod1, mod2 = mods[:, 0:48], mods[:, 48:96]
        modc = at("modc", [P, 16], F32, take(64))
        small = at("small", [P, 64], F32, take(256))
        gcols = at("gcols", [P, 396], F32, take(1584))
        hd = at("hd", [P, 48], F32, take(192))
        acc = at("acc", [P, T], F32, take(2048))
        o_acc = o - 2048
        junk2 = at("junk2", [P, DV], F32, o_acc)
        scratch = take(0)
        o_T = size - 12288 - 31 & ~31
        tbuf = [at(f"tbuf{i}", [P, T], F32, o_T + 2048 * i) for i in range(6)]
        A1, AC, A2 = small[:, 0:8], small[:, 8:16], small[:, 16:24]
        ssx, rx = small[:, 24:30], small[:, 30:36]
        mean, rstd = small[:, 36:40], small[:, 40:44]
        bi, bf = small[0:GR, 44:45], small[0:GR, 45:46]
        gc, mc, ngc = small[0:GR, 46:47], small[0:GR, 47:48], small[0:GR, 48:49]

        xn = at("xn", [P, TT + CTT, D], F32, scratch)
        vrow = [at(f"vrow{i}", [P, P], F32, o_T + 2048 * i) for i in range(3)]
        wm = at("wm", [P, KT, 2048], F32, scratch + 24576)
        mrow = at("mrow", [2, 2048], F32, o_h)
        junk = at("junk", [P, D], F32, o_x + 4096)
        wgr = at("wgr", [P, KT, NG], F32, o_x)
        wgh = at("wgh", [P, KT, NG], F32R, o_T + 4096)
        wgl = at("wgl", [P, KT, NG], F32R, o_T + 4096 + 3200)
        gI = at("gI", [GR, TC + T], F32, o_x + 3584)
        gZ = at("gZ", [GR, TC + T], F32, o_x + 3584 + 3072)
        gF = at("gF", [GR, TC + T], F32, o_x + 3584 + 6144)
        gG = at("gG", [GR, T], F32, o_x + 3584 + 9216)
        gN = at("gN", [GR, T], F32, o_x)
        dmc = at("dmc", [GR, GR], F32, o_x + 2048)
        Grow = at("Grow", [GR, T], F32, o_x + 0)
        s = scratch
        qh, ql = at("qh", [P, NH, T], F32R, s), at("ql", [P, NH, T], F32R, s + 8192)
        kh, kl = at("kh", [P, NH, T], F32R, s + 16384), at("kl", [P, NH, T], F32R, s + 24576)
        s += 32768
        vh = at("vh", [P, TT, NH, VE], F32R, s)
        vl = at("vl", [P, TT, NH, VE], F32R, s + TT * NH * VE * 4)
        s += 2 * TT * NH * VE * 4
        vc = at("vc", [P, CTT, NH, VE], F32, s)
        s += CTT * NH * VE * 4
        kc = at("kc", [P, CTT, NH * DK], F32, s)
        s += CTT * NH * DK * 4
        hch, hcl = at("hch", [P, KT, TC], F32R, s), at("hcl", [P, KT, TC], F32R, s + 8192)
        Wh = [at(f"Wh{i}", [P, T], F32R, s + 2048 * i) for i in range(2)]
        Wl = [at(f"Wl{i}", [P, T], F32R, s + 4096 + 2048 * i) for i in range(2)]
        WI = at("WI", [P, T], F32, s + 8192)
        qwh, qwl = at("qwh", [P, T], F32R, s + 10240), at("qwl", [P, T], F32R, s + 12288)
        masks = at("masks", [P, 2, P], F32, s + 14336)
        assert s + 16384 <= o_T, (s + 16384, o_T)
        Ch, Cl = at("Ch", [P, VE], F32R, o_rawm), at("Cl", [P, VE], F32R, o_rawm + 1056)
        kw = at("kw", [P, CTT, DK], F32, o_rawm + 2112)
        Gnat = at("Gnat", [GR, T], F32, o_rawm + 3168)
        hn = at("hn", [P, TT, NH * DV], F32, o_x)
        xr = at("xr", [P, TT, D], F32, scratch + 32768)
        yh, yl = at("yh", [P, KT, T], F32R, scratch), at("yl", [P, KT, T], F32R, scratch + 16384)
        fh, fl = at("fh", [P, FT, T], F32R, scratch), at("fl", [P, FT, T], F32R, scratch + FT * T * 4)
        assert scratch + FT * T * 8 <= o_T
        msum0 = at("msum0", [P, D], F32, o_T + 8192)
        msum1 = at("msum1", [P, D], F32, scratch + FT * T * 8)
        assert scratch + FT * T * 8 + 4096 <= o_T
        s = scratch
        qk = at("qk", [P, 16, T], F32, s)
        mh, ml = at("mh", [P, KT, T], F32R, s), at("ml", [P, KT, T], F32R, s + 16384)
        v2 = at("v2", [P, TT, WA + WB], F32, s + 32768)
        on = at("on", [P, CL, 512], F32, s + 49152)
        att = at("att", [P, 4, T], F32, s + 57344)
        wfr = at("wfr", [P, KT, NF], F32, s + 57344)
        wfh = at("wfh", [P, KT, NF], F32R, s + 57344 + 2176)
        wfl = at("wfl", [P, KT, NF], F32R, s + 57344 + 4352)
        FB = at("FB", [P, NHB, T], F32, s + 57344)
        dist0 = at("dist0", [P, CL, T], F32, s + 65536)
        dist12 = at("dist12", [P, 2, P], F32, s + 73728)
        causal = at("causal", [P, CL, T], F32, s + 74752)
        upA, upB = at("upA", [P, 2, D], F32, o_rawm), at("upB", [P, 2, D], F32, s + 82944)
        CF = [at(f"CF{i}", [P, T], F32, s + 91136 + 2048 * i) for i in range(2)]
        fA, fB = at("fA", [NHB, T], F32, s + 91136), at("fB", [NHB, T], F32, s + 93184)
        assert s + 95232 <= o_T
        fF = at("fF", [NHB, T], F32, o_acc)
        L = [at(f"L{i}", [P, KEYS_A], F32, o_T + 4 * KEYS_A * i) for i in range(2)]
        PT = [at(f"PT{i}", [P, KEYS_A], F32, o_T + 8 * KEYS_A + 4 * KEYS_A * i) for i in range(2)]
        fin = at("fin", [P, CL, D], F32, o_h)
        mean2, r12, G2 = small[:, 52:56], small[:, 56:60], AC
        A3 = small[:, 0:8]
        lsum, rsum, nmax = hd[:, 0:4], hd[:, 4:8], hd[:, 8:12]
        acc2 = at("acc2", [P, T], F32, o_T + 2048 * 4)

        bank = [ctx.enter_context(nc.psum_tensor(f"bank{i}", [P, 512], F32)) for i in range(8)]

        S = {n: sem(n) for n in (
            "mod_sum mod_rows loaded hi_ready lo_ready pe_used evacuated mod_loaded mod_used mod_evacuated "
            "vecs_in x_in c_in wm_in0 wm_in1 wm_in2 wm_in3 wm_in4 wm_in5 wm_in6 wm_in7 wg_in consts_in bias_in dve_step act_step "
            "masks_in wg_zero vec_t vec_cols silu_c pe_mod0 mod0_cols x_sq x_mean x_root x_scaled x_turned h_raw h_ready "
            "wg_split gates_in g_abs g_soft g_u g_em g_nat g_turned gcols_in "
            "gb_ready gb_copied wi_ready kw_ready s_ready s_free d_ready e_ready w_ready w_free q_ready num_ready "
            "num_free h_sq h_mean h_root hn_ready xr_in xr_turned xT_in o_sig hn_turned y_ready "
            "acc_ready stat_ready mean_ready root_ready diag_ready bc_ready t_ready n_raw n_ready "
            "glu_a glu_s f_ready ones_in out_done "
            "mean2_ready root2_ready tab_in wf_in bf_in up_in wf_split f_logits f_abs f_soft f_neg fb_ready fb_copied rescaled "
            "qk_ready l_free l_ready p_ready tr_ready pt_copied o_ready o_free cf_ready on_turned att_ready "
            "g_sig m_ready xg_ready fin_turned fin_copied scaled scaled_a").split()}

        block = ctx.enter_context(nc.Block())
        PERM = [(h, d) for h in range(NH) for d in range(2)]

        def row(idx):
            h, d = PERM[idx]
            return BWD * d + h

        def span(idx, j):
            s = j if idx % 2 == 0 else TT - 1 - j
            return s, (slice(s * P, T) if idx % 2 == 0 else slice(0, (s + 1) * P))

        r8 = raw[:, :].rearrange("p (t n) -> p t n", t=KT)
        r11 = raw[:, 0:FH * P].rearrange("p (t n) -> p t n", t=FH)

        @block.sync
        def _(sp):
            for i, (name, lo, n, c0) in enumerate((
                    ("c", V_C, 8, 0), ("c_ctx", V_CC, 8, 0), ("c_2", V_C2, 8, 0), ("g_mix", V_GMIX, 8, 0),
                    ("g_ffn", V_GFFN, 8, 0), ("a_head_gain", V_GAIN, 8, 0), ("norm_mix_2", V_NMIX, 8, 0),
                    ("norm_ffn_2", V_NFFN, 8, 0), ("g_final", V_GFIN, 8, 0), ("norm_final_2", V_NFIN, 8, 0),
                    ("b_mod", V_BMOD, 48, 0), ("b_ada_2", V_BADA, 48, 0), ("f_b_conv", V_FB, FT, 0))):
                src = a[name]
                src = src if len(src.shape) == 1 else src.rearrange("a n -> (a n)")
                sp.dma_start(vrow[lo // P][lo % P:lo % P + n, :],
                             src.rearrange("(t p) -> t p", p=P)).then_inc(S["vecs_in"], 16)
            sp.dma_start(vrow[2][0:3 * FT, :],
                         a["f_w_conv"].rearrange("a c (t p) -> (a c t) p", p=P)).then_inc(S["vecs_in"], 16)
            sp.dma_start(ident[:], a["k_ident"]).then_inc(S["consts_in"], 16)
            sp.dma_start(xn[:, 0:TT, :], a["x"].rearrange("a (t p) n -> p (a t) n", p=P)).then_inc(S["x_in"], 16)
            wmod = a["w_mod"].rearrange("a (t p) n -> p (a t) n", p=P)
            for k in range(KT):
                sp.dma_start(wm[:, k, :], wmod[:, k, 0:2 * D]).then_inc(S[f"wm_in{k}"], 16)
                if k == 0:
                    sp.dma_start(xn[:, TT:TT + CTT, :],
                                 a["ctx"].rearrange("a (t p) n -> p (a t) n", p=P)).then_inc(S["c_in"], 16)
            sp.wait_ge(S["wg_zero"], 3)
            win = a["a_w_in"].rearrange("a (t p) n -> p (a t) n", p=P)
            g0 = 2 * NH * DK + NH * DV + D
            for q in range(4):
                sp.dma_start(wgr[:, :, BWD * q:BWD * q + NH], win[:, :, g0 + NH * q:g0 + NH * q + NH]).then_inc(S["wg_in"], 16)
                sp.dma_start((bi, bf)[q // 2][BWD * (q % 2):BWD * (q % 2) + NH, :],
                             a["a_b_gate"][0, NH * q:NH * q + NH].rearrange("(n o) -> n o", o=1)).then_inc(S["bias_in"], 16)

            def load(u, dst, src):
                if not isinstance(u, int) or u >= 1:
                    sp.wait_ge(S["lo_ready"], u)
                sp.dma_start(dst, src).then_inc(S["loaded"], 16)

            wout = a["a_w_out"].rearrange("a (t p) n -> p (a t) n", p=P)
            for u in range(U_UP):
                if u < U_OUT:
                    load(u, r8, win[:, :, u * UC:(u + 1) * UC])
                else:
                    load(u, r8, wout[:, :, (u - U_OUT) * UC:(u - U_OUT + 1) * UC])
                if u == U_O:
                    sp.wait_ge(S["pe_used"], U_O)
                    sp.dma_start(masks[:], a["k_masks"]).then_inc(S["masks_in"], 16)
                    sp.wait_ge(S["num_free"], 2 * NH)
                    sp.dma_start(xr[:], a["x"].rearrange("a (t p) n -> p (a t) n", p=P)).then_inc(S["xr_in"], 16)
            wup = a["f_w_up"].rearrange("a (t p) (g n) -> p (a t) g n", p=P, g=2)
            r8g = raw[:, :].rearrange("p (t g n) -> p t g n", t=KT, g=2)
            def load_up(u, i, w):
                for g in range(2):
                    if g == 0:
                        sp.wait_ge(S["lo_ready"], u)
                    sp.dma_start(r8g[:, :, g, :], w[:, :, g, bass.ds(i * P, P)]).then_inc(S["loaded"], 8 * 2)
            with sp.Fori(0, FT) as i:
                load_up(U_UP + i, i, wup)
            wdn = a["f_w_down"].rearrange("a (t p) n -> p (a t) n", p=P)
            load(U_DOWN, r11, wdn[:, 0:FH, 0:P])
            load(U_DOWN + 1, r11, wdn[:, FH:FT, 0:P])
            with sp.Fori(1, KT) as m:
                for s in range(2):
                    load(U_DOWN + 2 * m + s, r11, wdn[:, s * FH:(s + 1) * FH, bass.ds(m * P, P)])
            win2 = a["w_in_2"].rearrange("a (t p) n -> p (a t) n", p=P)
            wz = a["w_in_2"][:, :, 3 * (WA + WB) + NHB:].rearrange("a (t p) (g n) -> p (a t) g n", p=P, g=2)
            for u in range(U_QKV2, U_GZ):
                load(u, r8, win2[:, :, (u - U_QKV2) * UC:(u - U_QKV2 + 1) * UC])
                if u == U_QKV2:
                    sp.wait_ge(S["pe_used"], U_QKV2)
                    sp.wait_ge(S["wg_zero"], 4)
                    sp.dma_start(wfr[:, :, 0:NHB], win2[:, :, 3 * (WA + WB):3 * (WA + WB) + NHB]).then_inc(S["wf_in"], 16)
                    sp.dma_start(small[0:NHB, 44:45], a["b_forget_2"].rearrange("o n -> n o")).then_inc(S["bf_in"], 16)
                    sp.dma_start(dist0[:], a["k_dist0"]).then_inc(S["tab_in"], 16)
                    sp.dma_start(dist12[:], a["k_dist12"]).then_inc(S["tab_in"], 16)
                    sp.dma_start(causal[:], a["k_causal"]).then_inc(S["tab_in"], 16)
                    sp.wait_ge(S["mod_evacuated"], 10)
                    sp.dma_start(upA[:], a["w_up_a_2"].rearrange("a (t p) n -> p (a t) n", p=P)).then_inc(S["up_in"], 16)
                    sp.dma_start(upB[:], a["w_up_b_2"].rearrange("a (t p) n -> p (a t) n", p=P)).then_inc(S["up_in"], 16)
            for m in range(KT):
                load_up(U_GZ + m, m, wz)
            wout2 = a["w_out_2"].rearrange("a (t p) n -> p (a t) n", p=P)
            for u in range(U_OUT2, U_IN2):
                load(u, r8, wout2[:, :, (u - U_OUT2) * UC:(u - U_OUT2 + 1) * UC])
            win3 = a["w_ffn_in_2"].rearrange("a (t p) (g n) -> p (a t) g n", p=P, g=2)
            with sp.Fori(0, FT) as i:
                load_up(U_IN2 + i, i, win3)
            wdn2 = a["w_ffn_out_2"].rearrange("a (t p) n -> p (a t) n", p=P)
            with sp.Fori(0, KT) as m:
                for s in range(2):
                    load(U_DOWN2 + 2 * m + s, r11, wdn2[:, s * FH:(s + 1) * FH, bass.ds(m * P, P)])
            dst = out.rearrange("o (b a c) n -> c a (o b) n", a=CA, c=CL)
            for c in range(CL):
                if c % 2 == 0:
                    sp.wait_ge(S["scaled"], c // 2 + 1)
                else:
                    sp.wait_ge(S["scaled_a"], c // 2 + 1)
                for q in range(CA):
                    sp.dma_start(dst[c, q], fin[q * CB:(q + 1) * CB, c, :]).then_inc(S["out_done"], 16)
            sp.wait_ge(S["out_done"], 16 * CL * CA)

        LOADS, n = {}, 0
        for u0, u1, per in ((0, U_UP, 16), (U_UP, U_DOWN, 32), (U_DOWN, U_GZ, 16), (U_GZ, U_OUT2, 32),
                            (U_OUT2, U_IN2, 16), (U_IN2, U_DOWN2, 32), (U_DOWN2, U_END, 16)):
            LOADS[u0] = (n, per)
            n += (u1 - u0) * per

        def loaded_count(u, u0):
            n, per = LOADS[u0]
            return n + (u - u0 + 1) * per

        @block.gpsimd
        def _(pool):
            pool.memset(ones[:], 1.0).then_inc(S["ones_in"], 1)
            pool.memset(wgr[:], 0.0).then_inc(S["wg_zero"], 1)
            pool.memset(small[:, 44:45], 0.0).then_inc(S["wg_zero"], 1)
            pool.memset(small[:, 45:46], 0.0).then_inc(S["wg_zero"], 1)

            def load_mod(j, w, q, c0):
                src = w[:, 2 * q:2 * q + 2, c0 if isinstance(c0, slice) else bass.ds(c0, D)]
                if not isinstance(j, int) or j >= 1:
                    pool.wait_ge(S["mod_used"], j)
                pool.dma_start(rawm[:], src).then_inc(S["mod_loaded"], 16)

            wmod = a["w_mod"].rearrange("a (t p) n -> p (a t) n", p=P)
            wada = a["w_ada_2"].rearrange("a (t p) n -> p (a t) n", p=P)
            for j in range(U_UP):
                if j == U_O:
                    pool.wait_ge(S["num_free"], 2 * NH)
                load_mod(j, wmod, j % 4, 2 * D + j // 4 * D)
            with pool.Fori(0, (FT + 2) // 4) as i:
                for q in range(4):
                    load_mod(U_UP + 4 * i + q, wada, q, i * D)
            pool.wait_ge(S["pe_used"], U_QKV2)
            pool.memset(wfr[:], 0.0).then_inc(S["wg_zero"], 1)
            pool.wait_ge(S["tab_in"], 48)
            for q in range(NHB * CL):
                h, c = q // CL, q % CL
                if c == 0:
                    pool.wait_ge(S["fb_copied"], h + 1)
                if q < 2:
                    pool.wait_ge(S["fb_copied"], NHB)
                else:
                    pool.wait_ge(S["l_free"], ROUNDS_A + q - 1)
                pool.tensor_tensor(CF[q % 2][:], causal[:, c, :], FB[:, h, :], ALU.add).then_inc(S["cf_ready"], 1)

        @block.scalar
        def _(act):
            st = Steps(act, S["act_step"])

            def high(u, s, n, phase=0, first=False):
                act.wait_ge(S["loaded"], loaded_count(u, phase))
                if not first:
                    act.wait_ge(S["pe_used"], u - 1)
                act.copy(whi[s][:, 0:n], raw[:, 0:n]).then_inc(S["hi_ready"], 1)

            act.wait_ge(S["x_in"], 16)
            for t in range(TT + CTT):
                if t == TT:
                    act.wait_ge(S["c_in"], 16)
                if t:
                    st.wait()
                ins = act.activation(junk[:], xn[:, t, :], ACT.Square, accum_out=ssx[:, t:t + 1])
                if t == TT + CTT - 1:
                    ins.then_inc(S["x_sq"], 1)
                else:
                    st.done(ins)
            act.wait_ge(S["vec_cols"], 3)
            act.activation(sil[:], vec[:, 0:24], ACT.Silu).then_inc(S["silu_c"], 1)
            act.wait_ge(S["x_mean"], 1)
            act.activation(rx, ssx, ACT.Sqrt).then_inc(S["x_root"], 1)
            high(0, 0, 2048, first=True)
            act.wait_ge(S["mod0_cols"], 4)
            for n in range(2 * KT):
                k, w = n // 2, (T, TC)[n % 2]
                act.wait_ge(S["x_turned"], n + 1)
                if n >= 2:
                    act.wait_ge(S["h_ready"], n - 1)
                sc, sh = ((A1, mod1), (AC, modc))[n % 2]
                act.activation(tbuf[n % 2][:, 0:w], bank[n % 6][:, 0:w], ACT.Identity,
                               bias=sh[:, k:k + 1], scale=sc[:, k:k + 1]).then_inc(S["h_raw"], 1)
            high(1, 1, 2048, first=True)
            act.wait_ge(S["g_abs"], 1)
            st.done(act.activation(gF[:], gF[:], ACT.Exp, scale=-1.0))
            st.wait()
            act.activation(gF[:], gF[:], ACT.Ln, bias=1.0).then_inc(S["g_soft"], 1)
            act.wait_ge(S["g_u"], 1)
            st.done(act.activation(gI[:, 0:TC], gI[:, 0:TC], ACT.Exp, bias=ngc))
            st.wait()
            act.wait_ge(S["g_u"], 2)
            act.activation(gF[:, TC:], gF[:, TC:], ACT.Exp, scale=-1.0).then_inc(S["g_em"], 1)
            for u in range(2, U_O + 1):
                high(u, u % 2, 2048)
            def gates_out(i):
                act.wait_ge(S["gb_ready"], i + 1)
                if i >= 2:
                    act.wait_ge(S["num_free"], i - 1)
                act.copy(tbuf[4 + i % 2][:], bank[6 + i % 2][:]).then_inc(S["gb_copied"], 1)
                act.wait_ge(S["gb_copied"], i + 1)
                if i >= 1:
                    act.wait_ge(S["q_ready"], i)
                act.activation(WI[:], tbuf[4 + i % 2][:], ACT.Exp, scale=-1.0,
                               bias=gcols[:, 360 + row(i):361 + row(i)]).then_inc(S["wi_ready"], 1)

            def decay(n):
                _, r = span(n // TT, n % TT)
                act.wait_ge(S["d_ready"], n + 1)
                act.activation(tbuf[n % 2][:, r], tbuf[n % 2][:, r], ACT.Exp, scale=-1.0).then_inc(S["e_ready"], 1)

            gates_out(0)
            decay(0)
            for i in range(2 * NH):
                for j in range(1, TT):
                    decay(i * TT + j)
                if i + 1 < 2 * NH:
                    gates_out(i + 1)
                    decay((i + 1) * TT)
                if i % 2:
                    act.wait_ge(S["num_free"], i + 1)
                    for t in range(TT):
                        if i > 1 or t:
                            act.wait_ge(S["h_sq"], t + 4 * (i // 2))
                        c = t * NH + i // 2
                        act.activation(junk2[:], hn[:, t, (i // 2) * DV:(i // 2 + 1) * DV], ACT.Square,
                                       accum_out=hd[:, c:c + 1]).then_inc(S["h_sq"], 1)
            act.wait_ge(S["h_mean"], 1)
            act.activation(hd[:, 0:16], hd[:, 0:16], ACT.Sqrt).then_inc(S["h_root"], 1)
            for u in range(U_O, U_OUT):
                high(u + 1, (u + 1) % 2, 2048)
                act.wait_ge(S["pe_used"], u + 1)
                for m in range(2):
                    n = 2 * (u - U_O) + m
                    if n >= 2:
                        act.wait_ge(S["y_ready"], n - 1)
                    act.activation(tbuf[m][:], bank[3 * (u % 2) + m][:], ACT.Sigmoid).then_inc(S["o_sig"], 1)
            for k in range(KT):
                act.wait_ge(S["xr_turned"], k + 1)
                if k == 0:
                    act.wait_ge(S["y_ready"], 2 * (U_OUT - U_O))
                act.copy(xT[:, k, :], bank[6 if k % 2 == 0 else 7][:]).then_inc(S["xT_in"], 1)
            for u in range(U_OUT, U_UP - 1):
                high(u + 1, (u + 1) % 2, 2048)

            def norm_apply(nth, A, B):
                for k in range(KT):
                    act.wait_ge(S["t_ready"], nth * KT + k + 1)
                    act.activation(tbuf[4 + k % 2][:], tbuf[2 + k % 2][:], ACT.Identity,
                                   bias=B[:, k:k + 1], scale=A[:, k:k + 1]).then_inc(S["n_raw"], 1)

            high(U_UP, 0, 2048, U_UP)
            act.wait_ge(S["mean_ready"], 1)
            act.activation(mean, mean, ACT.Sqrt).then_inc(S["root_ready"], 1)
            norm_apply(0, A2, mod1[:, 24:32])

            def up_act(u, i, s, nxt=True, phase=U_UP, n=2048):
                high(u + 1, 1 - s, n, phase)
                act.wait_ge(S["glu_a"], i + 1)
                act.activation(tbuf[2 + s][:], tbuf[s][:], ACT.Silu).then_inc(S["glu_s"], 1)

            with act.Fori(0, FT // 2 - 1) as i:
                for s in range(2):
                    up_act(U_UP + 2 * i + s, 2 * i + s, s)
            up_act(U_DOWN - 2, FT - 2, 0)
            up_act(U_DOWN - 1, FT - 1, 1, phase=U_DOWN, n=FH * P)
            with act.Fori(0, KT - 1) as m:
                for s in range(2):
                    high(U_DOWN + 2 * m + s + 1, 1 - s, FH * P, U_DOWN)
            high(U_DOWN + 2 * KT - 1, 1, FH * P, U_DOWN)
            high(U_QKV2, 0, 2048, U_DOWN)
            act.wait_ge(S["mean_ready"], 2)
            act.activation(mean, mean, ACT.Sqrt).then_inc(S["root_ready"], 1)
            act.wait_ge(S["mean2_ready"], 1)
            act.activation(mean2, mean2, ACT.Sqrt).then_inc(S["root2_ready"], 1)
            norm_apply(1, A3, mod2)
            for u in range(U_QKV2, U_GZ):
                if u + 1 < U_GZ:
                    high(u + 1, (u + 1) % 2, 2048, U_DOWN)
                else:
                    high(u + 1, (u + 1) % 2, 2048, U_GZ)
                if u == U_QKV2 + 8:
                    act.wait_ge(S["f_abs"], 1)
                    st.done(act.activation(fB[:], fB[:], ACT.Exp, scale=-1.0))
                    st.wait()
                    act.activation(fB[:], fB[:], ACT.Ln, bias=1.0).then_inc(S["f_soft"], 1)
            for r in range(ROUNDS + 1):
                if r < ROUNDS:
                    w = KEYS_A if r < ROUNDS_A else T
                    act.wait_ge(S["l_ready"], r + 1)
                    act.activation(L[r % 2][:, 0:w], L[r % 2][:, 0:w], ACT.Exp, scale=QK_SCALE, bias=nmax[:, r % 4:r % 4 + 1],
                                   accum_out=lsum[:, r % 4:r % 4 + 1]).then_inc(S["p_ready"], 1)
                if r >= 1:
                    q = r - 1
                    act.wait_ge(S["tr_ready"], q + 1)
                    if q >= 2:
                        act.wait_ge(S["o_ready"], q - 1)
                    ins = act.copy(PT[q % 2][:, 0:T], bank[4][:])
                    if q < ROUNDS_A:
                        st.done(ins)
                        ins = act.copy(PT[q % 2][:, T:], bank[5][:, 0:2 * P])
                    ins.then_inc(S["pt_copied"], 1)
            for f in range(4):
                act.wait_ge(S["on_turned"], f + 1)
                if f == 0:
                    act.wait_ge(S["cf_ready"], NHB * CL)
                act.copy(att[:, f, :], bank[4 + f][:]).then_inc(S["att_ready"], 1)
            for u in range(U_GZ, U_OUT2):
                high(u + 1, (u + 1) % 2, 2048, U_GZ if u + 1 < U_OUT2 else U_OUT2)
                act.wait_ge(S["pe_used"], u + 1)
                if u > U_GZ:
                    act.wait_ge(S["m_ready"], u - U_GZ)
                for g in range(2):
                    act.activation(tbuf[g][:], bank[3 * (u % 2) + g][:], ACT.Sigmoid).then_inc(S["g_sig"], 1)
            for u in range(U_OUT2, U_IN2 - 1):
                high(u + 1, (u + 1) % 2, 2048, U_OUT2)
            high(U_IN2, 0, 2048, U_IN2)
            act.wait_ge(S["mean_ready"], 3)
            act.activation(mean, mean, ACT.Sqrt).then_inc(S["root_ready"], 1)
            norm_apply(2, A2, mod2[:, 24:32])

            def in_act(u, i, s, phase=U_IN2, n=2048):
                high(u + 1, 1 - s, n, phase)
                act.wait_ge(S["pe_used"], u + 1)
                act.activation(tbuf[2 + s][:], bank[3 * s][:], ACT.Silu).then_inc(S["glu_s"], 1)

            with act.Fori(0, FT // 2 - 1) as i:
                for s in range(2):
                    in_act(U_IN2 + 2 * i + s, 2 * i + s, s)
            in_act(U_DOWN2 - 2, FT - 2, 0)
            in_act(U_DOWN2 - 1, FT - 1, 1, phase=U_DOWN2, n=FH * P)

            def turned_out(m, b):
                act.wait_ge(S["fin_turned"], m + 1)
                act.copy(fin[:, :, bass.ds(m * P, P)], bank[b][:].rearrange("p (c n) -> p c n", c=CL)).then_inc(S["fin_copied"], 1)

            for s in range(2):
                high(U_DOWN2 + s + 1, 1 - s, FH * P, U_DOWN2)
            for s in range(2):
                high(U_DOWN2 + 2 + s + 1, 1 - s, FH * P, U_DOWN2)
            turned_out(0, 6)
            with act.Fori(1, KT // 2 - 1) as i:
                for q in range(2):
                    for s in range(2):
                        high(U_DOWN2 + 4 * i + 2 * q + s + 1, 1 - s, FH * P, U_DOWN2)
                    turned_out(2 * i + q - 1, 7 - q)
            for q in range(2):
                for s in range(2):
                    if q == 0 or s == 0:
                        high(U_DOWN2 + 2 * (KT - 2) + 2 * q + s + 1, 1 - s, FH * P, U_DOWN2)
                turned_out(KT - 3 + q, 7 - q)
            turned_out(KT - 1, 7)
            act.wait_ge(S["mean_ready"], 4)
            act.activation(mean, mean, ACT.Sqrt).then_inc(S["root_ready"], 1)
            act.wait_ge(S["scaled"], 1)
            for c in (1, 3):
                act.activation(fin[:, c, :], fin[:, c, :], ACT.Copy, scale=rstd[:, c:c + 1]).then_inc(S["scaled_a"], 1)

        @block.vector
        def _(v):
            st = Steps(v, S["dve_step"])

            def low(u, s, n):
                v.wait_ge(S["hi_ready"], u + 1)
                v.tensor_tensor(wlo[s][:, 0:n], raw[:, 0:n], whi[s][:, 0:n].bitcast(F32), ALU.subtract).then_inc(S["lo_ready"], 1)

            def mod_add(j, q, acc_m, c0):
                v.wait_ge(S["mod_loaded"], (j + 1) * 16)
                for k in (2 * q, 2 * q + 1):
                    w = rawm[:, k % 2, :]
                    if k == 0:
                        ins = v.tensor_scalar(acc_m[:], w, sil[:, c0:c0 + 1], None, ALU.mult)
                    else:
                        ins = v.scalar_tensor_tensor(acc_m[:], w, sil[:, c0 + k:c0 + k + 1], acc_m[:], ALU.mult, ALU.add)
                    if k % 2 == 0:
                        st.done(ins)
                        st.wait()
                ins.then_inc(S["mod_used"], 1)
                v.wait_ge(S["mod_used"], j + 1)

            def mod_out(c):
                v.wait_ge(S["mod_sum"], c + 1)
                v.tensor_tensor(mods[:, bass.ds(16 + 8 * c, 8)], bank[7][:, 0:8], vec[:, bass.ds(V_BMOD + 16 + 8 * c, 8)],
                                ALU.add).then_inc(S["mod_evacuated"], 1)

            for i in range(3):
                c = (P, V_CONV - P + 0, 3 * FT)[i]
                v.wait_ge(S["vec_t"], i + 1)
                lo = (0, P, V_CONV)[i]
                v.tensor_copy(vec[:, lo:lo + c], bank[i][:, 0:c]).then_inc(S["vec_cols"], 1)
            v.wait_ge(S["x_sq"], 1)
            v.tensor_scalar(ssx, ssx, 1.0 / D, EPS, ALU.mult, ALU.add).then_inc(S["x_mean"], 1)
            v.wait_ge(S["x_root"], 1)
            st.done(v.reciprocal(rx, rx))
            st.wait()
            for t in range(TT + CTT):
                v.tensor_scalar(xn[:, t, :], xn[:, t, :], rx[:, t:t + 1], None, ALU.mult).then_inc(S["x_scaled"], 1)
            low(0, 0, 2048)
            for q in range(4):
                v.wait_ge(S["pe_mod0"], 1)
                v.tensor_copy(mrow[:, q * 512:(q + 1) * 512], bank[q][0:2, :]).then_inc(S["mod_rows"], 1)
            v.wait_ge(S["pe_mod0"], 2)
            v.wait_ge(S["vec_cols"], 3)
            v.wait_ge(S["consts_in"], 16)
            m0 = bank[7][:, 0:32].rearrange("p (m v) -> p v m", v=2)
            v.tensor_tensor(mod1[:, 0:16], m0[:, 0, :], vec[:, V_BMOD:V_BMOD + 16], ALU.add).then_inc(S["mod0_cols"], 1)
            v.tensor_tensor(modc[:], m0[:, 1, :], vec[:, V_BMOD:V_BMOD + 16], ALU.add).then_inc(S["mod0_cols"], 1)
            v.wait_ge(S["mod0_cols"], 2)
            v.scalar_tensor_tensor(A1, mod1[:, 8:16], 1.0, vec[:, V_GMIX:V_GMIX + 8], ALU.add, ALU.mult).then_inc(S["mod0_cols"], 1)
            v.scalar_tensor_tensor(AC, modc[:, 8:16], 1.0, vec[:, V_GMIX:V_GMIX + 8], ALU.add, ALU.mult).then_inc(S["mod0_cols"], 1)
            for n in range(2 * KT):
                k, w = n // 2, (T, TC)[n % 2]
                dh, dl = ((hh, hl), (hch, hcl))[n % 2]
                v.wait_ge(S["h_raw"], n + 1)
                st.done(v.tensor_copy(dh[:, k, :], tbuf[n % 2][:, 0:w]))
                st.wait()
                v.tensor_tensor(dl[:, k, :], tbuf[n % 2][:, 0:w], dh[:, k, :].bitcast(F32), ALU.subtract).then_inc(S["h_ready"], 1)
            v.wait_ge(S["wg_in"], 64)
            st.done(v.tensor_copy(wgh[:], wgr[:]))
            st.wait()
            v.tensor_tensor(wgl[:], wgr[:], wgh[:].bitcast(F32), ALU.subtract).then_inc(S["wg_split"], 1)
            v.memset(vh[:, :, :, DV:DV + 1].bitcast(F32), 1.0)
            v.memset(vh[:, :, :, DV + 1:VE].bitcast(F32), 0.0)
            v.memset(vl[:, :, :, DV:VE].bitcast(F32), 0.0)
            v.memset(vc[:, :, :, DV:DV + 1], 1.0)
            st.done(v.memset(vc[:, :, :, DV + 1:VE], 0.0))
            low(1, 1, 2048)
            v.wait_ge(S["gates_in"], 1)
            v.wait_ge(S["bias_in"], 64)
            for dst, p0 in ((gI, 0), (gZ, 2 * BWD)):
                for ps, c0, w in ((bank[5], 0, TC), (bank[6], TC, T)):
                    v.tensor_copy(dst[0:BWD, c0:c0 + w], ps[p0:p0 + BWD, 0:w])
                    st.done(v.tensor_copy(dst[BWD:GR, c0:c0 + w], ps[p0 + BWD:p0 + GR, 0:w][:, ::-1]))
            st.wait()
            st.done(v.tensor_scalar(gI[:], gI[:], bi, None, ALU.add))
            st.done(v.tensor_scalar(gZ[:], gZ[:], bf, None, ALU.add))
            st.wait()
            v.scalar_tensor_tensor(gF[:], gZ[:], -1.0, gZ[:], ALU.mult, ALU.max).then_inc(S["g_abs"], 1)
            st.done(v.tensor_scalar(gZ[:], gZ[:], 0.0, None, ALU.min))
            v.wait_ge(S["g_soft"], 1)
            st.wait()
            st.done(v.tensor_tensor(gZ[:], gZ[:], gF[:], ALU.subtract))
            st.wait()
            v.wait_ge(S["ones_in"], 1)
            one = ones[0:GR, 0:1]
            for c0, w in ((0, TC), (TC, T)):
                st.done(v.tensor_tensor_scan(gF[:, c0:c0 + w], one.broadcast_to([GR, w]), gZ[:, c0:c0 + w], 0.0, ALU.mult, ALU.add))
            st.wait()
            st.done(v.tensor_tensor(gI[:], gI[:], gF[:], ALU.subtract))
            st.wait()
            st.done(v.reduce_max(gc, gI[:, 0:TC], AX_X))
            st.wait()
            st.done(v.tensor_scalar(gc, gc, 0.0, None, ALU.max))
            st.wait()
            st.done(v.tensor_tensor(mc, gF[:, TC - 1:TC], gc, ALU.add))
            v.tensor_scalar(ngc, gc, -1.0, None, ALU.mult).then_inc(S["g_u"], 1)
            st.wait()
            st.done(v.tensor_tensor_scan(gG[:], gI[:, TC:], gI[:, TC:], mc, ALU.max, ALU.max))
            st.wait()
            v.tensor_tensor(gF[:, TC:], gF[:, TC:], gG[:], ALU.add).then_inc(S["g_u"], 1)
            v.tensor_scalar(dmc[:], ident[0:GR, 0:GR], mc, None, ALU.mult).then_inc(S["g_nat"], 1)
            v.wait_ge(S["g_em"], 1)
            v.wait_ge(S["g_u"], 2)
            for dst, src in ((gZ[:, 0:TC], gI[:, 0:TC]), (gZ[:, TC:], gI[:, TC:]), (gN[:], gF[:, TC:])):
                v.tensor_copy(dst[0:BWD], src[0:BWD]).then_inc(S["g_nat"], 1)
                v.tensor_copy(dst[BWD:GR], src[BWD:GR][:, ::-1]).then_inc(S["g_nat"], 1)

            def split(dh, dl, ps, sc=None):
                if sc is None:
                    st.done(v.tensor_copy(dh, ps))
                    st.wait()
                    return v.tensor_tensor(dl, ps, dh.bitcast(F32), ALU.subtract)
                st.done(v.tensor_scalar(dh, ps, sc, None, ALU.mult))
                st.wait()
                return v.scalar_tensor_tensor(dl, ps, sc, dh.bitcast(F32), ALU.mult, ALU.subtract)

            for u in range(U_Q, U_V):
                if u + 1 > 1:
                    low(u + 1, (u + 1) % 2, 2048)
                v.wait_ge(S["pe_used"], u + 1)
                b = 3 * (u % 2)
                for m in range(2):
                    f = 2 * (u % 2) + m
                    dh, dl, sc = (qh, ql, float(DK) ** -0.5) if u < U_K else (kh, kl, None)
                    ins = split(dh[:, f, :], dl[:, f, :], bank[b + m][:], sc)
                    if m == 0 or u >= U_K:
                        st.done(ins)
                if u >= U_K:
                    ins = v.tensor_copy(kc[:, :, (u - U_K) * UC:(u - U_K + 1) * UC],
                                        bank[b + 2][:].rearrange("p (t n) -> p t n", t=CTT))
                ins.then_inc(S["evacuated"], 1)
                mod_add(u, u % 4, msum0, V_C)
            v.wait_ge(S["g_turned"], 1)
            v.tensor_copy(gcols[:], bank[6][:, 0:396]).then_inc(S["gcols_in"], 1)
            for u in range(U_V, U_O):
                low(u + 1, (u + 1) % 2, 2048)
                v.wait_ge(S["pe_used"], u + 1)
                b, h = 3 * (u % 2), u - U_V
                for q in range(2):
                    st.done(split(vh[:, 2 * q:2 * q + 2, h, 0:DV], vl[:, 2 * q:2 * q + 2, h, 0:DV],
                                  bank[b + q][:].rearrange("p (t n) -> p t n", t=2)))
                v.tensor_copy(vc[:, :, h, 0:DV], bank[b + 2][:].rearrange("p (t n) -> p t n", t=CTT)).then_inc(S["evacuated"], 1)
                if u == U_V:
                    mod_out(0)
                mod_add(u, u % 4, msum0, V_C)
                if u == U_O - 1:
                    mod_out(1)
            v.tensor_copy(Gnat[0:BWD], gG[0:BWD, :]).then_inc(S["g_nat"], 1)
            v.tensor_copy(Gnat[BWD:GR], gG[BWD:GR, ::-1]).then_inc(S["g_nat"], 1)

            def weigh_keys(i):
                h, r = PERM[i][0], row(i)
                if i >= 1:
                    v.wait_ge(S["s_ready"], 5 * (i - 1) + 1)
                for t in range(CTT):
                    ins = v.tensor_scalar(kw[:, t, :], kc[:, t, h * DK:(h + 1) * DK],
                                          gcols[:, 288 + 36 * t + r:289 + 36 * t + r], None, ALU.mult)
                    if t == CTT - 1:
                        ins.then_inc(S["kw_ready"], 1)
                    else:
                        st.done(ins)
                st.wait()

            def state(i):
                h = PERM[i][0]
                n = 5 * i
                v.wait_ge(S["s_ready"], n + 1)
                if i >= 1:
                    v.wait_ge(S["num_ready"], i)
                st.done(v.tensor_copy(Ch[:], bank[4 + n % 2][:, 0:VE]))
                st.done(v.tensor_tensor(tbuf[2][:], qh[:, h, :].bitcast(F32), ql[:, h, :].bitcast(F32), ALU.add))
                st.wait()
                v.tensor_tensor(Cl[:], bank[4 + n % 2][:, 0:VE], Ch[:].bitcast(F32), ALU.subtract).then_inc(S["s_free"], 1)
                v.wait_ge(S["wi_ready"], i + 1)
                st.done(v.tensor_tensor(tbuf[2][:], tbuf[2][:], WI[:], ALU.mult))
                st.wait()
                st.done(v.tensor_copy(qwh[:], tbuf[2][:]))
                st.wait()
                v.tensor_tensor(qwl[:], tbuf[2][:], qwh[:].bitcast(F32), ALU.subtract).then_inc(S["q_ready"], 1)
                v.wait_ge(S["q_ready"], i + 1)

            def distance(n):
                i, j = n // TT, n % TT
                s_, r = span(i, j)
                v.wait_ge(S["gb_copied"], i + 1)
                v.tensor_scalar(tbuf[n % 2][:, r], tbuf[4 + i % 2][:, r], gcols[:, 36 * s_ + row(i):36 * s_ + row(i) + 1],
                                0.0, ALU.subtract, ALU.max).then_inc(S["d_ready"], 1)

            def weights(n):
                i, j = n // TT, n % TT
                s_, r = span(i, j)
                item = 5 * i + 1 + j
                v.wait_ge(S["e_ready"], n + 1)
                v.wait_ge(S["s_ready"], item + 1)
                w = tbuf[2 + n % 2]
                v.tensor_tensor(w[:, r], tbuf[n % 2][:, r], bank[4 + item % 2][:, r], ALU.mult).then_inc(S["s_free"], 1)
                v.wait_ge(S["s_free"], item + 1)
                dg = slice(s_ * P, (s_ + 1) * P)
                st.done(v.tensor_tensor(w[:, dg], w[:, dg], masks[:, i % 2, :], ALU.mult))
                st.wait()
                if n >= 2:
                    v.wait_ge(S["w_free"], n - 1)
                st.done(v.tensor_copy(Wh[n % 2][:, r], w[:, r]))
                st.wait()
                v.tensor_tensor(Wl[n % 2][:, r], w[:, r], Wh[n % 2][:, r].bitcast(F32), ALU.subtract).then_inc(S["w_ready"], 1)

            def heads_out(i):
                h, d = PERM[i]
                v.wait_ge(S["num_ready"], i + 1)
                for t in range(TT):
                    st.done(v.tensor_copy(hd[:, 16 + t:17 + t], bank[t][:, DV:DV + 1]))
                st.wait()
                em = gcols[:, 144 + row(i):288:36]
                st.done(v.scalar_tensor_tensor(hd[:, 24:28], hd[:, 16:20], -1.0, em, ALU.mult, ALU.max))
                st.wait()
                st.done(v.tensor_tensor(hd[:, 16:20], hd[:, 16:20], hd[:, 24:28], ALU.max))
                st.wait()
                st.done(v.reciprocal(hd[:, 20:24], hd[:, 16:20]))
                st.wait()
                for t in range(TT):
                    dst = hn[:, t, h * DV:(h + 1) * DV]
                    if d == 0:
                        ins = v.tensor_scalar(dst, bank[t][:, 0:DV], hd[:, 20 + t:21 + t], None, ALU.mult)
                    else:
                        ins = v.scalar_tensor_tensor(dst, bank[t][:, 0:DV], hd[:, 20 + t:21 + t], dst, ALU.mult, ALU.add)
                    if t == TT - 1:
                        ins.then_inc(S["num_free"], 1)
                    else:
                        st.done(ins)
                st.wait()
                v.wait_ge(S["num_free"], i + 1)

            v.wait_ge(S["masks_in"], 16)
            v.wait_ge(S["pe_used"], U_O)
            weigh_keys(0)
            state(0)
            distance(0)
            for i in range(2 * NH):
                last = i + 1 == 2 * NH
                for j in range(TT - 1):
                    distance(i * TT + j + 1)
                    weights(i * TT + j)
                if not last:
                    weigh_keys(i + 1)
                weights(i * TT + TT - 1)
                heads_out(i)
                if not last:
                    state(i + 1)
                    distance((i + 1) * TT)
            v.wait_ge(S["h_sq"], TT * NH)
            v.tensor_scalar(hd[:, 0:16], hd[:, 0:16], 1.0 / DV, EPS, ALU.mult, ALU.add).then_inc(S["h_mean"], 1)
            v.wait_ge(S["h_root"], 1)
            st.done(v.reciprocal(hd[:, 0:16], hd[:, 0:16]))
            st.wait()
            for t in range(TT):
                for h in range(NH):
                    z = hn[:, t, h * DV:(h + 1) * DV]
                    v.tensor_scalar(z, z, hd[:, t * NH + h:t * NH + h + 1], None, ALU.mult).then_inc(S["hn_ready"], 1)
            for u in range(U_O, U_OUT):
                low(u + 1, (u + 1) % 2, 2048)
                for m in range(2):
                    n = 2 * (u - U_O) + m
                    v.wait_ge(S["hn_turned"], n + 1)
                    v.wait_ge(S["o_sig"], n + 1)
                    ins = v.scalar_tensor_tensor(tbuf[2 + m][:], bank[6 if m == 0 else 3 * (u % 2) + 2][:],
                                                 vec[:, V_GAIN + n:V_GAIN + n + 1], tbuf[m][:], ALU.mult, ALU.mult)
                    if m == 0:
                        st.done(ins)
                        st.wait()
                    else:
                        ins.then_inc(S["evacuated"], 1)
                        v.wait_ge(S["evacuated"], u + 1)
                    st.done(v.tensor_copy(yh[:, n, :], tbuf[2 + m][:]))
                    st.wait()
                    v.tensor_tensor(yl[:, n, :], tbuf[2 + m][:], yh[:, n, :].bitcast(F32), ALU.subtract).then_inc(S["y_ready"], 1)
                mod_add(u, u % 4, msum0, V_C)

            v.wait_ge(S["mod_evacuated"], 1)
            def out_phase(u0, u1, mod, first_block):
                for u in range(u0, u1):
                    if u + 1 < u1:
                        low(u + 1, (u + 1) % 2, 2048)
                    v.wait_ge(S["pe_used"], u + 1)
                    for m in range(2):
                        n = 2 * (u - u0) + m
                        ins = v.scalar_tensor_tensor(xT[:, n, :], bank[3 * (u % 2) + m][:], mod[:, 16 + n:17 + n],
                                                     xT[:, n, :], ALU.mult, ALU.add)
                        if m == 1:
                            ins.then_inc(S["evacuated"], 1)
                            v.wait_ge(S["evacuated"], u + 1)
                        else:
                            st.done(ins)
                            st.wait()
                        if n == 0:
                            st.done(v.tensor_tensor(acc[:], xT[:, n, :], xT[:, n, :], ALU.mult))
                        else:
                            st.done(v.tensor_tensor(tbuf[3][:], xT[:, n, :], xT[:, n, :], ALU.mult))
                            st.wait()
                            ins = v.tensor_tensor(acc[:], acc[:], tbuf[3][:], ALU.add)
                            if n < KT - 1:
                                st.done(ins)
                            else:
                                ins.then_inc(S["acc_ready"], 1)
                    if first_block:
                        if u == u0:
                            mod_out(2)
                        mod_add(u, u % 4, msum1, V_C)
                    else:
                        if u + 1 == u1:
                            low(u1, 0, 2048)

            v.wait_ge(S["xT_in"], KT)
            out_phase(U_OUT, U_UP, mod1, True)

            def norm_stats(nth):
                v.wait_ge(S["stat_ready"], nth + 1)
                v.tensor_scalar(mean, bank[6][:, 0:TT], 1.0 / D, EPS, ALU.mult, ALU.add).then_inc(S["mean_ready"], 1)
                v.wait_ge(S["root_ready"], nth + 1)
                st.done(v.reciprocal(rstd, mean))
                st.wait()
                for t in range(TT):
                    v.tensor_scalar(tbuf[1][:, t * P:(t + 1) * P], ident[:], rstd[:, t:t + 1], None, ALU.mult).then_inc(S["diag_ready"], 1)
                v.wait_ge(S["bc_ready"], nth + 1 if nth < 2 else nth + 2)

            def reordered(ap, here):
                return ap.rearrange("p (b a c) -> p b a c" if here else "p (c a b) -> p b a c", a=CA, c=CL)

            def norm_dve(nth, dh, dl, move=False):
                if not move:
                    norm_stats(nth)
                for k in range(KT + 1):
                    if k < KT:
                        if move:
                            v.tensor_tensor(reordered(tbuf[2 + k % 2][:], False), reordered(xT[:, k, :], True),
                                            reordered(bank[6][:], True), ALU.mult).then_inc(S["t_ready"], 1)
                        else:
                            v.tensor_tensor(tbuf[2 + k % 2][:], xT[:, k, :], bank[6][:], ALU.mult).then_inc(S["t_ready"], 1)
                    if k >= 1:
                        q = k - 1
                        v.wait_ge(S["n_raw"], nth * KT + q + 1)
                        st.done(v.tensor_copy(dh[:, q, :], tbuf[4 + q % 2][:]))
                        st.wait()
                        v.tensor_tensor(dl[:, q, :], tbuf[4 + q % 2][:], dh[:, q, :].bitcast(F32), ALU.subtract).then_inc(S["n_ready"], 1)

            st.wait()
            v.wait_ge(S["mod_evacuated"], 3)
            st.done(v.scalar_tensor_tensor(A2, mod1[:, 32:40], 1.0, vec[:, V_GFFN:V_GFFN + 8], ALU.add, ALU.mult))
            st.wait()
            low(U_UP, 0, 2048)
            norm_dve(0, hh, hl)

            def up_out(u, i, s, n_next, q, c):
                low(u + 1, 1 - s, n_next)
                v.wait_ge(S["pe_used"], u + 1)
                g, val = bank[3 * s], bank[3 * s + 1]
                am = tbuf[s]

                def tap(j):
                    return vec[:, bass.ds(V_CONV + FT * j + i, 1)]
                W = GRID_W
                st.done(v.tensor_scalar(am[:], g[:], tap(1), vec[:, bass.ds(V_FB + i, 1)], ALU.mult, ALU.add))
                st.wait()
                st.done(v.scalar_tensor_tensor(am[:, W:], g[:, 0:T - W], tap(0), am[:, W:], ALU.mult, ALU.add))
                st.wait()
                v.scalar_tensor_tensor(am[:, 0:T - W], g[:, W:], tap(2), am[:, 0:T - W], ALU.mult, ALU.add).then_inc(S["glu_a"], 1)
                v.wait_ge(S["glu_s"], i + 1)
                v.tensor_tensor(tbuf[4 + s][:], tbuf[2 + s][:], val[:], ALU.mult).then_inc(S["evacuated"], 1)
                v.wait_ge(S["evacuated"], u + 1)
                f3 = tbuf[4 + s][:].rearrange("p (a n) -> p a n", a=1)
                st.done(v.tensor_copy(fh[:, bass.ds(i, 1), :], f3))
                st.wait()
                v.tensor_tensor(fl[:, bass.ds(i, 1), :], f3, fh[:, bass.ds(i, 1), :].bitcast(F32), ALU.subtract).then_inc(S["f_ready"], 1)
                if q == 0:
                    mod_out(c)
                mod_add(u, q, msum1, V_C2)

            PER = 4 * 4
            with v.Fori(0, FT // 4) as i:
                st.enter(i, PER)
                for q in range(4):
                    up_out(U_UP + 4 * i + q, 4 * i + q, q % 2, 2048, q, 3 + i)
            st.leave(FT // 4, PER)
            up_out(U_DOWN - 2, FT - 2, 0, 2048, 0, 3 + FT // 4)
            up_out(U_DOWN - 1, FT - 1, 1, FH * P, 1, 3 + FT // 4)
            mod_add(U_DOWN, 2, msum1, V_C2)

            def down_out(m, b, gate0, first, last, n_next=2048):
                u = m * 2 + U_DOWN
                low(u + 1, 1, FH * P)
                low(u + 2, 0, n_next if last else FH * P)
                v.wait_ge(S["pe_used"], u + 2)
                xm = xT[:, bass.ds(m, 1), :]
                v.scalar_tensor_tensor(xm, bank[b][:].rearrange("p (a n) -> p a n", a=1), mod1[:, bass.ds(gate0 + m, 1)], xm,
                                       ALU.mult, ALU.add).then_inc(S["evacuated"], 1)
                v.wait_ge(S["evacuated"], u + 1)
                sq = tbuf[5][:].rearrange("p (a n) -> p a n", a=1)
                st.done(v.tensor_tensor(sq, xm, xm, ALU.mult))
                st.wait()
                if first:
                    st.done(v.tensor_scalar(acc2[:], tbuf[5][:], G2[:, 0:1], None, ALU.mult))
                    v.tensor_copy(acc[:], tbuf[5][:]).then_inc(S["evacuated"], 1)
                else:
                    st.done(v.scalar_tensor_tensor(acc2[:], tbuf[5][:], G2[:, bass.ds(m, 1)], acc2[:], ALU.mult, ALU.add))
                    v.tensor_tensor(acc[:], acc[:], tbuf[5][:], ALU.add).then_inc(S["evacuated"], 1)
                st.wait()
                v.wait_ge(S["evacuated"], u + 2)

            st.done(v.tensor_tensor(G2, vec[:, V_GFIN:V_GFIN + 8], vec[:, V_GFIN:V_GFIN + 8], ALU.mult))
            st.wait()
            v.wait_ge(S["mod_evacuated"], 4)
            down_out(0, 0, 40, True, False)
            mod_add(U_DOWN + 1, 3, msum1, V_C2)
            down_out(1, 3, 40, False, False)
            mod_out(9)
            with v.Fori(1, KT // 2 - 1) as i:
                st.enter(i - 1, 4)
                for s in range(2):
                    down_out(2 * i + s, 3 * s, 40, False, False)
            st.leave(KT // 2 - 2, 4)
            down_out(KT - 2, 0, 40, False, False)
            down_out(KT - 1, 3, 40, False, True)
            v.wait_ge(S["mod_evacuated"], 10)
            st.done(v.scalar_tensor_tensor(A3, mod2[:, 8:16], 1.0, vec[:, V_NMIX:V_NMIX + 8], ALU.add, ALU.mult))
            st.done(v.scalar_tensor_tensor(A2, mod2[:, 32:40], 1.0, vec[:, V_NFFN:V_NFFN + 8], ALU.add, ALU.mult))
            st.wait()
            st.done(v.tensor_tensor(A3, A3, vec[:, V_GFIN:V_GFIN + 8], ALU.mult))
            v.wait_ge(S["stat_ready"], 2)
            v.tensor_scalar(mean, bank[6][:, 0:TT], 1.0 / D, EPS, ALU.mult, ALU.add).then_inc(S["mean_ready"], 1)
            st.done(v.tensor_scalar(mean2, bank[6][:, TT:2 * TT], 1.0 / D, None, ALU.mult))
            v.wait_ge(S["root_ready"], 2)
            st.done(v.reciprocal(rstd, mean))
            st.wait()
            st.done(v.tensor_tensor(r12, rstd, rstd, ALU.mult))
            st.wait()
            st.done(v.tensor_tensor(mean2, mean2, r12, ALU.mult))
            st.wait()
            v.tensor_scalar(mean2, mean2, EPS, None, ALU.add).then_inc(S["mean2_ready"], 1)
            v.wait_ge(S["root2_ready"], 1)
            st.done(v.reciprocal(mean2, mean2))
            st.wait()
            st.done(v.tensor_tensor(r12, rstd, mean2, ALU.mult))
            st.wait()
            for cols, dg in ((r12, tbuf[1]), (rstd, tbuf[0])):
                for t in range(TT):
                    v.tensor_scalar(dg[:, t * P:(t + 1) * P], ident[:], cols[:, t:t + 1], None, ALU.mult).then_inc(S["diag_ready"], 1)
            v.wait_ge(S["bc_ready"], 2)
            norm_dve(1, hh, hl, move=True)
            v.wait_ge(S["bc_ready"], 3)
            for u in range(U_QKV2, U_GZ):
                low(u + 1, (u + 1) % 2, 2048)
                k = u - U_QKV2
                if k < KT:
                    st.done(v.tensor_tensor(tbuf[k % 2][:], xT[:, k, :], bank[7][:], ALU.mult))
                    st.wait()
                    v.tensor_scalar(reordered(xT[:, k, :], False), reordered(tbuf[k % 2][:], True),
                                    vec[:, V_GFIN + k:V_GFIN + k + 1], None, ALU.mult).then_inc(S["rescaled"], 1)
                if k == 7:
                    v.wait_ge(S["wf_in"], 16)
                    st.done(v.tensor_copy(wfh[:], wfr[:]))
                    st.wait()
                    v.tensor_tensor(wfl[:], wfr[:], wfh[:].bitcast(F32), ALU.subtract).then_inc(S["wf_split"], 1)
                v.wait_ge(S["pe_used"], u + 1)
                b = 3 * (u % 2)
                for m in range(2):
                    if k in (6, 7, 8, 11):
                        c0 = (k - 6) * UC if k < 9 else WA
                        ins = v.tensor_copy(v2[:, 2 * m:2 * m + 2, c0:c0 + UC], bank[b + m][:].rearrange("p (t n) -> p t n", t=2))
                    else:
                        tile = 2 * k if k < 6 else 12 + 2 * (k - 9)
                        ins = v.tensor_copy(qk[:, tile + m, :], bank[b + m][:])
                    if m == 0:
                        st.done(ins)
                    else:
                        ins.then_inc(S["evacuated"], 1)
                if k == 8:
                    v.wait_ge(S["f_logits"], 1)
                    v.wait_ge(S["bf_in"], 16)
                    st.done(v.tensor_scalar(reordered(fA[:], True), reordered(bank[6][0:NHB, :], False), small[0:NHB, 44:45], None, ALU.add))
                    st.wait()
                    v.scalar_tensor_tensor(fB[:], fA[:], -1.0, fA[:], ALU.mult, ALU.max).then_inc(S["f_abs"], 1)
                    st.done(v.tensor_scalar(fA[:], fA[:], 0.0, None, ALU.min))
                    v.wait_ge(S["f_soft"], 1)
                    st.wait()
                    st.done(v.tensor_tensor(fA[:], fA[:], fB[:], ALU.subtract))
                    st.wait()
                    st.done(v.tensor_tensor_scan(fF[:], ones[0:NHB, 0:1].broadcast_to([NHB, T]), fA[:], 0.0, ALU.mult, ALU.add))
                    st.wait()
                    v.tensor_scalar(reordered(fB[:], False), reordered(fF[:], True), -1.0 / QK_SCALE, None, ALU.mult).then_inc(S["f_neg"], 1)
            for h in range(NHB):
                v.wait_ge(S["fb_ready"], h + 1)
                v.tensor_copy(FB[:, h, :], bank[6 + h % 2][:]).then_inc(S["fb_copied"], 1)
            v.wait_ge(S["tab_in"], 48)
            for r in range(ROUNDS + 3):
                if r < ROUNDS:
                    b, Lr = 2 * (r % 2), L[r % 2]
                    v.wait_ge(S["qk_ready"], r + 1)
                    if r >= 2:
                        v.wait_ge(S["tr_ready"], r - 1)
                    if r < ROUNDS_A:
                        i, c = r // CL, r % CL
                        for g, (dst, dist, src) in enumerate((
                                (Lr[:, 0:T], dist0[:, c, :], bank[b][:]),
                                (Lr[:, T:T + P], dist12[:, 0, :], bank[b + 1][:, 0:P]),
                                (Lr[:, T + P:], dist12[:, 1, :], bank[b + 1][:, P:2 * P]))):
                            ins = v.scalar_tensor_tensor(dst, dist, -SLOPES[GH * g + i] / QK_SCALE, src, ALU.mult, ALU.add)
                            if g < 2:
                                st.done(ins)
                        ins.then_inc(S["l_free"], 1)
                        w = KEYS_A
                    else:
                        q = r - ROUNDS_A
                        v.wait_ge(S["cf_ready"], q + 1)
                        v.tensor_tensor(Lr[:, 0:T], CF[q % 2][:], bank[b][:], ALU.add).then_inc(S["l_free"], 1)
                        w = T
                    v.wait_ge(S["l_free"], r + 1)
                    st.wait()
                    ins = v.reduce_max(nmax[:, r % 4:r % 4 + 1], Lr[:, 0:w], AX_X)
                    st.done(ins)
                    st.wait()
                    v.tensor_scalar(nmax[:, r % 4:r % 4 + 1], nmax[:, r % 4:r % 4 + 1], -QK_SCALE, None, ALU.mult).then_inc(S["l_ready"], 1)
                if r >= 3:
                    q = r - 3
                    v.wait_ge(S["o_ready"], q + 1)
                    st.done(v.reciprocal(rsum[:, q % 4:q % 4 + 1], lsum[:, q % 4:q % 4 + 1]))
                    st.wait()
                    c = q % CL
                    c0 = (q // CL) * HD if q < ROUNDS_A else GH * HD + (q - ROUNDS_A) // CL * HD
                    v.tensor_scalar(on[:, c, c0:c0 + HD], bank[6 + q % 2][:, 0:HD], rsum[:, q % 4:q % 4 + 1], None, ALU.mult).then_inc(S["o_free"], 1)
            for u in range(U_GZ, U_OUT2):
                low(u + 1, (u + 1) % 2, 2048)
                m, s = u - U_GZ, u % 2
                v.wait_ge(S["pe_used"], u + 1)
                v.wait_ge(S["g_sig"], 2 * m + 2)
                st.done(v.tensor_tensor(tbuf[2][:], tbuf[0][:], bank[3 * s + 2][:], ALU.mult))
                v.tensor_tensor(tbuf[3][:], tbuf[1][:], bank[6 + s][:], ALU.mult).then_inc(S["evacuated"], 1)
                v.wait_ge(S["evacuated"], u + 1)
                st.wait()
                st.done(v.tensor_tensor(tbuf[2][:], tbuf[2][:], tbuf[3][:], ALU.add))
                st.wait()
                st.done(v.tensor_copy(mh[:, m, :], tbuf[2][:]))
                st.wait()
                v.tensor_tensor(ml[:, m, :], tbuf[2][:], mh[:, m, :].bitcast(F32), ALU.subtract).then_inc(S["m_ready"], 1)
            v.wait_ge(S["rescaled"], KT)
            out_phase(U_OUT2, U_IN2, mod2, False)
            norm_dve(2, hh, hl)

            def in_out(u, i, s, n_next):
                low(u + 1, 1 - s, n_next)
                v.wait_ge(S["pe_used"], u + 1)
                v.wait_ge(S["glu_s"], FT + i + 1)
                v.tensor_tensor(tbuf[4 + s][:], tbuf[2 + s][:], bank[3 * s + 1][:], ALU.mult).then_inc(S["evacuated"], 1)
                v.wait_ge(S["evacuated"], u + 1)
                f3 = tbuf[4 + s][:].rearrange("p (a n) -> p a n", a=1)
                st.done(v.tensor_copy(fh[:, bass.ds(i, 1), :], f3))
                st.wait()
                v.tensor_tensor(fl[:, bass.ds(i, 1), :], f3, fh[:, bass.ds(i, 1), :].bitcast(F32), ALU.subtract).then_inc(S["f_ready"], 1)

            with v.Fori(0, FT // 2 - 1) as i:
                st.enter(i, 2)
                for s in range(2):
                    in_out(U_IN2 + 2 * i + s, 2 * i + s, s, 2048)
            st.leave(FT // 2 - 1, 2)
            in_out(U_DOWN2 - 2, FT - 2, 0, 2048)
            in_out(U_DOWN2 - 1, FT - 1, 1, FH * P)

            def last_out(m, q, first=False, last=False):
                u = m * 2 + U_DOWN2
                low(u + 1, 1, FH * P)
                if not last:
                    low(u + 2, 0, FH * P)
                v.wait_ge(S["pe_used"], u + 2)
                xm = xT[:, bass.ds(m, 1), :]
                v.scalar_tensor_tensor(xm, bank[3 * q][:].rearrange("p (a n) -> p a n", a=1), mod2[:, bass.ds(40 + m, 1)], xm,
                                       ALU.mult, ALU.add).then_inc(S["evacuated"], 1)
                v.wait_ge(S["evacuated"], u + 1)
                if not isinstance(m, int) or m >= 2:
                    v.wait_ge(S["fin_turned"], m - 1)
                v.tensor_scalar(tbuf[2 + q][:].rearrange("p (a n) -> p a n", a=1), xm, vec[:, bass.ds(V_NFIN + m, 1)], None,
                                ALU.mult).then_inc(S["xg_ready"], 1)
                if first:
                    v.tensor_tensor(acc[:].rearrange("p (a n) -> p a n", a=1), xm, xm, ALU.mult).then_inc(S["evacuated"], 1)
                else:
                    st.done(v.tensor_tensor(tbuf[5][:].rearrange("p (a n) -> p a n", a=1), xm, xm, ALU.mult))
                    st.wait()
                    v.tensor_tensor(acc[:], acc[:], tbuf[5][:], ALU.add).then_inc(S["evacuated"], 1)
                v.wait_ge(S["evacuated"], u + 2)

            last_out(0, 0, first=True)
            last_out(1, 1)
            with v.Fori(1, KT // 2 - 1) as i:
                st.enter(i - 1, 2)
                for q in range(2):
                    last_out(2 * i + q, q)
            st.leave(KT // 2 - 2, 2)
            last_out(KT - 2, 0)
            last_out(KT - 1, 1, last=True)
            v.wait_ge(S["stat_ready"], 4)
            v.tensor_scalar(mean, bank[0][:, 0:TT], 1.0 / D, EPS, ALU.mult, ALU.add).then_inc(S["mean_ready"], 1)
            v.wait_ge(S["root_ready"], 4)
            st.done(v.reciprocal(rstd, mean))
            st.wait()
            v.wait_ge(S["fin_copied"], KT)
            for c in (0, 2):
                v.tensor_scalar(fin[:, c, :], fin[:, c, :], rstd[:, c:c + 1], None, ALU.mult).then_inc(S["scaled"], 1)

        @block.tensor
        def _(pe):
            def mm3(dst, ah, al, bh, bl, first, last):
                pe.matmul(dst, ah, bh, start=first, stop=False)
                pe.matmul(dst, ah, bl, start=False, stop=False)
                return pe.matmul(dst, al, bh, start=False, stop=last)

            def unit(u):
                if isinstance(u, int):
                    pe.wait_ge(S["lo_ready"], u + 1)
                    if u >= 2:
                        pe.wait_ge(S["evacuated"], u - 1)
                else:
                    pe.wait_ge(S["lo_ready"], u + 1)
                    pe.wait_ge(S["evacuated"], u - 1)

            def features(s, bh, bl, m, b, k):
                return mm3(bank[b][:], whi[s][:, k * UC + m * P:k * UC + (m + 1) * P],
                           wlo[s][:, k * UC + m * P:k * UC + (m + 1) * P], bh[:, k, :], bl[:, k, :], k == 0, k == KT - 1)

            def mod_chunk(c, acc_m):
                pe.wait_ge(S["mod_used"], (c + 1) * 4)
                if not isinstance(c, int) or c >= 1:
                    pe.wait_ge(S["mod_evacuated"], c)
                for m in range(KT):
                    ins = pe.matmul(bank[7][:, m:m + 1], acc_m[:, m * P:(m + 1) * P], ones[:, 0:1], start=True, stop=True)
                ins.then_inc(S["mod_sum"], 1)

            pe.wait_ge(S["vecs_in"], 14 * 16)
            pe.wait_ge(S["consts_in"], 16)
            for i in range(3):
                c = (P, V_CONV - P, 3 * FT)[i]
                pe.transpose(bank[i][:, 0:c], vrow[i][0:c, :], ident[0:c, 0:c]).then_inc(S["vec_t"], 1)
            pe.wait_ge(S["silu_c"], 1)
            for k in range(KT):
                pe.wait_ge(S[f"wm_in{k}"], 16)
                for q in range(4):
                    ins = pe.matmul(bank[q][0:2, :], sil[:, k:16:8], wm[:, k, q * 512:(q + 1) * 512],
                                    start=(k == 0), stop=(k == KT - 1))
            ins.then_inc(S["pe_mod0"], 1)
            for m in range(16):
                if m % 4 == 0:
                    pe.wait_ge(S["mod_rows"], m // 4 + 1)
                ins = pe.transpose(bank[7][:, 2 * m:2 * m + 2], mrow[:, m * P:(m + 1) * P], ident[0:2, 0:2])
            ins.then_inc(S["pe_mod0"], 1)
            pe.wait_ge(S["vec_cols"], 3)
            pe.wait_ge(S["x_scaled"], TT + CTT)
            for n in range(2 * KT):
                k, t0, nt = n // 2, (0, TT)[n % 2], (TT, CTT)[n % 2]
                if n >= 6:
                    pe.wait_ge(S["h_raw"], n - 5)
                for t in range(nt):
                    ins = pe.transpose(bank[n % 6][:, t * P:(t + 1) * P], xn[:, t0 + t, k * P:(k + 1) * P], ident[:])
                ins.then_inc(S["x_turned"], 1)
            pe.wait_ge(S["h_ready"], 2 * KT)
            pe.wait_ge(S["wg_split"], 1)
            for bh, bl, ps, w in ((hh, hl, bank[6], T), (hch, hcl, bank[5], TC)):
                for k in range(KT):
                    ins = mm3(ps[0:NG, 0:w], wgh[:, k, :], wgl[:, k, :], bh[:, k, :], bl[:, k, :], k == 0, k == KT - 1)
            ins.then_inc(S["gates_in"], 1)
            pe.wait_ge(S["mod0_cols"], 4)

            def tokens(u, n, hs, ls, t, dst):
                for k in range(KT):
                    ins = mm3(dst, hs[:, k, t * P:(t + 1) * P], ls[:, k, t * P:(t + 1) * P],
                              whi[u % 2][:, k * UC:(k + 1) * UC], wlo[u % 2][:, k * UC:(k + 1) * UC], k == 0, k == KT - 1)
                return ins

            for u in range(U_Q, U_V):
                unit(u)
                b = 3 * (u % 2)
                for m in range(2):
                    for k in range(KT):
                        ins = features(u % 2, hh, hl, m, b + m, k)
                if u >= U_K:
                    for t in range(CTT):
                        ins = tokens(u, 0, hch, hcl, t, bank[b + 2][:, t * UC:(t + 1) * UC])
                ins.then_inc(S["pe_used"], 1)
            pe.wait_ge(S["g_nat"], 7)
            for t in range(TT):
                pe.transpose(bank[6][:, 36 * t:36 * t + GR], gZ[:, TC + t * P:TC + (t + 1) * P], ident[0:GR, 0:GR])
                pe.transpose(bank[6][:, 144 + 36 * t:144 + 36 * t + GR], gN[:, t * P:(t + 1) * P], ident[0:GR, 0:GR])
            for t in range(CTT):
                pe.transpose(bank[6][:, 288 + 36 * t:288 + 36 * t + GR], gZ[:, t * P:(t + 1) * P], ident[0:GR, 0:GR])
            pe.matmul(bank[6][:, 360:360 + GR], ones[0:GR, :], dmc[:], start=True, stop=True).then_inc(S["g_turned"], 1)
            for u in range(U_V, U_O):
                unit(u)
                b = 3 * (u % 2)
                for t in range(TT):
                    tokens(u, 0, hh, hl, t, bank[b + t // 2][:, (t % 2) * UC:(t % 2 + 1) * UC])
                for t in range(CTT):
                    ins = tokens(u, 0, hch, hcl, t, bank[b + 2][:, t * UC:(t + 1) * UC])
                ins.then_inc(S["pe_used"], 1)
                if u == U_V:
                    mod_chunk(0, msum0)
                if u == U_O - 1:
                    mod_chunk(1, msum0)

            def broadcast(i):
                if i >= 2:
                    pe.wait_ge(S["gb_copied"], i - 1)
                pe.matmul(bank[6 + i % 2][:], ident[0:GR, row(i):row(i) + 1].broadcast_to([GR, P]), Gnat[:],
                          start=True, stop=True).then_inc(S["gb_ready"], 1)

            def state(i):
                h, n = PERM[i][0], 5 * i
                pe.wait_ge(S["kw_ready"], i + 1)
                if n >= 2:
                    pe.wait_ge(S["s_free"], n - 1)
                for t in range(CTT):
                    ins = pe.matmul(bank[4 + n % 2][:, 0:VE], kw[:, t, :], vc[:, t, h, :], start=(t == 0), stop=(t == CTT - 1))
                ins.then_inc(S["s_ready"], 1)

            def scores(n):
                i, j = n // TT, n % TT
                h, (s_, r), item = PERM[i][0], span(i, j), 5 * i + 1 + j
                if item >= 2:
                    pe.wait_ge(S["s_free"], item - 1)
                ks = slice(s_ * P, (s_ + 1) * P)
                mm3(bank[4 + item % 2][:, r], kh[:, h, ks], kl[:, h, ks], qh[:, h, r], ql[:, h, r], True, True).then_inc(S["s_ready"], 1)

            def apply(n):
                i, j = n // TT, n % TT
                h, (s_, r) = PERM[i][0], span(i, j)
                pe.wait_ge(S["w_ready"], n + 1)
                if j == 0 and i >= 1:
                    pe.wait_ge(S["num_free"], i)
                for t in range(r.start // P, r.stop // P):
                    c = slice(t * P, (t + 1) * P)
                    ins = mm3(bank[t][:, 0:VE], Wh[n % 2][:, c], Wl[n % 2][:, c], vh[:, s_, h, :], vl[:, s_, h, :], j == 0, False)
                ins.then_inc(S["w_free"], 1)

            def carried(i):
                pe.wait_ge(S["q_ready"], i + 1)
                for t in range(TT):
                    c = slice(t * P, (t + 1) * P)
                    ins = mm3(bank[t][:, 0:VE], qwh[:, c], qwl[:, c], Ch[:], Cl[:], False, True)
                ins.then_inc(S["num_ready"], 1)

            pe.wait_ge(S["g_nat"], 9)
            pe.wait_ge(S["mod_evacuated"], 2)
            pe.wait_ge(S["gcols_in"], 1)
            pe.wait_ge(S["evacuated"], U_O)
            broadcast(0)
            state(0)
            scores(0)
            for i in range(2 * NH):
                last = i + 1 == 2 * NH
                for j in range(1, TT):
                    scores(i * TT + j)
                    apply(i * TT + j - 1)
                if not last:
                    broadcast(i + 1)
                    state(i + 1)
                apply(i * TT + TT - 1)
                carried(i)
                if not last:
                    scores((i + 1) * TT)
            for u in range(U_O, U_OUT):
                unit(u)
                if u == U_O:
                    pe.wait_ge(S["num_free"], 2 * NH)
                b = 3 * (u % 2)
                for m in range(2):
                    for k in range(KT):
                        ins = features(u % 2, hh, hl, m, b + m, k)
                ins.then_inc(S["pe_used"], 1)
                if u == U_O:
                    pe.wait_ge(S["hn_ready"], TT * NH)
                if u >= U_O + 1:
                    pe.wait_ge(S["evacuated"], u)
                for m in range(2):
                    f = 2 * (u - U_O) + m
                    for t in range(TT):
                        ins = pe.transpose(bank[6 if m == 0 else b + 2][:, t * P:(t + 1) * P], hn[:, t, f * P:(f + 1) * P], ident[:])
                    ins.then_inc(S["hn_turned"], 1)
            pe.wait_ge(S["xr_in"], 16)
            pe.wait_ge(S["evacuated"], U_OUT)
            for k in range(KT):
                if k >= 2:
                    pe.wait_ge(S["xT_in"], k - 1)
                for t in range(TT):
                    ins = pe.transpose(bank[6 if k % 2 == 0 else 7][:, t * P:(t + 1) * P], xr[:, t, k * P:(k + 1) * P], ident[:])
                ins.then_inc(S["xr_turned"], 1)
            pe.wait_ge(S["xT_in"], KT)
            for u in range(U_OUT, U_UP):
                unit(u)
                if u == U_OUT:
                    pe.wait_ge(S["y_ready"], KT)
                for m in range(2):
                    for k in range(KT):
                        ins = features(u % 2, yh, yl, m, 3 * (u % 2) + m, k)
                ins.then_inc(S["pe_used"], 1)
                if u == U_OUT:
                    mod_chunk(2, msum0)

            def norm_pe(nth, diag0):
                for t in range(TT):
                    ins = pe.matmul(bank[6][:, t:t + 1], acc[:, t * P:(t + 1) * P], ones[:, 0:1], start=True, stop=True)
                ins.then_inc(S["stat_ready"], 1)
                pe.wait_ge(S["mean_ready"], nth + 1)
                for t in range(TT):
                    pe.wait_ge(S["diag_ready"], diag0 + t + 1)
                    ins = pe.matmul(bank[6][:, t * P:(t + 1) * P], ones[:], tbuf[1][:, t * P:(t + 1) * P], start=True, stop=True)
                ins.then_inc(S["bc_ready"], 1)

            pe.wait_ge(S["acc_ready"], 1)
            norm_pe(0, 0)

            def up_unit(u, i, s, nth=None, mod=None):
                unit(u)
                for k in range(KT):
                    if nth is not None:
                        pe.wait_ge(S["n_ready"], nth * KT + k + 1)
                    for m in range(2):
                        ins = features(s, hh, hl, m, 3 * s + m, k)
                ins.then_inc(S["pe_used"], 1)
                if mod is not None:
                    mod_chunk(mod, msum1)

            for q in range(4):
                up_unit(U_UP + q, q, q % 2, nth=None if q else 0, mod=None if q else 3)
            with pe.Fori(1, FT // 4) as i:
                for q in range(4):
                    up_unit(U_UP + 4 * i + q, 4 * i + q, q % 2, mod=None if q else 3 + i)
            for q in range(FT % 4):
                up_unit(U_UP + FT // 4 * 4 + q, FT // 4 * 4 + q, q % 2, mod=None if q else 3 + FT // 4)

            def down_tile(m, b, first=False, base=U_DOWN, f0=0):
                for s in range(2):
                    u = m * 2 + base + s
                    pe.wait_ge(S["lo_ready"], u + 1)
                    if s == 0:
                        pe.wait_ge(S["evacuated"], u - 1 if first else u - 2)
                    for k in range(FH):
                        f = s * FH + k
                        if first and s == 0 and k == 0:
                            pe.wait_ge(S["f_ready"], f0 + FT - 2)
                        if first and f == FT - 2:
                            pe.wait_ge(S["f_ready"], f0 + FT)
                        ins = mm3(bank[b][:], whi[s][:, k * P:(k + 1) * P], wlo[s][:, k * P:(k + 1) * P],
                                  fh[:, f, :], fl[:, f, :], f == 0, f == FT - 1)
                    ins.then_inc(S["pe_used"], 1)

            down_tile(0, 0, True)
            down_tile(1, 3)
            mod_chunk(9, msum1)
            with pe.Fori(1, KT // 2) as i:
                for s in range(2):
                    down_tile(2 * i + s, 3 * s)

            pe.wait_ge(S["evacuated"], U_QKV2)
            for n, sums in enumerate((acc, acc2)):
                for t in range(TT):
                    ins = pe.matmul(bank[6][:, n * TT + t:n * TT + t + 1], sums[:, t * P:(t + 1) * P], ones[:, 0:1], start=True, stop=True)
            ins.then_inc(S["stat_ready"], 1)
            pe.wait_ge(S["mean2_ready"], 1)
            for n in range(2):
                for t in range(TT):
                    pe.wait_ge(S["diag_ready"], TT + n * TT + t + 1)
                    ins = pe.matmul(bank[6 + n][:, t * P:(t + 1) * P], ones[:], tbuf[1 - n][:, t * P:(t + 1) * P], start=True, stop=True)
                ins.then_inc(S["bc_ready"], 1)
            for u in range(U_QKV2, U_GZ):
                unit(u)
                k0, s = u - U_QKV2, u % 2
                b = 3 * s
                if k0 in (6, 7, 8, 11):
                    for t in range(TT):
                        ins = tokens(u, 0, hh, hl, t, bank[b + t // 2][:, (t % 2) * UC:(t % 2 + 1) * UC])
                else:
                    for k in range(KT):
                        if k0 == 0:
                            pe.wait_ge(S["n_ready"], KT + k + 1)
                        for m in range(2):
                            ins = features(s, hh, hl, m, b + m, k)
                ins.then_inc(S["pe_used"], 1)
                if k0 == 8:
                    pe.wait_ge(S["wf_split"], 1)
                    for k in range(KT):
                        ins = mm3(bank[6][0:NF, :], wfh[:, k, :], wfl[:, k, :], hh[:, k, :], hl[:, k, :], k == 0, k == KT - 1)
                    ins.then_inc(S["f_logits"], 1)
            pe.wait_ge(S["f_neg"], 1)
            pe.wait_ge(S["rescaled"], KT)
            for h in range(NHB):
                if h >= 2:
                    pe.wait_ge(S["fb_copied"], h - 1)
                pe.matmul(bank[6 + h % 2][:], ident[0:NHB, h:h + 1].broadcast_to([NHB, P]), fB[:], start=True, stop=True).then_inc(S["fb_ready"], 1)

            def logits(r):
                b = 2 * (r % 2)
                if r >= 2:
                    pe.wait_ge(S["l_free"], r - 1)
                c = r % CL
                cc = slice(c * P, (c + 1) * P)
                if r < ROUNDS_A:
                    i = r // CL
                    pp = slice((i % 2) * HD, (i % 2 + 1) * HD)
                    for g, (dst, keys) in enumerate(((bank[b][:], slice(0, T)), (bank[b + 1][:, 0:P], cc), (bank[b + 1][:, P:2 * P], cc))):
                        tile = (GH * g + i) // 2
                        ins = pe.matmul(dst, qk[pp, tile, cc], qk[pp, NHA // 2 + tile, keys], start=True, stop=True)
                else:
                    h = (r - ROUNDS_A) // CL
                    pp = slice((h % 2) * HD, (h % 2 + 1) * HD)
                    ins = pe.matmul(bank[b][:], qk[pp, 12 + h // 2, cc], qk[pp, 14 + h // 2, :], start=True, stop=True)
                ins.then_inc(S["qk_ready"], 1)

            def turn(r):
                pe.wait_ge(S["p_ready"], r + 1)
                if r >= 1:
                    pe.wait_ge(S["pt_copied"], r)
                for j in range(KEYS_A // P if r < ROUNDS_A else TT):
                    ins = pe.transpose(bank[4 + j // 4][:, (j % 4) * P:(j % 4 + 1) * P], L[r % 2][:, j * P:(j + 1) * P], ident[:])
                ins.then_inc(S["tr_ready"], 1)

            def values(r):
                pe.wait_ge(S["pt_copied"], r + 1)
                if r >= 2:
                    pe.wait_ge(S["o_free"], r - 1)
                c = r % CL
                if r < ROUNDS_A:
                    i = r // CL
                    terms = [(j, j, i) for j in range(TT)] + [(TT, c, GH + i), (TT + 1, c, 2 * GH + i)]
                else:
                    terms = [(j, j, NHA + (r - ROUNDS_A) // CL) for j in range(TT)]
                for n, (j, tile, head) in enumerate(terms):
                    ins = pe.matmul(bank[6 + r % 2][:, 0:HD], PT[r % 2][:, j * P:(j + 1) * P], v2[:, tile, head * HD:(head + 1) * HD],
                                    start=(n == 0), stop=(n == len(terms) - 1))
                ins.then_inc(S["o_ready"], 1)

            pe.wait_ge(S["evacuated"], U_GZ)
            for r in range(ROUNDS + 2):
                if r < ROUNDS:
                    logits(r)
                if 1 <= r <= ROUNDS:
                    turn(r - 1)
                if r >= 2:
                    if r == 2:
                        pe.wait_ge(S["fb_copied"], NHB)
                    values(r - 2)

            for u in range(U_GZ, U_OUT2):
                unit(u)
                m, s = u - U_GZ, u % 2
                if m == 0:
                    pe.wait_ge(S["l_free"], ROUNDS)
                for g in range(2):
                    for k in range(KT):
                        features(s, hh, hl, g, 3 * s + g, k)
                if m == 0:
                    pe.wait_ge(S["pt_copied"], ROUNDS)
                    pe.wait_ge(S["o_free"], ROUNDS)
                    for f in range(4):
                        for c in range(CL):
                            ins = pe.transpose(bank[4 + f][:, c * P:(c + 1) * P], on[:, c, f * P:(f + 1) * P], ident[:])
                        ins.then_inc(S["on_turned"], 1)
                    pe.wait_ge(S["att_ready"], 4)
                    pe.wait_ge(S["up_in"], 32)
                for w, b, f0 in ((upA, 3 * s + 2, 0), (upB, 6 + s, 2)):
                    for k in range(2):
                        ins = pe.matmul(bank[b][:], w[:, k, m * P:(m + 1) * P], att[:, f0 + k, :], start=(k == 0), stop=(k == 1))
                ins.then_inc(S["pe_used"], 1)
            for u in range(U_OUT2, U_IN2):
                unit(u)
                if u == U_OUT2:
                    pe.wait_ge(S["m_ready"], KT)
                for m in range(2):
                    for k in range(KT):
                        ins = features(u % 2, mh, ml, m, 3 * (u % 2) + m, k)
                ins.then_inc(S["pe_used"], 1)
            pe.wait_ge(S["acc_ready"], 2)
            norm_pe(2, 3 * TT)
            up_unit(U_IN2, 0, 0, nth=2)
            up_unit(U_IN2 + 1, 1, 1)
            with pe.Fori(1, FT // 2) as i:
                for s in range(2):
                    up_unit(U_IN2 + 2 * i + s, 2 * i + s, s)

            def turn_out(m, q):
                pe.wait_ge(S["xg_ready"], m + 1)
                if not isinstance(m, int) or m >= 2:
                    pe.wait_ge(S["fin_copied"], m - 1)
                for c in range(CL):
                    ins = pe.transpose(bank[6 + q][:, c * P:(c + 1) * P], tbuf[2 + q][:, c * P:(c + 1) * P], ident[:])
                ins.then_inc(S["fin_turned"], 1)

            down_tile(0, 0, True, U_DOWN2, FT)
            down_tile(1, 3, False, U_DOWN2)
            turn_out(0, 0)
            with pe.Fori(1, KT // 2) as i:
                for q in range(2):
                    down_tile(2 * i + q, 3 * q, False, U_DOWN2)
                    turn_out(2 * i + q - 1, 1 - q)
            turn_out(KT - 1, 1)
            pe.wait_ge(S["evacuated"], U_END)
            for t in range(TT):
                ins = pe.matmul(bank[0][:, t:t + 1], acc[:, t * P:(t + 1) * P], ones[:, 0:1], start=True, stop=True)
            ins.then_inc(S["stat_ready"], 1)


_INS = ["x", "c", "ctx", "c_ctx", "w_mod", "b_mod", "g_mix", "g_ffn", "a_w_in", "a_b_gate", "a_head_gain", "a_w_out",
        "f_w_up", "f_w_conv", "f_b_conv", "f_w_down", "g_final", "c_2", "w_ada_2", "b_ada_2", "norm_mix_2", "w_in_2",
        "b_forget_2", "w_up_a_2", "w_up_b_2", "w_out_2", "norm_ffn_2", "w_ffn_in_2", "w_ffn_out_2", "norm_final_2"]
_OUTS = [((1, T, D), "float32")]


def kernel(**inputs):
    import numpy as _np
    import concourse.bacc as _bacc
    from concourse import mybir as _mybir
    from concourse.bass_utils import run_bass_kernel_spmd as _run

    nc = _bacc.Bacc("TRN2", target_bir_lowering=False, num_devices=1)
    i = _np.arange(P)
    t = (i[:, None] // CB * CL + i[:, None] % CB * (CL * CA) + _np.arange(CL)[None, :])
    gap = t[:, :, None] - t.T.reshape(1, 1, T)
    same = gap[:, 0, 0:P]
    near = lambda ok, d: _np.where(ok, d, FAR).astype(_np.float32)
    consts = {
        "k_dist0": near((gap >= 0) & (gap <= WINDOW0), gap),
        "k_dist12": _np.stack([near(same >= 0, same), near((same >= 0) & (same % 16 == 0), same)], 1),
        "k_causal": _np.where(gap >= 0, 0, -FAR).astype(_np.float32),
        "k_ident": _np.eye(P, dtype=_np.float32),
        "k_masks": _np.stack([i[:, None] <= i[None, :], i[:, None] >= i[None, :]], 1).astype(_np.float32),
    }
    arrays, args = {}, {}
    for name in _INS + list(consts):
        a = consts[name] if name in consts else _np.ascontiguousarray(inputs[name])
        arrays[f"in_{name}_dram"] = a
        args[name] = nc.dram_tensor(f"in_{name}_dram", a.shape, _mybir.dt.from_np(a.dtype), kind="ExternalInput").ap()
    for n, (shape, dtype) in enumerate(_OUTS):
        out = nc.dram_tensor(f"out_{n}_dram", shape, _mybir.dt.from_np(_np.dtype(dtype)), kind="ExternalOutput").ap()
    program(nc, args, out)
    r = _run(nc, [arrays], core_ids=[0])
    return r.results[0]["out_0_dram"]
```

```python
from contextlib import ExitStack

import numpy as np
import concourse.bass as bass
from concourse import mybir

F32 = mybir.dt.float32
F32R = mybir.dt.float32r
ALU = mybir.AluOpType
ACT = mybir.ActivationFunctionType
AX_X = mybir.AxisListType.X

P = 128
D = 1024
KT = D // P
T = 512
TT = T // P
TC = 256
CTT = TC // P
GRID_W = 64
NH, DK, DV = 4, 128, 256
VE = DV + 2
FF = 2816
FT = FF // P
FH = FT // 2
EPS = 1e-6
UC = 256
BWD = 32
GR = BWD + NH
NG = 2 * BWD + GR

U_Q, U_K, U_V, U_O, U_OUT = 0, 2, 4, 8, 12
U_UP = 16
U_DOWN = U_UP + FT
U_QKV2 = U_DOWN + 2 * KT
U_GZ = U_QKV2 + 12
U_OUT2 = U_GZ + KT
U_IN2 = U_OUT2 + 4
U_DOWN2 = U_IN2 + FT
U_END = U_DOWN2 + 2 * KT

CL, CA, CB = 4, 4, 32
HD = 64
GH, GROUPS = 4, 3
NHA, NHB = GH * GROUPS, 4
WA, WB = NHA * HD, NHB * HD
WINDOW0 = 128
QK_SCALE = HD ** -0.5
SLOPES = [2.0 ** (-8.0 * (h + 1) / NHA) for h in range(NHA)]
KEYS_A = T + 2 * P
ROUNDS_A = GH * CL
ROUNDS = ROUNDS_A + NHB * CL
FAR = 1e30
NF = 68

V_C, V_CC, V_C2, V_GMIX, V_GFFN, V_GAIN, V_NMIX, V_NFFN, V_GFIN, V_NFIN, V_BMOD = (
    0, 8, 16, 24, 32, 40, 48, 56, 64, 72, 80)
V_BADA, V_FB, V_CONV = 128, 176, 198
NV = V_CONV + 3 * FT


class Steps:

    def __init__(self, eng, sem):
        self.eng, self.sem, self.n, self.reg, self.at = eng, sem, 0, 0, 0

    def done(self, ins):
        ins.then_inc(self.sem, 1)
        self.n += 1
        return ins

    def wait(self, back=0):
        self.eng.wait_ge(self.sem, self.n - back + self.reg)

    def enter(self, i, per):
        self.at, self.reg = self.n, i * per

    def leave(self, iters, per):
        assert self.n - self.at == per, (self.n - self.at, per)
        self.n, self.reg = self.at + per * iters, 0


def program(nc, a, out):
    with ExitStack() as ctx:
        arena = nc.sbuf_base + 31 & ~31
        size = (nc.sbuf_usable_end - arena) & ~31
        slab = ctx.enter_context(nc.sbuf_tensor("slab", [P, size // 4], F32))

        def at(name, shape, dt, off):
            return nc.alloc_sbuf_tensor_at(name, shape, dt, offset=arena + off)

        def sem(name):
            return ctx.enter_context(nc.semaphore(name))

        o = 0

        def take(n):
            nonlocal o
            was, o = o, o + (n + 31 & ~31)
            return was

        o_raw, o_hi, o_lo, o_rawm = take(8192), take(16384), take(16384), take(8192)
        o_x, o_h = take(16384), take(32768)
        raw = at("raw", [P, 2048], F32, o_raw)
        whi = [at(f"whi{s}", [P, 2048], F32R, o_hi + 8192 * s) for s in range(2)]
        wlo = [at(f"wlo{s}", [P, 2048], F32R, o_lo + 8192 * s) for s in range(2)]
        rawm = at("rawm", [P, 2, D], F32, o_rawm)
        xT = at("xT", [P, KT, T], F32, o_x)
        hh = at("hh", [P, KT, T], F32R, o_h)
        hl = at("hl", [P, KT, T], F32R, o_h + 16384)

        ident = at("ident", [P, P], F32, take(512))
        ones = at("ones", [P, P], F32, take(512))
        vec = at("vec", [P, NV], F32, take(4 * NV))
        sil = at("sil", [P, 24], F32, take(96))
        mods = at("mods", [P, 96], F32, take(384))
        mod1, mod2 = mods[:, 0:48], mods[:, 48:96]
        modc = at("modc", [P, 16], F32, take(64))
        small = at("small", [P, 64], F32, take(256))
        gcols = at("gcols", [P, 396], F32, take(1584))
        hd = at("hd", [P, 48], F32, take(192))
        acc = at("acc", [P, T], F32, take(2048))
        o_acc = o - 2048
        junk2 = at("junk2", [P, DV], F32, o_acc)
        scratch = take(0)
        o_T = size - 12288 - 31 & ~31
        tbuf = [at(f"tbuf{i}", [P, T], F32, o_T + 2048 * i) for i in range(6)]
        A1, AC, A2 = small[:, 0:8], small[:, 8:16], small[:, 16:24]
        ssx, rx = small[:, 24:30], small[:, 30:36]
        mean, rstd = small[:, 36:40], small[:, 40:44]
        bi, bf = small[0:GR, 44:45], small[0:GR, 45:46]
        gc, mc, ngc = small[0:GR, 46:47], small[0:GR, 47:48], small[0:GR, 48:49]

        xn = at("xn", [P, TT + CTT, D], F32, scratch)
        vrow = [at(f"vrow{i}", [P, P], F32, o_T + 2048 * i) for i in range(3)]
        wm = at("wm", [P, KT, 2048], F32, scratch + 24576)
        mrow = at("mrow", [2, 2048], F32, o_h)
        hbuf = [at(f"hbuf{i}", [P, T], F32, scratch + 24576 + 2048 * i) for i in range(4)]
        junk = at("junk", [P, D], F32, o_x + 4096)
        wgr = at("wgr", [P, KT, NG], F32, o_x)
        wgh = at("wgh", [P, KT, NG], F32R, o_T + 4096)
        wgl = at("wgl", [P, KT, NG], F32R, o_T + 4096 + 3200)
        gI = at("gI", [GR, TC + T], F32, o_x + 3584)
        gZ = at("gZ", [GR, TC + T], F32, o_x + 3584 + 3072)
        gF = at("gF", [GR, TC + T], F32, o_x + 3584 + 6144)
        gG = at("gG", [GR, T], F32, o_x + 3584 + 9216)
        gN = at("gN", [GR, T], F32, o_x)
        dmc = at("dmc", [GR, GR], F32, o_x + 2048)
        s = scratch
        qh, ql = at("qh", [P, NH, T], F32R, s), at("ql", [P, NH, T], F32R, s + 8192)
        kh, kl = at("kh", [P, NH, T], F32R, s + 16384), at("kl", [P, NH, T], F32R, s + 24576)
        s += 32768
        vh = at("vh", [P, TT, NH, VE], F32R, s)
        vl = at("vl", [P, TT, NH, VE], F32R, s + TT * NH * VE * 4)
        s += 2 * TT * NH * VE * 4
        vc = at("vc", [P, CTT, NH, VE], F32, s)
        s += CTT * NH * VE * 4
        kc = at("kc", [P, CTT, NH * DK], F32, s)
        s += CTT * NH * DK * 4
        hch, hcl = at("hch", [P, KT, TC], F32R, s), at("hcl", [P, KT, TC], F32R, s + 8192)
        Wh = [at(f"Wh{i}", [P, T], F32R, s + 2048 * i) for i in range(2)]
        Wl = [at(f"Wl{i}", [P, T], F32R, s + 4096 + 2048 * i) for i in range(2)]
        WI = at("WI", [P, T], F32, s + 8192)
        qwh, qwl = at("qwh", [P, T], F32R, s + 10240), at("qwl", [P, T], F32R, s + 12288)
        masks = at("masks", [P, 2, P], F32, s + 14336)
        ngcols = at("ngcols", [P, 36 * TT], F32, s + 15360)
        assert s + 16384 <= o_T, (s + 16384, o_T)
        Ch, Cl = at("Ch", [P, VE], F32R, o_rawm), at("Cl", [P, VE], F32R, o_rawm + 1056)
        kw = at("kw", [P, CTT, DK], F32, o_rawm + 2112)
        Gnat = at("Gnat", [GR, T], F32, o_rawm + 3168)
        qw = at("qw", [P, T], F32, o_rawm + 5216)
        dec = [at(f"dec{i}", [P, T], F32, o_raw + 2048 * i) for i in range(4)]
        hn = at("hn", [P, TT, NH * DV], F32, o_x)
        xr = at("xr", [P, TT, D], F32, scratch + 32768)
        yh, yl = at("yh", [P, KT, T], F32R, scratch), at("yl", [P, KT, T], F32R, scratch + 16384)
        fh, fl = at("fh", [P, FT, T], F32R, scratch), at("fl", [P, FT, T], F32R, scratch + FT * T * 4)
        assert scratch + FT * T * 8 <= o_T
        msum0 = at("msum0", [P, D], F32, o_T + 8192)
        msum1 = at("msum1", [P, D], F32, scratch + FT * T * 8)
        assert scratch + FT * T * 8 + 4096 <= o_T
        s = scratch
        qk = at("qk", [P, 16, T], F32, s)
        mh, ml = at("mh", [P, KT, T], F32R, s), at("ml", [P, KT, T], F32R, s + 16384)
        v2 = at("v2", [P, TT, WA + WB], F32, s + 32768)
        on = at("on", [P, CL, 512], F32, s + 49152)
        att = at("att", [P, 4, T], F32, s + 57344)
        wfr = at("wfr", [P, KT, NF], F32, s + 57344)
        wfh = at("wfh", [P, KT, NF], F32R, s + 57344 + 2176)
        wfl = at("wfl", [P, KT, NF], F32R, s + 57344 + 4352)
        FB = at("FB", [P, NHB, T], F32, s + 57344)
        dist0 = at("dist0", [P, CL, T], F32, s + 65536)
        dist12 = at("dist12", [P, 2, P], F32, s + 73728)
        causal = at("causal", [P, CL, T], F32, s + 74752)
        upA, upB = at("upA", [P, 2, D], F32, o_rawm), at("upB", [P, 2, D], F32, s + 82944)
        CF = [at(f"CF{i}", [P, T], F32, s + 91136 + 2048 * i) for i in range(2)]
        fA, fB = at("fA", [NHB, T], F32, s + 91136), at("fB", [NHB, T], F32, s + 93184)
        assert s + 95232 <= o_T
        fF = at("fF", [NHB, T], F32, o_acc)
        L = [at(f"L{i}", [P, KEYS_A], F32, o_T + 4 * KEYS_A * i if i < 2 else o_raw) for i in range(3)]
        PT = [at(f"PT{i}", [P, KEYS_A], F32, o_T + 8 * KEYS_A + 4 * KEYS_A * i) for i in range(2)]
        fin = at("fin", [P, CL, D], F32, o_h)
        z2, r12, G2 = small[:, 52:56], small[:, 56:60], AC
        A3 = small[:, 0:8]
        lsum, rsum, nmax = hd[:, 0:8], hd[:, 8:16], hd[:, 16:24]
        acc2 = at("acc2", [P, T], F32, o_T + 2048 * 4)

        bank = [ctx.enter_context(nc.psum_tensor(f"bank{i}", [P, 512], F32)) for i in range(8)]

        S = {n: sem(n) for n in (
            "mod_sum mod_rows loaded hi_ready lo_ready pe_used evacuated mod_loaded mod_used mod_evacuated "
            "vecs_in x_in c_in wm_in0 wm_in1 wm_in2 wm_in3 wm_in4 wm_in5 wm_in6 wm_in7 wg_in consts_in "
            "bias_in dve_step act_step pool_step masks_in wg_zero vec_t vec_cols silu_c pe_mod0 mod0_cols "
            "x_sq x_mean x_root x_scaled x_turned h_raw h_high h_ready wg_split gates_in g_abs g_soft g_u "
            "g_em g_nat g_turned gcols_in gb_ready gb_copied wi_ready kw_ready c_ready ch_ready cl_ready "
            "s_ready w_raw e_ready masked wh_ready w_ready w_free qw_raw qwh_ready q_ready num_ready num_free "
            "h_sq h_mean h_root hn_ready xr_in xr_turned xT_in o_sig hn_turned y_ready acc_ready stat_ready "
            "mean_ready root_ready diag_ready bc_ready t_ready out_half n_high n_ready glu_a glu_s "
            "f_ready ones_in out_done mean2_ready root2_ready tab_in wf_in bf_in up_in wf_split f_logits "
            "f_abs f_soft f_neg fb_ready fb_copied rescaled qk_ready l_free l_ready p_ready tr_ready "
            "pt_copied o_ready o_free cf_ready on_turned att_ready g_sig m_ready xg_ready fin_turned "
            "fin_copied scaled scaled_a").split()}

        block = ctx.enter_context(nc.Block())
        PERM = [(h, d) for h in range(NH) for d in range(2)]

        def row(idx):
            h, d = PERM[idx]
            return BWD * d + h

        def span(idx, j):
            s = j if idx % 2 == 0 else TT - 1 - j
            return s, (slice(s * P, T) if idx % 2 == 0 else slice(0, (s + 1) * P))

        r8 = raw[:, :].rearrange("p (t n) -> p t n", t=KT)
        r11 = raw[:, 0:FH * P].rearrange("p (t n) -> p t n", t=FH)

        @block.sync
        def _(sp):
            for i, (name, lo, n, c0) in enumerate((
                    ("c", V_C, 8, 0), ("c_ctx", V_CC, 8, 0), ("c_2", V_C2, 8, 0), ("g_mix", V_GMIX, 8, 0),
                    ("g_ffn", V_GFFN, 8, 0), ("a_head_gain", V_GAIN, 8, 0), ("norm_mix_2", V_NMIX, 8, 0),
                    ("norm_ffn_2", V_NFFN, 8, 0), ("g_final", V_GFIN, 8, 0), ("norm_final_2", V_NFIN, 8, 0),
                    ("b_mod", V_BMOD, 48, 0), ("b_ada_2", V_BADA, 48, 0), ("f_b_conv", V_FB, FT, 0))):
                src = a[name]
                src = src if len(src.shape) == 1 else src.rearrange("a n -> (a n)")
                sp.dma_start(vrow[lo // P][lo % P:lo % P + n, :],
                             src.rearrange("(t p) -> t p", p=P)).then_inc(S["vecs_in"], 16)
            sp.dma_start(vrow[2][0:3 * FT, :],
                         a["f_w_conv"].rearrange("a c (t p) -> (a c t) p", p=P)).then_inc(S["vecs_in"], 16)
            sp.dma_start(ident[:], a["k_ident"]).then_inc(S["consts_in"], 16)
            wmod = a["w_mod"].rearrange("a (t p) n -> p (a t) n", p=P)
            for k in range(KT):
                sp.dma_start(wm[:, k, :], wmod[:, k, 0:2 * D]).then_inc(S[f"wm_in{k}"], 16)
                if k == 4:
                    sp.dma_start(xn[:, 0:TT, :], a["x"].rearrange("a (t p) n -> p (a t) n", p=P)).then_inc(S["x_in"], 16)
                if k == 5:
                    sp.dma_start(xn[:, TT:TT + CTT, :],
                                 a["ctx"].rearrange("a (t p) n -> p (a t) n", p=P)).then_inc(S["c_in"], 16)
            sp.wait_ge(S["wg_zero"], 3)
            win = a["a_w_in"].rearrange("a (t p) n -> p (a t) n", p=P)
            g0 = 2 * NH * DK + NH * DV + D
            for q in range(4):
                sp.dma_start(wgr[:, :, BWD * q:BWD * q + NH], win[:, :, g0 + NH * q:g0 + NH * q + NH]).then_inc(S["wg_in"], 16)
                sp.dma_start((bi, bf)[q // 2][BWD * (q % 2):BWD * (q % 2) + NH, :],
                             a["a_b_gate"][0, NH * q:NH * q + NH].rearrange("(n o) -> n o", o=1)).then_inc(S["bias_in"], 16)

            def load(u, dst, src):
                if not isinstance(u, int) or u >= 1:
                    sp.wait_ge(S["lo_ready"], u)
                sp.dma_start(dst, src).then_inc(S["loaded"], 16)

            wout = a["a_w_out"].rearrange("a (t p) n -> p (a t) n", p=P)
            for u in range(U_UP):
                if u == U_O + 1:
                    sp.wait_ge(S["num_free"], 2 * NH * TT)
                if u < U_OUT:
                    load(u, r8, win[:, :, u * UC:(u + 1) * UC])
                else:
                    load(u, r8, wout[:, :, (u - U_OUT) * UC:(u - U_OUT + 1) * UC])
                if u == U_O:
                    sp.wait_ge(S["pe_used"], U_O)
                    sp.dma_start(masks[:], a["k_masks"]).then_inc(S["masks_in"], 16)
                if u == U_O + 1:
                    sp.dma_start(xr[:], a["x"].rearrange("a (t p) n -> p (a t) n", p=P)).then_inc(S["xr_in"], 16)
            wup = a["f_w_up"].rearrange("a (t p) (g n) -> p (a t) g n", p=P, g=2)
            r8g = raw[:, :].rearrange("p (t g n) -> p t g n", t=KT, g=2)
            def load_up(u, i, w):
                for g in range(2):
                    if g == 0:
                        sp.wait_ge(S["lo_ready"], u)
                    sp.dma_start(r8g[:, :, g, :], w[:, :, g, bass.ds(i * P, P)]).then_inc(S["loaded"], 8 * 2)
            with sp.Fori(0, FT) as i:
                load_up(U_UP + i, i, wup)
            wdn = a["f_w_down"].rearrange("a (t p) n -> p (a t) n", p=P)
            load(U_DOWN, r11, wdn[:, 0:FH, 0:P])
            load(U_DOWN + 1, r11, wdn[:, FH:FT, 0:P])
            with sp.Fori(1, KT) as m:
                for s in range(2):
                    load(U_DOWN + 2 * m + s, r11, wdn[:, s * FH:(s + 1) * FH, bass.ds(m * P, P)])
            win2 = a["w_in_2"].rearrange("a (t p) n -> p (a t) n", p=P)
            wz = a["w_in_2"][:, :, 3 * (WA + WB) + NHB:].rearrange("a (t p) (g n) -> p (a t) g n", p=P, g=2)
            for u in range(U_QKV2, U_GZ):
                load(u, r8, win2[:, :, (u - U_QKV2) * UC:(u - U_QKV2 + 1) * UC])
                if u == U_QKV2:
                    sp.wait_ge(S["pe_used"], U_QKV2)
                    sp.wait_ge(S["wg_zero"], 4)
                    sp.dma_start(wfr[:, :, 0:NHB], win2[:, :, 3 * (WA + WB):3 * (WA + WB) + NHB]).then_inc(S["wf_in"], 16)
                    sp.dma_start(small[0:NHB, 44:45], a["b_forget_2"].rearrange("o n -> n o")).then_inc(S["bf_in"], 16)
                    sp.dma_start(dist0[:], a["k_dist0"]).then_inc(S["tab_in"], 16)
                    sp.dma_start(dist12[:], a["k_dist12"]).then_inc(S["tab_in"], 16)
                    sp.dma_start(causal[:], a["k_causal"]).then_inc(S["tab_in"], 16)
                    sp.wait_ge(S["mod_evacuated"], 10)
                    sp.dma_start(upA[:], a["w_up_a_2"].rearrange("a (t p) n -> p (a t) n", p=P)).then_inc(S["up_in"], 16)
                    sp.dma_start(upB[:], a["w_up_b_2"].rearrange("a (t p) n -> p (a t) n", p=P)).then_inc(S["up_in"], 16)
            for m in range(KT):
                if m == 1:
                    sp.wait_ge(S["tr_ready"], ROUNDS)
                load_up(U_GZ + m, m, wz)
            wout2 = a["w_out_2"].rearrange("a (t p) n -> p (a t) n", p=P)
            for u in range(U_OUT2, U_IN2):
                load(u, r8, wout2[:, :, (u - U_OUT2) * UC:(u - U_OUT2 + 1) * UC])
            win3 = a["w_ffn_in_2"].rearrange("a (t p) (g n) -> p (a t) g n", p=P, g=2)
            with sp.Fori(0, FT) as i:
                load_up(U_IN2 + i, i, win3)
            wdn2 = a["w_ffn_out_2"].rearrange("a (t p) n -> p (a t) n", p=P)
            with sp.Fori(0, KT) as m:
                for s in range(2):
                    load(U_DOWN2 + 2 * m + s, r11, wdn2[:, s * FH:(s + 1) * FH, bass.ds(m * P, P)])
            dst = out.rearrange("o (b a c) n -> c a (o b) n", a=CA, c=CL)
            for c in range(CL):
                if c % 2 == 0:
                    sp.wait_ge(S["scaled"], c // 2 + 1)
                else:
                    sp.wait_ge(S["scaled_a"], c // 2 + 1)
                for q in range(CA):
                    sp.dma_start(dst[c, q], fin[q * CB:(q + 1) * CB, c, :]).then_inc(S["out_done"], 16)
            sp.wait_ge(S["out_done"], 16 * CL * CA)

        LOADS, n = {}, 0
        for u0, u1, per in ((0, U_UP, 16), (U_UP, U_DOWN, 32), (U_DOWN, U_GZ, 16), (U_GZ, U_OUT2, 32),
                            (U_OUT2, U_IN2, 16), (U_IN2, U_DOWN2, 32), (U_DOWN2, U_END, 16)):
            LOADS[u0] = (n, per)
            n += (u1 - u0) * per

        def loaded_count(u, u0):
            n, per = LOADS[u0]
            return n + (u - u0 + 1) * per

        @block.gpsimd
        def _(pool):
            pool.memset(ones[:], 1.0).then_inc(S["ones_in"], 1)
            pool.memset(wgr[:], 0.0).then_inc(S["wg_zero"], 1)
            pool.memset(small[:, 44:45], 0.0).then_inc(S["wg_zero"], 1)
            pool.memset(small[:, 45:46], 0.0).then_inc(S["wg_zero"], 1)

            def load_mod(j, w, q, c0):
                src = w[:, 2 * q:2 * q + 2, c0 if isinstance(c0, slice) else bass.ds(c0, D)]
                if not isinstance(j, int) or j >= 1:
                    pool.wait_ge(S["mod_used"], j)
                pool.dma_start(rawm[:], src).then_inc(S["mod_loaded"], 16)

            def mask(n):
                i, (s_, _) = n // TT, span(n // TT, n % TT)
                dg = slice(s_ * P, (s_ + 1) * P)
                pool.wait_ge(S["e_ready"], n + 1)
                pool.tensor_tensor(dec[n % 4][:, dg], dec[n % 4][:, dg], masks[:, i % 2, :], ALU.mult).then_inc(S["masked"], 1)

            def weigh_queries(i):
                h = PERM[i][0]
                if i >= 1:
                    pool.wait_ge(S["q_ready"], i)
                pool.tensor_tensor(qw[:], qh[:, h, :].bitcast(F32), ql[:, h, :].bitcast(F32), ALU.add).then_inc(S["pool_step"], 1)
                pool.wait_ge(S["pool_step"], i + 1)
                pool.wait_ge(S["wi_ready"], i + 1)
                pool.tensor_tensor(qw[:], qw[:], WI[:], ALU.mult).then_inc(S["qw_raw"], 1)

            def attention_pool():
                pool.wait_ge(S["masks_in"], 16)
                pool.wait_ge(S["mod_used"], U_O)
                weigh_queries(0)
                for n in range(2 * NH * TT):
                    mask(n)
                    if n % TT == 1 and n > TT:
                        weigh_queries(n // TT)

            wmod = a["w_mod"].rearrange("a (t p) n -> p (a t) n", p=P)
            wada = a["w_ada_2"].rearrange("a (t p) n -> p (a t) n", p=P)
            pool.wait_ge(S["c_in"], 16)
            for j in range(U_UP):
                if j == U_O:
                    attention_pool()
                    pool.wait_ge(S["num_free"], 2 * NH * TT)
                load_mod(j, wmod, j % 4, 2 * D + j // 4 * D)
            with pool.Fori(0, (FT + 2) // 4) as i:
                for q in range(4):
                    load_mod(U_UP + 4 * i + q, wada, q, i * D)
            pool.wait_ge(S["pe_used"], U_QKV2)
            pool.memset(wfr[:], 0.0).then_inc(S["wg_zero"], 1)
            pool.wait_ge(S["tab_in"], 48)
            for q in range(NHB * CL):
                h, c = q // CL, q % CL
                if c == 0:
                    pool.wait_ge(S["fb_copied"], h + 1)
                if q < 2:
                    pool.wait_ge(S["fb_copied"], NHB)
                else:
                    pool.wait_ge(S["l_free"], ROUNDS_A + q - 1)
                pool.tensor_tensor(CF[q % 2][:], causal[:, c, :], FB[:, h, :], ALU.add).then_inc(S["cf_ready"], 1)

        @block.scalar
        def _(act):
            st = Steps(act, S["act_step"])

            def high(u, s, n, phase=0, first=False):
                act.wait_ge(S["loaded"], loaded_count(u, phase))
                if not first:
                    act.wait_ge(S["pe_used"], u - 1)
                act.copy(whi[s][:, 0:n], raw[:, 0:n]).then_inc(S["hi_ready"], 1)

            act.wait_ge(S["vec_cols"], 3)
            act.activation(sil[:], vec[:, 0:24], ACT.Silu).then_inc(S["silu_c"], 1)
            act.wait_ge(S["x_in"], 16)
            for t in range(TT + CTT):
                if t == TT:
                    act.wait_ge(S["c_in"], 16)
                if t:
                    st.wait()
                ins = act.activation(junk[:], xn[:, t, :], ACT.Square, accum_out=ssx[:, t:t + 1])
                if t == TT + CTT - 1:
                    ins.then_inc(S["x_sq"], 1)
                else:
                    st.done(ins)
            act.wait_ge(S["x_mean"], 1)
            act.activation(rx, ssx, ACT.Sqrt).then_inc(S["x_root"], 1)
            high(0, 0, 2048, first=True)
            act.wait_ge(S["mod0_cols"], 4)
            for n in range(2 * KT):
                k, w = n // 2, (T, TC)[n % 2]
                act.wait_ge(S["x_turned"], n + 1)
                if n >= 4:
                    act.wait_ge(S["h_ready"], n - 3)
                sc, sh = ((A1, mod1), (AC, modc))[n % 2]
                act.activation(hbuf[n % 4][:, 0:w], bank[n % 6][:, 0:w], ACT.Identity,
                               bias=sh[:, k:k + 1], scale=sc[:, k:k + 1]).then_inc(S["h_raw"], 1)
            high(1, 1, 2048, first=True)
            act.wait_ge(S["g_abs"], 1)
            st.done(act.activation(gF[:], gF[:], ACT.Exp, scale=-1.0))
            st.wait()
            act.activation(gF[:], gF[:], ACT.Ln, bias=1.0).then_inc(S["g_soft"], 1)
            high(2, 0, 2048)
            act.wait_ge(S["g_u"], 1)
            st.done(act.activation(gI[:, 0:TC], gI[:, 0:TC], ACT.Exp, bias=ngc))
            st.wait()
            act.wait_ge(S["g_u"], 2)
            act.activation(gF[:, TC:], gF[:, TC:], ACT.Exp, scale=-1.0).then_inc(S["g_em"], 1)
            for u in range(3, U_O + 1):
                high(u, u % 2, 2048)
            def gates_out(i):
                if i == 0:
                    act.wait_ge(S["mod_sum"], 2)
                act.wait_ge(S["gb_ready"], i + 1)
                act.copy(tbuf[4 + i % 2][:], bank[6][:]).then_inc(S["gb_copied"], 1)
                act.wait_ge(S["gb_copied"], i + 1)

            def carry_decay(i):
                if i >= 1:
                    act.wait_ge(S["qw_raw"], i)
                act.activation(WI[:], tbuf[4 + i % 2][:], ACT.Exp, scale=-1.0,
                               bias=gcols[:, 360 + row(i):361 + row(i)]).then_inc(S["wi_ready"], 1)

            def decay(n):
                i = n // TT
                s_, r = span(i, n % TT)
                if n >= 4:
                    act.wait_ge(S["w_raw"], n - 3)
                c = 36 * s_ + row(i)
                st.done(act.activation(dec[n % 4][:, r], tbuf[4 + i % 2][:, r], ACT.Relu, bias=ngcols[:, c:c + 1], scale=1.0))
                st.wait()
                act.activation(dec[n % 4][:, r], dec[n % 4][:, r], ACT.Exp, scale=-1.0).then_inc(S["e_ready"], 1)

            def weights_high(n):
                _, r = span(n // TT, n % TT)
                act.wait_ge(S["w_raw"], n + 1)
                if n >= 2:
                    act.wait_ge(S["w_free"], n - 1)
                act.copy(Wh[n % 2][:, r], tbuf[n % 4][:, r]).then_inc(S["wh_ready"], 1)

            def carry_high(i):
                act.wait_ge(S["c_ready"], i + 1)
                if i >= 1:
                    act.wait_ge(S["num_ready"], i)
                act.copy(Ch[:], bank[7][:, 0:VE]).then_inc(S["ch_ready"], 1)
                act.wait_ge(S["qw_raw"], i + 1)
                act.copy(qwh[:], qw[:]).then_inc(S["qwh_ready"], 1)

            def head_squares(h, t):
                act.wait_ge(S["num_free"], (2 * h + 1) * TT + t + 1)
                if h or t:
                    act.wait_ge(S["h_sq"], t + TT * h)
                c = t * NH + h
                act.activation(junk2[:], hn[:, t, h * DV:(h + 1) * DV], ACT.Square,
                               accum_out=hd[:, c:c + 1]).then_inc(S["h_sq"], 1)

            act.wait_ge(S["gcols_in"], 1)
            act.wait_ge(S["pe_used"], U_O)
            st.done(act.activation(ngcols[:], gcols[:, 0:36 * TT], ACT.Identity, scale=-1.0))
            st.wait()
            gates_out(0)
            carry_decay(0)
            act.wait_ge(S["lo_ready"], U_O + 1)
            for n in range(TT):
                decay(n)
            gates_out(1)
            for i in range(2 * NH):
                more = i + 1 < 2 * NH
                for j in range(TT):
                    n = i * TT + j
                    weights_high(n)
                    if n + 4 < 2 * NH * TT:
                        decay(n + 4)
                    if j == 1 and more:
                        carry_decay(i + 1)
                    if j == 3 and i + 2 < 2 * NH:
                        gates_out(i + 2)
                    if j == 0:
                        carry_high(i)
                    if i >= 2 and i % 2 == 0:
                        head_squares(i // 2 - 1, j)
            for t in range(TT):
                head_squares(NH - 1, t)
            act.wait_ge(S["h_mean"], 1)
            act.activation(hd[:, 0:16], hd[:, 0:16], ACT.Sqrt).then_inc(S["h_root"], 1)
            for u in range(U_O, U_OUT):
                high(u + 1, (u + 1) % 2, 2048)
                act.wait_ge(S["pe_used"], u + 1)
                for m in range(2):
                    n = 2 * (u - U_O) + m
                    if n >= 2:
                        act.wait_ge(S["y_ready"], n - 1)
                    act.activation(tbuf[m][:], bank[3 * (u % 2) + m][:], ACT.Sigmoid).then_inc(S["o_sig"], 1)
            for k in range(KT):
                act.wait_ge(S["xr_turned"], k + 1)
                if k == 0:
                    act.wait_ge(S["y_ready"], 2 * (U_OUT - U_O))
                act.copy(xT[:, k, :], bank[6 if k % 2 == 0 else 7][:]).then_inc(S["xT_in"], 1)
            for u in range(U_OUT, U_UP - 1):
                high(u + 1, (u + 1) % 2, 2048)

            def norm_apply(nth, A, B):
                for k in range(KT):
                    act.wait_ge(S["t_ready"], nth * KT + k + 1)
                    if k >= 2:
                        act.wait_ge(S["n_ready"], nth * KT + k - 1)
                    act.activation(tbuf[4 + k % 2][:], tbuf[2 + k % 2][:], ACT.Identity,
                                   bias=B[:, k:k + 1], scale=A[:, k:k + 1])
                    act.activation(hh[:, k, :], tbuf[2 + k % 2][:], ACT.Identity,
                                   bias=B[:, k:k + 1], scale=A[:, k:k + 1]).then_inc(S["n_high"], 1)

            high(U_UP, 0, 2048, U_UP)
            act.wait_ge(S["mean_ready"], 1)
            act.activation(mean, mean, ACT.Sqrt).then_inc(S["root_ready"], 1)
            norm_apply(0, A2, mod1[:, 24:32])

            def up_act(u, i, s, nxt=True, phase=U_UP, n=2048):
                high(u + 1, 1 - s, n, phase)
                act.wait_ge(S["glu_a"], i + 1)
                act.activation(tbuf[2 + s][:], tbuf[s][:], ACT.Silu).then_inc(S["glu_s"], 1)

            with act.Fori(0, FT // 2 - 1) as i:
                for s in range(2):
                    up_act(U_UP + 2 * i + s, 2 * i + s, s)
            up_act(U_DOWN - 2, FT - 2, 0)
            up_act(U_DOWN - 1, FT - 1, 1, phase=U_DOWN, n=FH * P)
            with act.Fori(0, KT - 1) as m:
                for s in range(2):
                    high(U_DOWN + 2 * m + s + 1, 1 - s, FH * P, U_DOWN)
            high(U_DOWN + 2 * KT - 1, 1, FH * P, U_DOWN)
            high(U_QKV2, 0, 2048, U_DOWN)
            act.wait_ge(S["mean2_ready"], 1)
            act.activation(z2, z2, ACT.Sqrt).then_inc(S["root2_ready"], 1)
            act.activation(mean, mean, ACT.Sqrt).then_inc(S["root_ready"], 1)
            norm_apply(1, A3, mod2)
            for u in range(U_QKV2, U_GZ):
                if u + 1 < U_GZ:
                    high(u + 1, (u + 1) % 2, 2048, U_DOWN)
                else:
                    high(u + 1, (u + 1) % 2, 2048, U_GZ)
                if u == U_QKV2 + 8:
                    act.wait_ge(S["f_abs"], 1)
                    st.done(act.activation(fB[:], fB[:], ACT.Exp, scale=-1.0))
                    st.wait()
                    act.activation(fB[:], fB[:], ACT.Ln, bias=1.0).then_inc(S["f_soft"], 1)
            for r in range(ROUNDS + 2):
                if r >= 2:
                    q = r - 2
                    act.wait_ge(S["tr_ready"], q + 1)
                    if q >= 2:
                        act.wait_ge(S["o_ready"], q - 1)
                    ins = act.copy(PT[q % 2][:, 0:T], bank[4][:])
                    if q < ROUNDS_A:
                        st.done(ins)
                        ins = act.copy(PT[q % 2][:, T:], bank[5][:, 0:2 * P])
                    ins.then_inc(S["pt_copied"], 1)
                if r < ROUNDS:
                    w = KEYS_A if r < ROUNDS_A else T
                    act.wait_ge(S["l_ready"], r + 1)
                    act.activation(L[r % 3][:, 0:w], L[r % 3][:, 0:w], ACT.Exp, scale=QK_SCALE, bias=nmax[:, r % 8:r % 8 + 1],
                                   accum_out=lsum[:, r % 8:r % 8 + 1]).then_inc(S["p_ready"], 1)
            for f in range(4):
                act.wait_ge(S["on_turned"], f + 1)
                if f == 0:
                    act.wait_ge(S["cf_ready"], NHB * CL)
                act.copy(att[:, f, :], bank[4 + f][:]).then_inc(S["att_ready"], 1)
            for u in range(U_GZ, U_OUT2):
                high(u + 1, (u + 1) % 2, 2048, U_GZ if u + 1 < U_OUT2 else U_OUT2)
                act.wait_ge(S["pe_used"], u + 1)
                if u > U_GZ:
                    act.wait_ge(S["m_ready"], u - U_GZ)
                for g in range(2):
                    act.activation(tbuf[g][:], bank[3 * (u % 2) + g][:], ACT.Sigmoid).then_inc(S["g_sig"], 1)
            for u in range(U_OUT2, U_IN2 - 1):
                high(u + 1, (u + 1) % 2, 2048, U_OUT2)
            high(U_IN2, 0, 2048, U_IN2)
            act.wait_ge(S["mean_ready"], 2)
            act.activation(mean, mean, ACT.Sqrt).then_inc(S["root_ready"], 1)
            norm_apply(2, A2, mod2[:, 24:32])

            def in_act(u, i, s, phase=U_IN2, n=2048):
                high(u + 1, 1 - s, n, phase)
                act.wait_ge(S["pe_used"], u + 1)
                act.activation(tbuf[2 + s][:], bank[3 * s][:], ACT.Silu).then_inc(S["glu_s"], 1)

            with act.Fori(0, FT // 2 - 1) as i:
                for s in range(2):
                    in_act(U_IN2 + 2 * i + s, 2 * i + s, s)
            in_act(U_DOWN2 - 2, FT - 2, 0)
            in_act(U_DOWN2 - 1, FT - 1, 1, phase=U_DOWN2, n=FH * P)

            def turned_out(m, b):
                act.wait_ge(S["fin_turned"], m + 1)
                act.copy(fin[:, :, bass.ds(m * P, P)], bank[b][:].rearrange("p (c n) -> p c n", c=CL)).then_inc(S["fin_copied"], 1)

            for s in range(2):
                high(U_DOWN2 + s + 1, 1 - s, FH * P, U_DOWN2)
            for s in range(2):
                high(U_DOWN2 + 2 + s + 1, 1 - s, FH * P, U_DOWN2)
            turned_out(0, 6)
            with act.Fori(1, KT // 2 - 1) as i:
                for q in range(2):
                    for s in range(2):
                        high(U_DOWN2 + 4 * i + 2 * q + s + 1, 1 - s, FH * P, U_DOWN2)
                    turned_out(2 * i + q - 1, 7 - q)
            for q in range(2):
                for s in range(2):
                    if q == 0 or s == 0:
                        high(U_DOWN2 + 2 * (KT - 2) + 2 * q + s + 1, 1 - s, FH * P, U_DOWN2)
                turned_out(KT - 3 + q, 7 - q)
            turned_out(KT - 1, 7)
            act.wait_ge(S["mean_ready"], 3)
            act.activation(mean, mean, ACT.Sqrt).then_inc(S["root_ready"], 1)
            act.wait_ge(S["scaled"], 1)
            for c in (1, 3):
                act.activation(fin[:, c, :], fin[:, c, :], ACT.Copy, scale=rstd[:, c:c + 1]).then_inc(S["scaled_a"], 1)

        @block.vector
        def _(v):
            st = Steps(v, S["dve_step"])

            def low(u, s, n):
                v.wait_ge(S["hi_ready"], u + 1)
                v.tensor_tensor(wlo[s][:, 0:n], raw[:, 0:n], whi[s][:, 0:n].bitcast(F32), ALU.subtract).then_inc(S["lo_ready"], 1)

            def mod_add(j, q, acc_m, c0):
                v.wait_ge(S["mod_loaded"], (j + 1) * 16)
                for k in (2 * q, 2 * q + 1):
                    w = rawm[:, k % 2, :]
                    if k == 0:
                        ins = v.tensor_scalar(acc_m[:], w, sil[:, c0:c0 + 1], None, ALU.mult)
                    else:
                        ins = v.scalar_tensor_tensor(acc_m[:], w, sil[:, c0 + k:c0 + k + 1], acc_m[:], ALU.mult, ALU.add)
                    if k % 2 == 0:
                        st.done(ins)
                        st.wait()
                ins.then_inc(S["mod_used"], 1)
                v.wait_ge(S["mod_used"], j + 1)

            def mod_out(c):
                v.wait_ge(S["mod_sum"], c + 1)
                v.tensor_tensor(mods[:, bass.ds(16 + 8 * c, 8)], bank[7][:, 0:8], vec[:, bass.ds(V_BMOD + 16 + 8 * c, 8)],
                                ALU.add).then_inc(S["mod_evacuated"], 1)

            for i in range(3):
                c = (P, V_CONV - P, 3 * FT)[i]
                v.wait_ge(S["vec_t"], i + 1)
                lo = (0, P, V_CONV)[i]
                v.tensor_copy(vec[:, lo:lo + c], bank[i][:, 0:c]).then_inc(S["vec_cols"], 1)
            v.wait_ge(S["x_sq"], 1)
            v.tensor_scalar(ssx, ssx, 1.0 / D, EPS, ALU.mult, ALU.add).then_inc(S["x_mean"], 1)
            v.wait_ge(S["x_root"], 1)
            st.done(v.reciprocal(rx, rx))
            st.wait()
            for t in range(TT + CTT):
                v.tensor_scalar(xn[:, t, :], xn[:, t, :], rx[:, t:t + 1], None, ALU.mult).then_inc(S["x_scaled"], 1)
            for q in range(4):
                v.wait_ge(S["pe_mod0"], 1)
                v.tensor_copy(mrow[:, q * 512:(q + 1) * 512], bank[q][0:2, :]).then_inc(S["mod_rows"], 1)
            v.wait_ge(S["pe_mod0"], 2)
            v.wait_ge(S["vec_cols"], 3)
            v.wait_ge(S["consts_in"], 16)
            m0 = bank[7][:, 0:32].rearrange("p (m v) -> p v m", v=2)
            v.tensor_tensor(mod1[:, 0:16], m0[:, 0, :], vec[:, V_BMOD:V_BMOD + 16], ALU.add).then_inc(S["mod0_cols"], 1)
            v.tensor_tensor(modc[:], m0[:, 1, :], vec[:, V_BMOD:V_BMOD + 16], ALU.add).then_inc(S["mod0_cols"], 1)
            v.wait_ge(S["mod0_cols"], 2)
            v.scalar_tensor_tensor(A1, mod1[:, 8:16], 1.0, vec[:, V_GMIX:V_GMIX + 8], ALU.add, ALU.mult).then_inc(S["mod0_cols"], 1)
            v.scalar_tensor_tensor(AC, modc[:, 8:16], 1.0, vec[:, V_GMIX:V_GMIX + 8], ALU.add, ALU.mult).then_inc(S["mod0_cols"], 1)
            v.wait_ge(S["wg_in"], 64)
            st.done(v.tensor_copy(wgh[:], wgr[:]))
            st.wait()
            v.tensor_tensor(wgl[:], wgr[:], wgh[:].bitcast(F32), ALU.subtract).then_inc(S["wg_split"], 1)
            for n in range(2 * KT + 1):
                if n < 2 * KT:
                    k, w = n // 2, (T, TC)[n % 2]
                    v.wait_ge(S["h_raw"], n + 1)
                    v.tensor_copy((hh, hch)[n % 2][:, k, :], hbuf[n % 4][:, 0:w]).then_inc(S["h_high"], 1)
                if n >= 1:
                    q = n - 1
                    k, w = q // 2, (T, TC)[q % 2]
                    v.wait_ge(S["h_high"], q + 1)
                    v.tensor_tensor((hl, hcl)[q % 2][:, k, :], hbuf[q % 4][:, 0:w],
                                    (hh, hch)[q % 2][:, k, :].bitcast(F32), ALU.subtract).then_inc(S["h_ready"], 1)
            low(0, 0, 2048)
            def split(dh, dl, ps, sc=None):
                if sc is None:
                    st.done(v.tensor_copy(dh, ps))
                    st.wait()
                    return v.tensor_tensor(dl, ps, dh.bitcast(F32), ALU.subtract)
                st.done(v.tensor_scalar(dh, ps, sc, None, ALU.mult))
                st.wait()
                return v.scalar_tensor_tensor(dl, ps, sc, dh.bitcast(F32), ALU.mult, ALU.subtract)

            def keys_out(u):
                v.wait_ge(S["pe_used"], u + 1)
                b = 3 * (u % 2)
                for m in range(2):
                    f = 2 * (u % 2) + m
                    dh, dl, sc = (qh, ql, float(DK) ** -0.5) if u < U_K else (kh, kl, None)
                    ins = split(dh[:, f, :], dl[:, f, :], bank[b + m][:], sc)
                    if m == 0 or u >= U_K:
                        st.done(ins)
                if u >= U_K:
                    ins = v.tensor_copy(kc[:, :, (u - U_K) * UC:(u - U_K + 1) * UC],
                                        bank[b + 2][:].rearrange("p (t n) -> p t n", t=CTT))
                ins.then_inc(S["evacuated"], 1)
                low(u + 2, u % 2, 2048)
            v.memset(vh[:, :, :, DV:DV + 1].bitcast(F32), 1.0)
            v.memset(vh[:, :, :, DV + 1:VE].bitcast(F32), 0.0)
            v.memset(vl[:, :, :, DV:VE].bitcast(F32), 0.0)
            v.memset(vc[:, :, :, DV:DV + 1], 1.0)
            st.done(v.memset(vc[:, :, :, DV + 1:VE], 0.0))
            v.wait_ge(S["gates_in"], 1)
            v.wait_ge(S["bias_in"], 64)
            for dst, p0 in ((gI, 0), (gZ, 2 * BWD)):
                for ps, c0, w in ((bank[7], 0, TC), (bank[6], TC, T)):
                    v.tensor_copy(dst[0:BWD, c0:c0 + w], ps[p0:p0 + BWD, 0:w])
                    st.done(v.tensor_copy(dst[BWD:GR, c0:c0 + w], ps[p0 + BWD:p0 + GR, 0:w][:, ::-1]))
            st.wait()
            st.done(v.tensor_scalar(gI[:], gI[:], bi, None, ALU.add))
            st.done(v.tensor_scalar(gZ[:], gZ[:], bf, None, ALU.add))
            st.wait()
            v.scalar_tensor_tensor(gF[:], gZ[:], -1.0, gZ[:], ALU.mult, ALU.max).then_inc(S["g_abs"], 1)
            st.done(v.tensor_scalar(gZ[:], gZ[:], 0.0, None, ALU.min))
            low(1, 1, 2048)
            v.wait_ge(S["g_soft"], 1)
            st.wait()
            st.done(v.tensor_tensor(gZ[:], gZ[:], gF[:], ALU.subtract))
            st.wait()
            v.wait_ge(S["ones_in"], 1)
            one = ones[0:GR, 0:1]
            for c0, w in ((0, TC), (TC, T)):
                st.done(v.tensor_tensor_scan(gF[:, c0:c0 + w], one.broadcast_to([GR, w]), gZ[:, c0:c0 + w], 0.0, ALU.mult, ALU.add))
            st.wait()
            st.done(v.tensor_tensor(gI[:], gI[:], gF[:], ALU.subtract))
            st.wait()
            st.done(v.reduce_max(gc, gI[:, 0:TC], AX_X))
            st.wait()
            st.done(v.tensor_scalar(gc, gc, 0.0, None, ALU.max))
            st.wait()
            st.done(v.tensor_tensor(mc, gF[:, TC - 1:TC], gc, ALU.add))
            v.tensor_scalar(ngc, gc, -1.0, None, ALU.mult).then_inc(S["g_u"], 1)
            st.wait()
            st.done(v.tensor_tensor_scan(gG[:], gI[:, TC:], gI[:, TC:], mc, ALU.max, ALU.max))
            st.wait()
            v.tensor_tensor(gF[:, TC:], gF[:, TC:], gG[:], ALU.add).then_inc(S["g_u"], 1)
            v.tensor_scalar(dmc[:], ident[0:GR, 0:GR], mc, None, ALU.mult).then_inc(S["g_nat"], 1)
            keys_out(0)
            v.wait_ge(S["g_em"], 1)
            v.wait_ge(S["g_u"], 2)
            for dst, src in ((gZ[:, 0:TC], gI[:, 0:TC]), (gZ[:, TC:], gI[:, TC:]), (gN[:], gF[:, TC:])):
                v.tensor_copy(dst[0:BWD], src[0:BWD]).then_inc(S["g_nat"], 1)
                v.tensor_copy(dst[BWD:GR], src[BWD:GR][:, ::-1]).then_inc(S["g_nat"], 1)

            for u in range(U_Q, U_V):
                if u > U_Q:
                    keys_out(u)
                mod_add(u, u % 4, msum0, V_C)
            v.wait_ge(S["g_turned"], 1)
            v.tensor_copy(gcols[:], bank[6][:, 0:396]).then_inc(S["gcols_in"], 1)
            for u in range(U_V, U_O):
                v.wait_ge(S["pe_used"], u + 1)
                b, h = 3 * (u % 2), u - U_V
                for q in range(2):
                    st.done(split(vh[:, 2 * q:2 * q + 2, h, 0:DV], vl[:, 2 * q:2 * q + 2, h, 0:DV],
                                  bank[b + q][:].rearrange("p (t n) -> p t n", t=2)))
                v.tensor_copy(vc[:, :, h, 0:DV], bank[b + 2][:].rearrange("p (t n) -> p t n", t=CTT)).then_inc(S["evacuated"], 1)
                if u == U_V:
                    mod_out(0)
                if u < U_O - 1:
                    low(u + 2, u % 2, 2048)
                    mod_add(u, u % 4, msum0, V_C)
                if u == U_O - 2:
                    mod_add(u + 1, (u + 1) % 4, msum0, V_C)
                    v.tensor_copy(Gnat[0:BWD], gG[0:BWD, :]).then_inc(S["g_nat"], 1)
                    v.tensor_copy(Gnat[BWD:GR], gG[BWD:GR, ::-1]).then_inc(S["g_nat"], 1)
                if u == U_O - 1:
                    mod_out(1)

            def weigh_keys(i):
                h, r = PERM[i][0], row(i)
                if i >= 1:
                    v.wait_ge(S["c_ready"], i)
                for t in range(CTT):
                    ins = v.tensor_scalar(kw[:, t, :], kc[:, t, h * DK:(h + 1) * DK],
                                          gcols[:, 288 + 36 * t + r:289 + 36 * t + r], None, ALU.mult)
                    if t == CTT - 1:
                        ins.then_inc(S["kw_ready"], 1)
                    else:
                        st.done(ins)

            def carry_low(i):
                v.wait_ge(S["ch_ready"], i + 1)
                v.tensor_tensor(Cl[:], bank[7][:, 0:VE], Ch[:].bitcast(F32), ALU.subtract).then_inc(S["cl_ready"], 1)
                v.wait_ge(S["qwh_ready"], i + 1)
                v.tensor_tensor(qwl[:], qw[:], qwh[:].bitcast(F32), ALU.subtract).then_inc(S["q_ready"], 1)

            def weights(n):
                _, r = span(n // TT, n % TT)
                if n >= 4:
                    v.wait_ge(S["w_ready"], n - 3)
                v.wait_ge(S["masked"], n + 1)
                v.wait_ge(S["s_ready"], n + 1)
                v.tensor_tensor(tbuf[n % 4][:, r], dec[n % 4][:, r], bank[4 + n % 2][:, r], ALU.mult).then_inc(S["w_raw"], 1)

            def weights_low(n):
                _, r = span(n // TT, n % TT)
                v.wait_ge(S["wh_ready"], n + 1)
                v.tensor_tensor(Wl[n % 2][:, r], tbuf[n % 4][:, r], Wh[n % 2][:, r].bitcast(F32), ALU.subtract).then_inc(S["w_ready"], 1)

            def heads_out(i):
                h, d = PERM[i]
                v.wait_ge(S["num_ready"], i + 1)
                for t in range(TT):
                    st.done(v.tensor_copy(hd[:, 16 + t:17 + t], bank[t][:, DV:DV + 1]))
                st.wait()
                em = gcols[:, 144 + row(i):288:36]
                st.done(v.scalar_tensor_tensor(hd[:, 24:28], hd[:, 16:20], -1.0, em, ALU.mult, ALU.max))
                st.wait()
                st.done(v.tensor_tensor(hd[:, 16:20], hd[:, 16:20], hd[:, 24:28], ALU.max))
                st.wait()
                st.done(v.reciprocal(hd[:, 20:24], hd[:, 16:20]))
                st.wait()
                for t in range(TT):
                    dst = hn[:, t, h * DV:(h + 1) * DV]
                    if d == 0:
                        ins = v.tensor_scalar(dst, bank[t][:, 0:DV], hd[:, 20 + t:21 + t], None, ALU.mult)
                    else:
                        ins = v.scalar_tensor_tensor(dst, bank[t][:, 0:DV], hd[:, 20 + t:21 + t], dst, ALU.mult, ALU.add)
                    ins.then_inc(S["num_free"], 1)
                v.wait_ge(S["num_free"], (i + 1) * TT)

            v.wait_ge(S["pe_used"], U_O)
            weigh_keys(0)
            weights(0)
            for i in range(2 * NH):
                for j in range(TT):
                    n = i * TT + j
                    if n + 1 < 2 * NH * TT and (j or not i):
                        weights(n + 1)
                    if j or not i:
                        weights_low(n)
                    if j == 1:
                        carry_low(i)
                    if j == 2 and i + 1 < 2 * NH:
                        weigh_keys(i + 1)
                if i + 1 < 2 * NH:
                    weights(n + 2)
                    weights_low(n + 1)
                heads_out(i)
            v.wait_ge(S["h_sq"], TT * NH)
            v.tensor_scalar(hd[:, 0:16], hd[:, 0:16], 1.0 / DV, EPS, ALU.mult, ALU.add).then_inc(S["h_mean"], 1)
            v.wait_ge(S["h_root"], 1)
            st.done(v.reciprocal(hd[:, 0:16], hd[:, 0:16]))
            st.wait()
            for t in range(TT):
                for h in range(NH):
                    z = hn[:, t, h * DV:(h + 1) * DV]
                    v.tensor_scalar(z, z, hd[:, t * NH + h:t * NH + h + 1], None, ALU.mult).then_inc(S["hn_ready"], 1)
            for u in range(U_O, U_OUT):
                low(u + 1, (u + 1) % 2, 2048)
                for m in range(2):
                    n = 2 * (u - U_O) + m
                    v.wait_ge(S["hn_turned"], n + 1)
                    v.wait_ge(S["o_sig"], n + 1)
                    ins = v.scalar_tensor_tensor(tbuf[2 + m][:], bank[6 if m == 0 else 3 * (u % 2) + 2][:],
                                                 vec[:, V_GAIN + n:V_GAIN + n + 1], tbuf[m][:], ALU.mult, ALU.mult)
                    if m == 0:
                        st.done(ins)
                        st.wait()
                    else:
                        ins.then_inc(S["evacuated"], 1)
                        v.wait_ge(S["evacuated"], u + 1)
                    st.done(v.tensor_copy(yh[:, n, :], tbuf[2 + m][:]))
                    st.wait()
                    v.tensor_tensor(yl[:, n, :], tbuf[2 + m][:], yh[:, n, :].bitcast(F32), ALU.subtract).then_inc(S["y_ready"], 1)
                mod_add(u, u % 4, msum0, V_C)

            v.wait_ge(S["mod_evacuated"], 1)
            def out_phase(u0, u1, mod, first_block):
                for u in range(u0, u1):
                    low(u + 1, (u + 1) % 2, 2048)
                    for m in range(2):
                        if m == 0:
                            v.wait_ge(S["out_half"], u - u0 + (1 if first_block else 5))
                        else:
                            v.wait_ge(S["pe_used"], u + 1)
                        n = 2 * (u - u0) + m
                        ins = v.scalar_tensor_tensor(xT[:, n, :], bank[3 * (u % 2) + m][:], mod[:, 16 + n:17 + n],
                                                     xT[:, n, :], ALU.mult, ALU.add)
                        if m == 1:
                            ins.then_inc(S["evacuated"], 1)
                            v.wait_ge(S["evacuated"], u + 1)
                        else:
                            st.done(ins)
                            st.wait()
                        if n == 0:
                            st.done(v.tensor_tensor(acc[:], xT[:, n, :], xT[:, n, :], ALU.mult))
                        else:
                            st.done(v.tensor_tensor(tbuf[3][:], xT[:, n, :], xT[:, n, :], ALU.mult))
                            st.wait()
                            ins = v.tensor_tensor(acc[:], acc[:], tbuf[3][:], ALU.add)
                            if n < KT - 1:
                                st.done(ins)
                            else:
                                ins.then_inc(S["acc_ready"], 1)
                    if first_block:
                        if u == u0:
                            mod_out(2)
                        if u + 1 < u1:
                            mod_add(u, u % 4, msum1, V_C)

            v.wait_ge(S["xT_in"], KT)
            out_phase(U_OUT, U_UP, mod1, True)

            def norm_stats(nth):
                v.wait_ge(S["stat_ready"], nth + 1)
                v.tensor_scalar(mean, bank[6][:, 0:TT], 1.0 / D, EPS, ALU.mult, ALU.add).then_inc(S["mean_ready"], 1)
                v.wait_ge(S["root_ready"], nth + 1)
                st.done(v.reciprocal(rstd, mean))
                st.wait()
                for t in range(TT):
                    v.tensor_scalar(tbuf[1][:, t * P:(t + 1) * P], ident[:], rstd[:, t:t + 1], None, ALU.mult).then_inc(S["diag_ready"], 1)
                v.wait_ge(S["bc_ready"], nth + 1 if nth < 2 else nth + 2)

            def reordered(ap, here):
                return ap.rearrange("p (b a c) -> p b a c" if here else "p (c a b) -> p b a c", a=CA, c=CL)

            def norm_dve(nth, dl, move=False):
                for k in range(KT + 1):
                    if k < KT:
                        if k >= 2:
                            v.wait_ge(S["n_high"], nth * KT + k - 1)
                        if move:
                            v.tensor_tensor(reordered(tbuf[2 + k % 2][:], False), reordered(xT[:, k, :], True),
                                            reordered(bank[6][:], True), ALU.mult).then_inc(S["t_ready"], 1)
                        else:
                            v.tensor_tensor(tbuf[2 + k % 2][:], xT[:, k, :], bank[6][:], ALU.mult).then_inc(S["t_ready"], 1)
                    if k >= 1:
                        q = k - 1
                        v.wait_ge(S["n_high"], nth * KT + q + 1)
                        v.tensor_tensor(dl[:, q, :], tbuf[4 + q % 2][:], hh[:, q, :].bitcast(F32), ALU.subtract).then_inc(S["n_ready"], 1)

            st.wait()
            v.wait_ge(S["mod_evacuated"], 3)
            st.done(v.scalar_tensor_tensor(A2, mod1[:, 32:40], 1.0, vec[:, V_GFFN:V_GFFN + 8], ALU.add, ALU.mult))
            st.wait()
            norm_stats(0)
            norm_dve(0, hl)
            mod_add(U_UP - 1, (U_UP - 1) % 4, msum1, V_C)

            def up_out(u, i, s, n_next, q, c):
                low(u + 1, 1 - s, n_next)
                v.wait_ge(S["pe_used"], u + 1)
                g, val = bank[3 * s], bank[3 * s + 1]
                am = tbuf[s]

                def tap(j):
                    return vec[:, bass.ds(V_CONV + FT * j + i, 1)]
                W = GRID_W
                st.done(v.tensor_scalar(am[:], g[:], tap(1), vec[:, bass.ds(V_FB + i, 1)], ALU.mult, ALU.add))
                st.wait()
                st.done(v.scalar_tensor_tensor(am[:, W:], g[:, 0:T - W], tap(0), am[:, W:], ALU.mult, ALU.add))
                st.wait()
                v.scalar_tensor_tensor(am[:, 0:T - W], g[:, W:], tap(2), am[:, 0:T - W], ALU.mult, ALU.add).then_inc(S["glu_a"], 1)
                v.wait_ge(S["glu_s"], i + 1)
                v.tensor_tensor(tbuf[4 + s][:], tbuf[2 + s][:], val[:], ALU.mult).then_inc(S["evacuated"], 1)
                v.wait_ge(S["evacuated"], u + 1)
                f3 = tbuf[4 + s][:].rearrange("p (a n) -> p a n", a=1)
                st.done(v.tensor_copy(fh[:, bass.ds(i, 1), :], f3))
                st.wait()
                v.tensor_tensor(fl[:, bass.ds(i, 1), :], f3, fh[:, bass.ds(i, 1), :].bitcast(F32), ALU.subtract).then_inc(S["f_ready"], 1)
                if q == 0:
                    mod_out(c)
                mod_add(u, q, msum1, V_C2)

            PER = 4 * 4
            with v.Fori(0, FT // 4) as i:
                st.enter(i, PER)
                for q in range(4):
                    up_out(U_UP + 4 * i + q, 4 * i + q, q % 2, 2048, q, 3 + i)
            st.leave(FT // 4, PER)
            up_out(U_DOWN - 2, FT - 2, 0, 2048, 0, 3 + FT // 4)
            up_out(U_DOWN - 1, FT - 1, 1, FH * P, 1, 3 + FT // 4)

            def down_out(m, b, gate0, first, last, n_next=2048):
                u = m * 2 + U_DOWN
                low(u + 1, 1, FH * P)
                if first:
                    mod_add(U_DOWN, 2, msum1, V_C2)
                low(u + 2, 0, n_next if last else FH * P)
                v.wait_ge(S["pe_used"], u + 2)
                xm = xT[:, bass.ds(m, 1), :]
                v.scalar_tensor_tensor(xm, bank[b][:].rearrange("p (a n) -> p a n", a=1), mod1[:, bass.ds(gate0 + m, 1)], xm,
                                       ALU.mult, ALU.add).then_inc(S["evacuated"], 1)
                v.wait_ge(S["evacuated"], u + 1)
                sq = tbuf[5][:].rearrange("p (a n) -> p a n", a=1)
                st.done(v.tensor_tensor(sq, xm, xm, ALU.mult))
                st.wait()
                if first:
                    st.done(v.tensor_scalar(acc2[:], tbuf[5][:], G2[:, 0:1], None, ALU.mult))
                    v.tensor_copy(acc[:], tbuf[5][:]).then_inc(S["evacuated"], 1)
                else:
                    st.done(v.scalar_tensor_tensor(acc2[:], tbuf[5][:], G2[:, bass.ds(m, 1)], acc2[:], ALU.mult, ALU.add))
                    v.tensor_tensor(acc[:], acc[:], tbuf[5][:], ALU.add).then_inc(S["evacuated"], 1)
                st.wait()
                v.wait_ge(S["evacuated"], u + 2)

            st.done(v.tensor_tensor(G2, vec[:, V_GFIN:V_GFIN + 8], vec[:, V_GFIN:V_GFIN + 8], ALU.mult))
            st.wait()
            v.wait_ge(S["mod_evacuated"], 4)
            down_out(0, 0, 40, True, False)
            mod_add(U_DOWN + 1, 3, msum1, V_C2)
            down_out(1, 3, 40, False, False)
            mod_out(9)
            with v.Fori(1, KT // 2 - 1) as i:
                st.enter(i - 1, 4)
                for s in range(2):
                    down_out(2 * i + s, 3 * s, 40, False, False)
            st.leave(KT // 2 - 2, 4)
            down_out(KT - 2, 0, 40, False, False)
            down_out(KT - 1, 3, 40, False, True)
            v.wait_ge(S["mod_evacuated"], 10)
            st.done(v.scalar_tensor_tensor(A3, mod2[:, 8:16], 1.0, vec[:, V_NMIX:V_NMIX + 8], ALU.add, ALU.mult))
            st.done(v.scalar_tensor_tensor(A2, mod2[:, 32:40], 1.0, vec[:, V_NFFN:V_NFFN + 8], ALU.add, ALU.mult))
            st.wait()
            st.done(v.tensor_tensor(A3, A3, vec[:, V_GFIN:V_GFIN + 8], ALU.mult))
            v.wait_ge(S["stat_ready"], 2)
            st.done(v.tensor_scalar(mean, bank[6][:, 0:TT], 1.0 / D, EPS, ALU.mult, ALU.add))
            st.wait()
            st.done(v.tensor_scalar(z2, mean, EPS, None, ALU.mult))
            st.wait()
            v.scalar_tensor_tensor(z2, bank[6][:, TT:2 * TT], 1.0 / D, z2, ALU.mult, ALU.add).then_inc(S["mean2_ready"], 1)
            v.wait_ge(S["root2_ready"], 1)
            st.done(v.reciprocal(r12, z2))
            st.wait()
            for t in range(TT):
                v.tensor_scalar(tbuf[1][:, t * P:(t + 1) * P], ident[:], r12[:, t:t + 1], None, ALU.mult).then_inc(S["diag_ready"], 1)
            v.wait_ge(S["root_ready"], 2)
            st.done(v.reciprocal(rstd, mean))
            st.wait()
            for t in range(TT):
                v.tensor_scalar(tbuf[0][:, t * P:(t + 1) * P], ident[:], rstd[:, t:t + 1], None, ALU.mult).then_inc(S["diag_ready"], 1)
            v.wait_ge(S["bc_ready"], 2)
            norm_dve(1, hl, move=True)
            v.wait_ge(S["bc_ready"], 3)
            for u in range(U_QKV2, U_GZ):
                low(u + 1, (u + 1) % 2, 2048)
                k = u - U_QKV2
                if k < KT:
                    st.done(v.tensor_tensor(tbuf[2 + k % 2][:], xT[:, k, :], bank[7][:], ALU.mult))
                    st.wait()
                    v.tensor_scalar(reordered(xT[:, k, :], False), reordered(tbuf[2 + k % 2][:], True),
                                    vec[:, V_GFIN + k:V_GFIN + k + 1], None, ALU.mult).then_inc(S["rescaled"], 1)
                if k == 7:
                    v.wait_ge(S["wf_in"], 16)
                    st.done(v.tensor_copy(wfh[:], wfr[:]))
                    st.wait()
                    v.tensor_tensor(wfl[:], wfr[:], wfh[:].bitcast(F32), ALU.subtract).then_inc(S["wf_split"], 1)
                v.wait_ge(S["pe_used"], u + 1)
                b = 3 * (u % 2)
                for m in range(2):
                    if k in (6, 7, 8, 11):
                        c0 = (k - 6) * UC if k < 9 else WA
                        ins = v.tensor_copy(v2[:, 2 * m:2 * m + 2, c0:c0 + UC], bank[b + m][:].rearrange("p (t n) -> p t n", t=2))
                    else:
                        tile = 2 * k if k < 6 else 12 + 2 * (k - 9)
                        ins = v.tensor_copy(qk[:, tile + m, :], bank[b + m][:])
                    if m == 0:
                        st.done(ins)
                    else:
                        ins.then_inc(S["evacuated"], 1)
                if k == 8:
                    v.wait_ge(S["f_logits"], 1)
                    v.wait_ge(S["bf_in"], 16)
                    st.done(v.tensor_scalar(reordered(fA[:], True), reordered(bank[6][0:NHB, :], False), small[0:NHB, 44:45], None, ALU.add))
                    st.wait()
                    v.scalar_tensor_tensor(fB[:], fA[:], -1.0, fA[:], ALU.mult, ALU.max).then_inc(S["f_abs"], 1)
                    st.done(v.tensor_scalar(fA[:], fA[:], 0.0, None, ALU.min))
                    v.wait_ge(S["f_soft"], 1)
                    st.wait()
                    st.done(v.tensor_tensor(fA[:], fA[:], fB[:], ALU.subtract))
                    st.wait()
                    st.done(v.tensor_tensor_scan(fF[:], ones[0:NHB, 0:1].broadcast_to([NHB, T]), fA[:], 0.0, ALU.mult, ALU.add))
                    st.wait()
                    v.tensor_scalar(reordered(fB[:], False), reordered(fF[:], True), -1.0 / QK_SCALE, None, ALU.mult).then_inc(S["f_neg"], 1)
                if k == 10:
                    for h in range(NHB):
                        v.wait_ge(S["fb_ready"], h + 1)
                        v.tensor_copy(FB[:, h, :], bank[6 + h % 2][:]).then_inc(S["fb_copied"], 1)
            v.wait_ge(S["tab_in"], 48)
            for r in range(ROUNDS + 4):
                if r < ROUNDS:
                    b, Lr = 2 * (r % 2), L[r % 3]
                    v.wait_ge(S["qk_ready"], r + 1)
                    if r >= 3:
                        v.wait_ge(S["tr_ready"], r - 2)
                    if r < ROUNDS_A:
                        i, c = r // CL, r % CL
                        for g, (dst, dist, src) in enumerate((
                                (Lr[:, 0:T], dist0[:, c, :], bank[b][:]),
                                (Lr[:, T:T + P], dist12[:, 0, :], bank[b + 1][:, 0:P]),
                                (Lr[:, T + P:], dist12[:, 1, :], bank[b + 1][:, P:2 * P]))):
                            ins = v.scalar_tensor_tensor(dst, dist, -SLOPES[GH * g + i] / QK_SCALE, src, ALU.mult, ALU.add)
                            if g < 2:
                                st.done(ins)
                        ins.then_inc(S["l_free"], 1)
                        w = KEYS_A
                    else:
                        q = r - ROUNDS_A
                        v.wait_ge(S["cf_ready"], q + 1)
                        v.tensor_tensor(Lr[:, 0:T], CF[q % 2][:], bank[b][:], ALU.add).then_inc(S["l_free"], 1)
                        w = T
                    v.wait_ge(S["l_free"], r + 1)
                    st.wait()
                    ins = v.reduce_max(nmax[:, r % 8:r % 8 + 1], Lr[:, 0:w], AX_X)
                    st.done(ins)
                    st.wait()
                    v.tensor_scalar(nmax[:, r % 8:r % 8 + 1], nmax[:, r % 8:r % 8 + 1], -QK_SCALE, None, ALU.mult).then_inc(S["l_ready"], 1)
                if r >= 4:
                    q = r - 4
                    v.wait_ge(S["o_ready"], q + 1)
                    st.done(v.reciprocal(rsum[:, q % 8:q % 8 + 1], lsum[:, q % 8:q % 8 + 1]))
                    st.wait()
                    c = q % CL
                    c0 = (q // CL) * HD if q < ROUNDS_A else GH * HD + (q - ROUNDS_A) // CL * HD
                    v.tensor_scalar(on[:, c, c0:c0 + HD], bank[6 + q % 2][:, 0:HD], rsum[:, q % 8:q % 8 + 1], None, ALU.mult).then_inc(S["o_free"], 1)
            for u in range(U_GZ, U_OUT2):
                low(u + 1, (u + 1) % 2, 2048)
                m, s = u - U_GZ, u % 2
                v.wait_ge(S["pe_used"], u + 1)
                v.wait_ge(S["g_sig"], 2 * m + 2)
                st.done(v.tensor_tensor(tbuf[2][:], tbuf[0][:], bank[3 * s + 2][:], ALU.mult))
                v.tensor_tensor(tbuf[3][:], tbuf[1][:], bank[6 + s][:], ALU.mult).then_inc(S["evacuated"], 1)
                v.wait_ge(S["evacuated"], u + 1)
                st.wait()
                st.done(v.tensor_tensor(tbuf[2][:], tbuf[2][:], tbuf[3][:], ALU.add))
                st.wait()
                st.done(v.tensor_copy(mh[:, m, :], tbuf[2][:]))
                st.wait()
                v.tensor_tensor(ml[:, m, :], tbuf[2][:], mh[:, m, :].bitcast(F32), ALU.subtract).then_inc(S["m_ready"], 1)
            v.wait_ge(S["rescaled"], KT)
            out_phase(U_OUT2, U_IN2, mod2, False)
            norm_stats(2)
            norm_dve(2, hl)

            def in_out(u, i, s, n_next):
                low(u + 1, 1 - s, n_next)
                v.wait_ge(S["pe_used"], u + 1)
                v.wait_ge(S["glu_s"], FT + i + 1)
                v.tensor_tensor(tbuf[4 + s][:], tbuf[2 + s][:], bank[3 * s + 1][:], ALU.mult).then_inc(S["evacuated"], 1)
                v.wait_ge(S["evacuated"], u + 1)
                f3 = tbuf[4 + s][:].rearrange("p (a n) -> p a n", a=1)
                st.done(v.tensor_copy(fh[:, bass.ds(i, 1), :], f3))
                st.wait()
                v.tensor_tensor(fl[:, bass.ds(i, 1), :], f3, fh[:, bass.ds(i, 1), :].bitcast(F32), ALU.subtract).then_inc(S["f_ready"], 1)

            with v.Fori(0, FT // 2 - 1) as i:
                st.enter(i, 2)
                for s in range(2):
                    in_out(U_IN2 + 2 * i + s, 2 * i + s, s, 2048)
            st.leave(FT // 2 - 1, 2)
            in_out(U_DOWN2 - 2, FT - 2, 0, 2048)
            in_out(U_DOWN2 - 1, FT - 1, 1, FH * P)

            def last_out(m, q, first=False, last=False):
                u = m * 2 + U_DOWN2
                low(u + 1, 1, FH * P)
                if not last:
                    low(u + 2, 0, FH * P)
                v.wait_ge(S["pe_used"], u + 2)
                xm = xT[:, bass.ds(m, 1), :]
                v.scalar_tensor_tensor(xm, bank[3 * q][:].rearrange("p (a n) -> p a n", a=1), mod2[:, bass.ds(40 + m, 1)], xm,
                                       ALU.mult, ALU.add).then_inc(S["evacuated"], 1)
                v.wait_ge(S["evacuated"], u + 1)
                if not isinstance(m, int) or m >= 2:
                    v.wait_ge(S["fin_turned"], m - 1)
                v.tensor_scalar(tbuf[2 + q][:].rearrange("p (a n) -> p a n", a=1), xm, vec[:, bass.ds(V_NFIN + m, 1)], None,
                                ALU.mult).then_inc(S["xg_ready"], 1)
                if first:
                    v.tensor_tensor(acc[:].rearrange("p (a n) -> p a n", a=1), xm, xm, ALU.mult).then_inc(S["evacuated"], 1)
                else:
                    st.done(v.tensor_tensor(tbuf[5][:].rearrange("p (a n) -> p a n", a=1), xm, xm, ALU.mult))
                    st.wait()
                    v.tensor_tensor(acc[:], acc[:], tbuf[5][:], ALU.add).then_inc(S["evacuated"], 1)
                v.wait_ge(S["evacuated"], u + 2)

            last_out(0, 0, first=True)
            last_out(1, 1)
            with v.Fori(1, KT // 2 - 1) as i:
                st.enter(i - 1, 2)
                for q in range(2):
                    last_out(2 * i + q, q)
            st.leave(KT // 2 - 2, 2)
            last_out(KT - 2, 0)
            last_out(KT - 1, 1, last=True)
            v.wait_ge(S["stat_ready"], 4)
            v.tensor_scalar(mean, bank[0][:, 0:TT], 1.0 / D, EPS, ALU.mult, ALU.add).then_inc(S["mean_ready"], 1)
            v.wait_ge(S["root_ready"], 4)
            st.done(v.reciprocal(rstd, mean))
            st.wait()
            v.wait_ge(S["fin_copied"], KT)
            for c in (0, 2):
                v.tensor_scalar(fin[:, c, :], fin[:, c, :], rstd[:, c:c + 1], None, ALU.mult).then_inc(S["scaled"], 1)

        @block.tensor
        def _(pe):
            def mm3(dst, ah, al, bh, bl, first, last):
                pe.matmul(dst, ah, bh, start=first, stop=False)
                pe.matmul(dst, ah, bl, start=False, stop=False)
                return pe.matmul(dst, al, bh, start=False, stop=last)

            def unit(u):
                if isinstance(u, int):
                    pe.wait_ge(S["lo_ready"], u + 1)
                    if u >= 2:
                        pe.wait_ge(S["evacuated"], u - 1)
                else:
                    pe.wait_ge(S["lo_ready"], u + 1)
                    pe.wait_ge(S["evacuated"], u - 1)

            def features(s, bh, bl, m, b, k):
                return mm3(bank[b][:], whi[s][:, k * UC + m * P:k * UC + (m + 1) * P],
                           wlo[s][:, k * UC + m * P:k * UC + (m + 1) * P], bh[:, k, :], bl[:, k, :], k == 0, k == KT - 1)

            def mod_chunk(c, acc_m):
                pe.wait_ge(S["mod_used"], (c + 1) * 4)
                if not isinstance(c, int) or c >= 1:
                    pe.wait_ge(S["mod_evacuated"], c)
                for m in range(KT):
                    ins = pe.matmul(bank[7][:, m:m + 1], acc_m[:, m * P:(m + 1) * P], ones[:, 0:1], start=True, stop=True)
                ins.then_inc(S["mod_sum"], 1)

            pe.wait_ge(S["vecs_in"], 14 * 16)
            pe.wait_ge(S["consts_in"], 16)
            for i in range(3):
                c = (P, V_CONV - P, 3 * FT)[i]
                pe.transpose(bank[i][:, 0:c], vrow[i][0:c, :], ident[0:c, 0:c]).then_inc(S["vec_t"], 1)
            pe.wait_ge(S["silu_c"], 1)
            for k in range(KT):
                pe.wait_ge(S[f"wm_in{k}"], 16)
                for q in range(4):
                    ins = pe.matmul(bank[q][0:2, :], sil[:, k:16:8], wm[:, k, q * 512:(q + 1) * 512],
                                    start=(k == 0), stop=(k == KT - 1))
            ins.then_inc(S["pe_mod0"], 1)
            for m in range(16):
                if m % 4 == 0:
                    pe.wait_ge(S["mod_rows"], m // 4 + 1)
                ins = pe.transpose(bank[7][:, 2 * m:2 * m + 2], mrow[:, m * P:(m + 1) * P], ident[0:2, 0:2])
            ins.then_inc(S["pe_mod0"], 1)
            pe.wait_ge(S["vec_cols"], 3)
            pe.wait_ge(S["x_scaled"], TT + CTT)
            def gates(k):
                pe.wait_ge(S["h_ready"], 2 * k + 2)
                for bh, bl, ps, w in ((hh, hl, bank[6], T), (hch, hcl, bank[7], TC)):
                    ins = mm3(ps[0:NG, 0:w], wgh[:, k, :], wgl[:, k, :], bh[:, k, :], bl[:, k, :], k == 0, k == KT - 1)
                return ins

            for n in range(2 * KT):
                k, t0, nt = n // 2, (0, TT)[n % 2], (TT, CTT)[n % 2]
                if n >= 6:
                    pe.wait_ge(S["h_raw"], n - 5)
                for t in range(nt):
                    ins = pe.transpose(bank[n % 6][:, t * P:(t + 1) * P], xn[:, t0 + t, k * P:(k + 1) * P], ident[:])
                ins.then_inc(S["x_turned"], 1)
                if n == 5:
                    pe.wait_ge(S["mod0_cols"], 4)
                    pe.wait_ge(S["wg_split"], 1)
                if n > 5 and n % 2:
                    gates(k - 3)
            for k in range(KT - 3, KT):
                ins = gates(k)
            ins.then_inc(S["gates_in"], 1)
            pe.wait_ge(S["mod0_cols"], 4)

            def tokens(u, n, hs, ls, t, dst):
                for k in range(KT):
                    ins = mm3(dst, hs[:, k, t * P:(t + 1) * P], ls[:, k, t * P:(t + 1) * P],
                              whi[u % 2][:, k * UC:(k + 1) * UC], wlo[u % 2][:, k * UC:(k + 1) * UC], k == 0, k == KT - 1)
                return ins

            for u in range(U_Q, U_V):
                unit(u)
                b = 3 * (u % 2)
                for m in range(2):
                    for k in range(KT):
                        ins = features(u % 2, hh, hl, m, b + m, k)
                if u >= U_K:
                    for t in range(CTT):
                        ins = tokens(u, 0, hch, hcl, t, bank[b + 2][:, t * UC:(t + 1) * UC])
                ins.then_inc(S["pe_used"], 1)
            pe.wait_ge(S["g_nat"], 7)
            for t in range(TT):
                pe.transpose(bank[6][:, 36 * t:36 * t + GR], gZ[:, TC + t * P:TC + (t + 1) * P], ident[0:GR, 0:GR])
                pe.transpose(bank[6][:, 144 + 36 * t:144 + 36 * t + GR], gN[:, t * P:(t + 1) * P], ident[0:GR, 0:GR])
            for t in range(CTT):
                pe.transpose(bank[6][:, 288 + 36 * t:288 + 36 * t + GR], gZ[:, t * P:(t + 1) * P], ident[0:GR, 0:GR])
            pe.matmul(bank[6][:, 360:360 + GR], ones[0:GR, :], dmc[:], start=True, stop=True).then_inc(S["g_turned"], 1)
            for u in range(U_V, U_O):
                unit(u)
                b = 3 * (u % 2)
                for t in range(TT):
                    tokens(u, 0, hh, hl, t, bank[b + t // 2][:, (t % 2) * UC:(t % 2 + 1) * UC])
                for t in range(CTT):
                    ins = tokens(u, 0, hch, hcl, t, bank[b + 2][:, t * UC:(t + 1) * UC])
                ins.then_inc(S["pe_used"], 1)
                if u == U_V:
                    mod_chunk(0, msum0)
                if u == U_O - 1:
                    mod_chunk(1, msum0)

            def broadcast(i):
                if i >= 1:
                    pe.wait_ge(S["gb_copied"], i)
                pe.matmul(bank[6][:], ident[0:GR, row(i):row(i) + 1].broadcast_to([GR, P]), Gnat[:],
                          start=True, stop=True).then_inc(S["gb_ready"], 1)

            def state(i):
                h = PERM[i][0]
                pe.wait_ge(S["kw_ready"], i + 1)
                if i >= 1:
                    pe.wait_ge(S["cl_ready"], i)
                for t in range(CTT):
                    ins = pe.matmul(bank[7][:, 0:VE], kw[:, t, :], vc[:, t, h, :], start=(t == 0), stop=(t == CTT - 1))
                ins.then_inc(S["c_ready"], 1)

            def scores(n):
                i = n // TT
                h, (s_, r) = PERM[i][0], span(i, n % TT)
                if n >= 2:
                    pe.wait_ge(S["w_raw"], n - 1)
                ks = slice(s_ * P, (s_ + 1) * P)
                mm3(bank[4 + n % 2][:, r], kh[:, h, ks], kl[:, h, ks], qh[:, h, r], ql[:, h, r], True, True).then_inc(S["s_ready"], 1)

            def apply(n):
                i, j = n // TT, n % TT
                h, (s_, r) = PERM[i][0], span(i, j)
                pe.wait_ge(S["w_ready"], n + 1)
                for t in range(r.start // P, r.stop // P):
                    c = slice(t * P, (t + 1) * P)
                    if j == 0 and i >= 1:
                        pe.wait_ge(S["num_free"], (i - 1) * TT + t + 1)
                    ins = mm3(bank[t][:, 0:VE], Wh[n % 2][:, c], Wl[n % 2][:, c], vh[:, s_, h, :], vl[:, s_, h, :], j == 0, False)
                ins.then_inc(S["w_free"], 1)

            def carried(i):
                pe.wait_ge(S["cl_ready"], i + 1)
                pe.wait_ge(S["q_ready"], i + 1)
                for t in range(TT):
                    c = slice(t * P, (t + 1) * P)
                    ins = mm3(bank[t][:, 0:VE], qwh[:, c], qwl[:, c], Ch[:], Cl[:], False, True)
                ins.then_inc(S["num_ready"], 1)

            pe.wait_ge(S["g_nat"], 9)
            pe.wait_ge(S["gcols_in"], 1)
            broadcast(0)
            pe.wait_ge(S["evacuated"], U_O)
            scores(0)
            pe.wait_ge(S["mod_evacuated"], 2)
            state(0)
            scores(1)
            broadcast(1)
            for i in range(2 * NH):
                for j in range(TT):
                    n = i * TT + j
                    if n + 2 < 2 * NH * TT:
                        scores(n + 2)
                    apply(n)
                    if j == 1 and i + 2 < 2 * NH:
                        broadcast(i + 2)
                carried(i)
                if i + 1 < 2 * NH:
                    state(i + 1)
            for u in range(U_O, U_OUT):
                unit(u)
                if u == U_O:
                    pe.wait_ge(S["num_free"], 2 * NH * TT)
                b = 3 * (u % 2)
                for m in range(2):
                    for k in range(KT):
                        ins = features(u % 2, hh, hl, m, b + m, k)
                ins.then_inc(S["pe_used"], 1)
                if u == U_O:
                    pe.wait_ge(S["hn_ready"], TT * NH)
                if u >= U_O + 1:
                    pe.wait_ge(S["evacuated"], u)
                for m in range(2):
                    f = 2 * (u - U_O) + m
                    for t in range(TT):
                        ins = pe.transpose(bank[6 if m == 0 else b + 2][:, t * P:(t + 1) * P], hn[:, t, f * P:(f + 1) * P], ident[:])
                    ins.then_inc(S["hn_turned"], 1)
            pe.wait_ge(S["xr_in"], 16)
            pe.wait_ge(S["evacuated"], U_OUT)
            for k in range(KT):
                if k >= 2:
                    pe.wait_ge(S["xT_in"], k - 1)
                for t in range(TT):
                    ins = pe.transpose(bank[6 if k % 2 == 0 else 7][:, t * P:(t + 1) * P], xr[:, t, k * P:(k + 1) * P], ident[:])
                ins.then_inc(S["xr_turned"], 1)
            pe.wait_ge(S["xT_in"], KT)
            for u in range(U_OUT, U_UP):
                unit(u)
                if u == U_OUT:
                    pe.wait_ge(S["y_ready"], KT)
                for m in range(2):
                    for k in range(KT):
                        ins = features(u % 2, yh, yl, m, 3 * (u % 2) + m, k)
                    ins.then_inc(S["pe_used" if m else "out_half"], 1)
                if u == U_OUT:
                    mod_chunk(2, msum0)

            def norm_pe(diag0):
                for t in range(TT):
                    ins = pe.matmul(bank[6][:, t:t + 1], acc[:, t * P:(t + 1) * P], ones[:, 0:1], start=True, stop=True)
                ins.then_inc(S["stat_ready"], 1)
                for t in range(TT):
                    pe.wait_ge(S["diag_ready"], diag0 + t + 1)
                    ins = pe.matmul(bank[6][:, t * P:(t + 1) * P], ones[:], tbuf[1][:, t * P:(t + 1) * P], start=True, stop=True)
                ins.then_inc(S["bc_ready"], 1)

            pe.wait_ge(S["acc_ready"], 1)
            norm_pe(0)

            def up_unit(u, i, s, nth=None, mod=None):
                unit(u)
                for k in range(KT):
                    if nth is not None:
                        pe.wait_ge(S["n_ready"], nth * KT + k + 1)
                    for m in range(2):
                        ins = features(s, hh, hl, m, 3 * s + m, k)
                ins.then_inc(S["pe_used"], 1)
                if mod is not None:
                    mod_chunk(mod, msum1)

            for q in range(4):
                up_unit(U_UP + q, q, q % 2, nth=None if q else 0, mod=None if q else 3)
            with pe.Fori(1, FT // 4) as i:
                for q in range(4):
                    up_unit(U_UP + 4 * i + q, 4 * i + q, q % 2, mod=None if q else 3 + i)
            for q in range(FT % 4):
                up_unit(U_UP + FT // 4 * 4 + q, FT // 4 * 4 + q, q % 2, mod=None if q else 3 + FT // 4)

            def down_tile(m, b, first=False, base=U_DOWN, f0=0):
                for s in range(2):
                    u = m * 2 + base + s
                    pe.wait_ge(S["lo_ready"], u + 1)
                    if s == 0:
                        pe.wait_ge(S["evacuated"], u - 1 if first else u - 2)
                    for k in range(FH):
                        f = s * FH + k
                        if first and s == 0 and k == 0:
                            pe.wait_ge(S["f_ready"], f0 + FT - 2)
                        if first and f == FT - 2:
                            pe.wait_ge(S["f_ready"], f0 + FT)
                        ins = mm3(bank[b][:], whi[s][:, k * P:(k + 1) * P], wlo[s][:, k * P:(k + 1) * P],
                                  fh[:, f, :], fl[:, f, :], f == 0, f == FT - 1)
                    ins.then_inc(S["pe_used"], 1)

            down_tile(0, 0, True)
            down_tile(1, 3)
            mod_chunk(9, msum1)
            with pe.Fori(1, KT // 2) as i:
                for s in range(2):
                    down_tile(2 * i + s, 3 * s)

            pe.wait_ge(S["evacuated"], U_QKV2)
            for n, sums in enumerate((acc, acc2)):
                for t in range(TT):
                    ins = pe.matmul(bank[6][:, n * TT + t:n * TT + t + 1], sums[:, t * P:(t + 1) * P], ones[:, 0:1], start=True, stop=True)
            ins.then_inc(S["stat_ready"], 1)
            for n in range(2):
                for t in range(TT):
                    pe.wait_ge(S["diag_ready"], TT + n * TT + t + 1)
                    ins = pe.matmul(bank[6 + n][:, t * P:(t + 1) * P], ones[:], tbuf[1 - n][:, t * P:(t + 1) * P], start=True, stop=True)
                ins.then_inc(S["bc_ready"], 1)
            for u in range(U_QKV2, U_GZ):
                unit(u)
                k0, s = u - U_QKV2, u % 2
                b = 3 * s
                if k0 in (6, 7, 8, 11):
                    for t in range(TT):
                        ins = tokens(u, 0, hh, hl, t, bank[b + t // 2][:, (t % 2) * UC:(t % 2 + 1) * UC])
                else:
                    for k in range(KT):
                        if k0 == 0:
                            pe.wait_ge(S["n_ready"], KT + k + 1)
                        for m in range(2):
                            ins = features(s, hh, hl, m, b + m, k)
                ins.then_inc(S["pe_used"], 1)
                if k0 == 8:
                    pe.wait_ge(S["wf_split"], 1)
                    for k in range(KT):
                        ins = mm3(bank[6][0:NF, :], wfh[:, k, :], wfl[:, k, :], hh[:, k, :], hl[:, k, :], k == 0, k == KT - 1)
                    ins.then_inc(S["f_logits"], 1)
                if k0 == 10:
                    pe.wait_ge(S["f_neg"], 1)
                    pe.wait_ge(S["rescaled"], KT)
                    for h in range(NHB):
                        if h >= 2:
                            pe.wait_ge(S["fb_copied"], h - 1)
                        pe.matmul(bank[6 + h % 2][:], ident[0:NHB, h:h + 1].broadcast_to([NHB, P]), fB[:], start=True, stop=True).then_inc(S["fb_ready"], 1)

            def logits(r):
                b = 2 * (r % 2)
                if r >= 2:
                    pe.wait_ge(S["l_free"], r - 1)
                c = r % CL
                cc = slice(c * P, (c + 1) * P)
                if r < ROUNDS_A:
                    i = r // CL
                    pp = slice((i % 2) * HD, (i % 2 + 1) * HD)
                    for g, (dst, keys) in enumerate(((bank[b][:], slice(0, T)), (bank[b + 1][:, 0:P], cc), (bank[b + 1][:, P:2 * P], cc))):
                        tile = (GH * g + i) // 2
                        ins = pe.matmul(dst, qk[pp, tile, cc], qk[pp, NHA // 2 + tile, keys], start=True, stop=True)
                else:
                    h = (r - ROUNDS_A) // CL
                    pp = slice((h % 2) * HD, (h % 2 + 1) * HD)
                    ins = pe.matmul(bank[b][:], qk[pp, 12 + h // 2, cc], qk[pp, 14 + h // 2, :], start=True, stop=True)
                ins.then_inc(S["qk_ready"], 1)

            def turn(r):
                pe.wait_ge(S["p_ready"], r + 1)
                if r >= 1:
                    pe.wait_ge(S["pt_copied"], r)
                for j in range(KEYS_A // P if r < ROUNDS_A else TT):
                    ins = pe.matmul(bank[4 + j // 4][:, (j % 4) * P:(j % 4 + 1) * P], L[r % 3][:, j * P:(j + 1) * P], ident[:], start=True, stop=True)
                ins.then_inc(S["tr_ready"], 1)

            def values(r):
                pe.wait_ge(S["pt_copied"], r + 1)
                if r >= 2:
                    pe.wait_ge(S["o_free"], r - 1)
                c = r % CL
                if r < ROUNDS_A:
                    i = r // CL
                    terms = [(j, j, i) for j in range(TT)] + [(TT, c, GH + i), (TT + 1, c, 2 * GH + i)]
                else:
                    terms = [(j, j, NHA + (r - ROUNDS_A) // CL) for j in range(TT)]
                for n, (j, tile, head) in enumerate(terms):
                    ins = pe.matmul(bank[6 + r % 2][:, 0:HD], PT[r % 2][:, j * P:(j + 1) * P], v2[:, tile, head * HD:(head + 1) * HD],
                                    start=(n == 0), stop=(n == len(terms) - 1))
                ins.then_inc(S["o_ready"], 1)

            pe.wait_ge(S["evacuated"], U_GZ)
            for r in range(ROUNDS + 3):
                if r < ROUNDS:
                    logits(r)
                if r >= 3:
                    if r == 3:
                        pe.wait_ge(S["fb_copied"], NHB)
                    values(r - 3)
                if 2 <= r < ROUNDS + 2:
                    turn(r - 2)

            for u in range(U_GZ, U_OUT2):
                unit(u)
                m, s = u - U_GZ, u % 2
                if m == 0:
                    pe.wait_ge(S["l_free"], ROUNDS)
                for g in range(2):
                    for k in range(KT):
                        features(s, hh, hl, g, 3 * s + g, k)
                if m == 0:
                    pe.wait_ge(S["pt_copied"], ROUNDS)
                    pe.wait_ge(S["o_free"], ROUNDS)
                    for f in range(4):
                        for c in range(CL):
                            ins = pe.transpose(bank[4 + f][:, c * P:(c + 1) * P], on[:, c, f * P:(f + 1) * P], ident[:])
                        ins.then_inc(S["on_turned"], 1)
                    pe.wait_ge(S["att_ready"], 4)
                    pe.wait_ge(S["up_in"], 32)
                for w, b, f0 in ((upA, 3 * s + 2, 0), (upB, 6 + s, 2)):
                    for k in range(2):
                        ins = pe.matmul(bank[b][:], w[:, k, m * P:(m + 1) * P], att[:, f0 + k, :], start=(k == 0), stop=(k == 1))
                ins.then_inc(S["pe_used"], 1)
            for u in range(U_OUT2, U_IN2):
                unit(u)
                if u == U_OUT2:
                    for k in range(KT):
                        pe.wait_ge(S["m_ready"], k + 1)
                        for m in range(2):
                            ins = features(u % 2, mh, ml, m, 3 * (u % 2) + m, k)
                            if k == KT - 1:
                                ins.then_inc(S["pe_used" if m else "out_half"], 1)
                else:
                    for m in range(2):
                        for k in range(KT):
                            ins = features(u % 2, mh, ml, m, 3 * (u % 2) + m, k)
                        ins.then_inc(S["pe_used" if m else "out_half"], 1)
            pe.wait_ge(S["acc_ready"], 2)
            norm_pe(3 * TT)
            up_unit(U_IN2, 0, 0, nth=2)
            up_unit(U_IN2 + 1, 1, 1)
            with pe.Fori(1, FT // 2) as i:
                for s in range(2):
                    up_unit(U_IN2 + 2 * i + s, 2 * i + s, s)

            def turn_out(m, q):
                pe.wait_ge(S["xg_ready"], m + 1)
                if not isinstance(m, int) or m >= 2:
                    pe.wait_ge(S["fin_copied"], m - 1)
                for c in range(CL):
                    ins = pe.transpose(bank[6 + q][:, c * P:(c + 1) * P], tbuf[2 + q][:, c * P:(c + 1) * P], ident[:])
                ins.then_inc(S["fin_turned"], 1)

            down_tile(0, 0, True, U_DOWN2, FT)
            down_tile(1, 3, False, U_DOWN2)
            turn_out(0, 0)
            with pe.Fori(1, KT // 2) as i:
                for q in range(2):
                    down_tile(2 * i + q, 3 * q, False, U_DOWN2)
                    turn_out(2 * i + q - 1, 1 - q)
            turn_out(KT - 1, 1)
            pe.wait_ge(S["evacuated"], U_END)
            for t in range(TT):
                ins = pe.matmul(bank[0][:, t:t + 1], acc[:, t * P:(t + 1) * P], ones[:, 0:1], start=True, stop=True)
            ins.then_inc(S["stat_ready"], 1)


_INS = ["x", "c", "ctx", "c_ctx", "w_mod", "b_mod", "g_mix", "g_ffn", "a_w_in", "a_b_gate", "a_head_gain", "a_w_out",
        "f_w_up", "f_w_conv", "f_b_conv", "f_w_down", "g_final", "c_2", "w_ada_2", "b_ada_2", "norm_mix_2", "w_in_2",
        "b_forget_2", "w_up_a_2", "w_up_b_2", "w_out_2", "norm_ffn_2", "w_ffn_in_2", "w_ffn_out_2", "norm_final_2"]
_OUTS = [((1, T, D), "float32")]


def kernel(**inputs):
    import numpy as _np
    import concourse.bacc as _bacc
    from concourse import mybir as _mybir
    from concourse.bass_utils import run_bass_kernel_spmd as _run

    nc = _bacc.Bacc("TRN2", target_bir_lowering=False, num_devices=1)
    i = _np.arange(P)
    t = (i[:, None] // CB * CL + i[:, None] % CB * (CL * CA) + _np.arange(CL)[None, :])
    gap = t[:, :, None] - t.T.reshape(1, 1, T)
    same = gap[:, 0, 0:P]
    near = lambda ok, d: _np.where(ok, d, FAR).astype(_np.float32)
    consts = {
        "k_dist0": near((gap >= 0) & (gap <= WINDOW0), gap),
        "k_dist12": _np.stack([near(same >= 0, same), near((same >= 0) & (same % 16 == 0), same)], 1),
        "k_causal": _np.where(gap >= 0, 0, -FAR).astype(_np.float32),
        "k_ident": _np.eye(P, dtype=_np.float32),
        "k_masks": _np.stack([i[:, None] <= i[None, :], i[:, None] >= i[None, :]], 1).astype(_np.float32),
    }
    arrays, args = {}, {}
    for name in _INS + list(consts):
        a = consts[name] if name in consts else _np.ascontiguousarray(inputs[name])
        arrays[f"in_{name}_dram"] = a
        args[name] = nc.dram_tensor(f"in_{name}_dram", a.shape, _mybir.dt.from_np(a.dtype), kind="ExternalInput").ap()
    for n, (shape, dtype) in enumerate(_OUTS):
        out = nc.dram_tensor(f"out_{n}_dram", shape, _mybir.dt.from_np(_np.dtype(dtype)), kind="ExternalOutput").ap()
    program(nc, args, out)
    r = _run(nc, [arrays], core_ids=[0])
    return r.results[0]["out_0_dram"]
```
